# Optimizing a Trainium2 kernel written in Bass

```python
import jax, jax.numpy as jnp
from jax import lax
import numpy as np
import math

D_MODEL = 1024
BATCH = 1
SEQ = 512
DEPTH = 1

EPS = 1e-6
N_MOD = 6
CONV_WIDTH = D_MODEL
CONV_KERNEL = 31
MLSTM_HEADS = 4
MLSTM_HEAD_DIM = D_MODEL // MLSTM_HEADS
MLSTM_WIDTH = MLSTM_HEADS * MLSTM_HEAD_DIM
QK_CONV = 4
CHUNK = 64
D_FF = ((8 * D_MODEL + 3 * 256 - 1) // (3 * 256)) * 256

N_GLU = 2 * CONV_WIDTH
N_QK = 2 * MLSTM_WIDTH
N_V = MLSTM_WIDTH
N_O = MLSTM_WIDTH
N_IF = 2 * MLSTM_HEADS
N_MERGE = 2 * D_MODEL
N_IN = N_GLU + N_QK + N_V + N_O + N_IF + N_MERGE
IN_SPLITS = (N_GLU, N_GLU + N_QK, N_GLU + N_QK + N_V, N_GLU + N_QK + N_V + N_O,
             N_GLU + N_QK + N_V + N_O + N_IF)
F_BIAS_OFFSET = N_GLU + N_QK + N_V + N_O + MLSTM_HEADS


def rms_norm(x, g):
    xf = x.astype(jnp.float32)
    y = xf * lax.rsqrt(jnp.mean(xf * xf, axis=-1, keepdims=True) + EPS)
    return (y * g.astype(jnp.float32)).astype(x.dtype)

def layer_norm(x, g, b):
    xf = x.astype(jnp.float32)
    mu = jnp.mean(xf, axis=-1, keepdims=True)
    var = jnp.mean(jnp.square(xf - mu), axis=-1, keepdims=True)
    y = (xf - mu) * lax.rsqrt(var + EPS)
    return (y * g.astype(jnp.float32) + b.astype(jnp.float32)).astype(x.dtype)

def causal_depthwise_conv(x, w, b):
    k = w.shape[0]
    y = lax.conv_general_dilated(
        x, w[:, None, :].astype(x.dtype), window_strides=(1,), padding=((k - 1, 0),),
        dimension_numbers=("NWC", "WIO", "NWC"), feature_group_count=x.shape[-1])
    return y + b

def mlstm_chunkwise(q, k, v, i_pre, f_pre):
    bsz, nh, s, dh = q.shape
    nc = s // CHUNK

    def to_chunks(t):
        return jnp.moveaxis(t.reshape(t.shape[:2] + (nc, CHUNK) + t.shape[3:]), 2, 0)

    log_f = jax.nn.log_sigmoid(f_pre)
    xs = (to_chunks(q), to_chunks(k), to_chunks(v), to_chunks(i_pre), to_chunks(log_f))
    causal = jnp.tril(jnp.ones((CHUNK, CHUNK), dtype=bool))

    def step(carry, inp):
        c_st, n_st, m_st = carry
        qc, kc, vc, ic, lfc = inp
        b = jnp.cumsum(lfc, axis=-1)
        d_log = jnp.where(causal, b[..., :, None] - b[..., None, :] + ic[..., None, :], -jnp.inf)
        inter_log = b + m_st[..., None]
        m_t = jnp.maximum(inter_log, jnp.max(d_log, axis=-1))
        dmat = jnp.exp(d_log - m_t[..., None])
        inter_w = jnp.exp(inter_log - m_t)
        sc = jnp.einsum("bhtd,bhsd->bhts", qc, kc) * dmat
        num = (jnp.einsum("bhts,bhse->bhte", sc, vc)
               + inter_w[..., None] * jnp.einsum("bhtd,bhde->bhte", qc, c_st))
        qn = jnp.sum(sc, axis=-1) + inter_w * jnp.einsum("bhtd,bhd->bht", qc, n_st)
        h = num / jnp.maximum(jnp.abs(qn), jnp.exp(-m_t))[..., None]
        b_last = b[..., -1]
        a = b_last[..., None] - b + ic
        m_new = jnp.maximum(b_last + m_st, jnp.max(a, axis=-1))
        decay = jnp.exp(b_last + m_st - m_new)
        w = jnp.exp(a - m_new[..., None])
        c_new = decay[..., None, None] * c_st + jnp.einsum("bhs,bhsd,bhse->bhde", w, kc, vc)
        n_new = decay[..., None] * n_st + jnp.einsum("bhs,bhsd->bhd", w, kc)
        return (c_new, n_new, m_new), h

    init = (jnp.zeros((bsz, nh, dh, dh), jnp.float32),
            jnp.zeros((bsz, nh, dh), jnp.float32),
            jnp.zeros((bsz, nh), jnp.float32))
    _, h = lax.scan(step, init, xs)
    return jnp.moveaxis(h, 0, 2).reshape(bsz, nh, s, dh)

def first_inputs(seed: int = 0) -> dict:
    key = jax.random.key(seed)
    ks = jax.random.split(key, 24)
    f32 = jnp.float32

    def nrm(k, shape, scale):
        return jax.random.normal(k, shape, f32) * scale

    x = jax.random.normal(ks[0], (BATCH, SEQ, D_MODEL), f32)
    c = jax.random.normal(ks[1], (BATCH, D_MODEL), f32)
    w_ada = nrm(ks[2], (DEPTH, D_MODEL, N_MOD * D_MODEL), 0.5 * D_MODEL ** -0.5)
    b_ada = nrm(ks[3], (DEPTH, N_MOD * D_MODEL), 0.02)
    norm_mix_g = 1.0 + nrm(ks[4], (DEPTH, D_MODEL), 0.1)
    w_in = nrm(ks[5], (DEPTH, D_MODEL, N_IN), D_MODEL ** -0.5)
    f_bias = jnp.linspace(3.0, 6.0, MLSTM_HEADS, dtype=f32)
    b_in = nrm(ks[6], (DEPTH, N_IN), 0.02)
    b_in = b_in.at[:, F_BIAS_OFFSET:F_BIAS_OFFSET + MLSTM_HEADS].add(f_bias)
    conv_dw_w = nrm(ks[7], (DEPTH, CONV_KERNEL, CONV_WIDTH), CONV_KERNEL ** -0.5)
    conv_dw_b = nrm(ks[8], (DEPTH, CONV_WIDTH), 0.02)
    conv_ln_g = 1.0 + nrm(ks[9], (DEPTH, CONV_WIDTH), 0.1)
    conv_ln_b = nrm(ks[10], (DEPTH, CONV_WIDTH), 0.02)
    w_conv_pw = nrm(ks[11], (DEPTH, CONV_WIDTH, D_MODEL), CONV_WIDTH ** -0.5)
    b_conv_pw = nrm(ks[12], (DEPTH, D_MODEL), 0.02)
    qk_conv_w = nrm(ks[13], (DEPTH, QK_CONV, N_QK), QK_CONV ** -0.5)
    qk_conv_b = nrm(ks[14], (DEPTH, N_QK), 0.02)
    mlstm_norm_g = 1.0 + nrm(ks[15], (DEPTH, MLSTM_WIDTH), 0.1)
    w_out = nrm(ks[16], (DEPTH, D_MODEL, D_MODEL), D_MODEL ** -0.5)
    norm_ffn_g = 1.0 + nrm(ks[17], (DEPTH, D_MODEL), 0.1)
    w_ffn_up = nrm(ks[18], (DEPTH, D_MODEL, 2 * D_FF), D_MODEL ** -0.5)
    w_ffn_down = nrm(ks[19], (DEPTH, D_FF, D_MODEL), D_FF ** -0.5)
    final_norm_g = 1.0 + nrm(ks[20], (D_MODEL,), 0.1)
    return {"x": x, "c": c, "w_ada": w_ada, "b_ada": b_ada, "norm_mix_g": norm_mix_g,
            "w_in": w_in, "b_in": b_in, "conv_dw_w": conv_dw_w, "conv_dw_b": conv_dw_b,
            "conv_ln_g": conv_ln_g, "conv_ln_b": conv_ln_b, "w_conv_pw": w_conv_pw,
            "b_conv_pw": b_conv_pw, "qk_conv_w": qk_conv_w, "qk_conv_b": qk_conv_b,
            "mlstm_norm_g": mlstm_norm_g, "w_out": w_out, "norm_ffn_g": norm_ffn_g,
            "w_ffn_up": w_ffn_up, "w_ffn_down": w_ffn_down, "final_norm_g": final_norm_g}

def first_block(x, c, w_ada, b_ada, norm_mix_g, w_in, b_in, conv_dw_w, conv_dw_b,
              conv_ln_g, conv_ln_b, w_conv_pw, b_conv_pw, qk_conv_w, qk_conv_b,
              mlstm_norm_g, w_out, norm_ffn_g, w_ffn_up, w_ffn_down, final_norm_g):
    bsz, s, _ = x.shape
    for l in range(DEPTH):
        mod = jnp.einsum("bd,de->be", jax.nn.silu(c), w_ada[l]) + b_ada[l]
        sh1, sc1, g1, sh2, sc2, g2 = jnp.split(mod[:, None, :], N_MOD, axis=-1)

        h = rms_norm(x, norm_mix_g[l]) * (1.0 + sc1) + sh1
        proj = jnp.einsum("bsd,de->bse", h, w_in[l]) + b_in[l]
        glu_in, qk_in, v, o_pre, if_pre, merge_pre = jnp.split(proj, IN_SPLITS, axis=-1)

        a = glu_in[..., :CONV_WIDTH] * jax.nn.sigmoid(glu_in[..., CONV_WIDTH:])
        a = causal_depthwise_conv(a, conv_dw_w[l], conv_dw_b[l])
        a = jax.nn.silu(layer_norm(a, conv_ln_g[l], conv_ln_b[l]))
        y_conv = jnp.einsum("bsc,cd->bsd", a, w_conv_pw[l]) + b_conv_pw[l]

        qk = jax.nn.silu(causal_depthwise_conv(qk_in, qk_conv_w[l], qk_conv_b[l]))
        q, k = jnp.split(qk, 2, axis=-1)

        def heads(t):
            return t.reshape(bsz, s, MLSTM_HEADS, MLSTM_HEAD_DIM).transpose(0, 2, 1, 3).astype(jnp.float32)

        gates = jnp.moveaxis(if_pre, -1, 1).astype(jnp.float32)
        hm = mlstm_chunkwise(heads(q), heads(k) * (MLSTM_HEAD_DIM ** -0.5), heads(v),
                             gates[:, :MLSTM_HEADS], gates[:, MLSTM_HEADS:])
        mu = jnp.mean(hm, axis=-1, keepdims=True)
        var = jnp.mean(jnp.square(hm - mu), axis=-1, keepdims=True)
        hm = ((hm - mu) * lax.rsqrt(var + EPS)).transpose(0, 2, 1, 3).reshape(bsz, s, MLSTM_WIDTH)
        hm = (hm * mlstm_norm_g[l].astype(jnp.float32)).astype(x.dtype)
        y_mlstm = jax.nn.sigmoid(o_pre) * hm

        g_conv, g_mlstm = jnp.split(jax.nn.sigmoid(merge_pre), 2, axis=-1)
        y = jnp.einsum("bsd,de->bse", g_conv * y_conv + g_mlstm * y_mlstm, w_out[l])
        x = x + g1 * y

        h = rms_norm(x, norm_ffn_g[l]) * (1.0 + sc2) + sh2
        gt, up = jnp.split(jnp.einsum("bsd,df->bsf", h, w_ffn_up[l]), 2, axis=-1)
        x = x + g2 * jnp.einsum("bsf,fd->bsd", jax.nn.silu(gt) * up, w_ffn_down[l])
    return rms_norm(x, final_norm_g)


PLE_DIM = 256
D_MIX = D_MODEL
RET_HEADS = 4
RET_HEAD_DIM = 128
RET_WIDTH = RET_HEADS * RET_HEAD_DIM
RET_CHUNK = 128
MLA_HEADS = 8
MLA_NOPE_DIM = 64
MLA_ROPE_DIM = 32
MLA_QK_DIM = MLA_NOPE_DIM + MLA_ROPE_DIM
MLA_V_DIM = 64
MLA_WIDTH = MLA_HEADS * MLA_V_DIM
MLA_Q_LORA = 384
MLA_KV_LORA = 256
Q_BLOCK = 128
IN_COLS = 4 * RET_WIDTH + MLA_Q_LORA + MLA_KV_LORA + MLA_ROPE_DIM
D_FF_2 = ((8 * D_MODEL // 3 + 255) // 256) * 256
ROPE_BASE = 10000.0


def rmsnorm(x, w):
    xf = x.astype(jnp.float32)
    y = xf * lax.rsqrt(jnp.mean(xf * xf, axis=-1, keepdims=True) + EPS)
    return (y * w.astype(jnp.float32)).astype(x.dtype)

def head_groupnorm(x, w):
    xf = x.astype(jnp.float32)
    mu = jnp.mean(xf, axis=-1, keepdims=True)
    var = jnp.mean(jnp.square(xf - mu), axis=-1, keepdims=True)
    y = (xf - mu) * lax.rsqrt(var + EPS)
    B, S, H, d = x.shape
    return (y.reshape(B, S, H * d) * w.astype(jnp.float32)).astype(x.dtype)

def rope(x, positions):
    d = x.shape[-1]
    half = d // 2
    inv = 1.0 / (ROPE_BASE ** (jnp.arange(half, dtype=jnp.float32) / half))
    ang = positions.astype(jnp.float32)[..., None] * inv
    cos = jnp.cos(ang)[:, :, None, :].astype(x.dtype)
    sin = jnp.sin(ang)[:, :, None, :].astype(x.dtype)
    x1, x2 = x[..., :half], x[..., half:]
    return jnp.concatenate([x1 * cos - x2 * sin, x2 * cos + x1 * sin], axis=-1)

def retention_chunkwise(q, k, v):
    B, S, H, d = q.shape
    C = RET_CHUNK
    N = S // C
    dt = q.dtype
    log_g = jnp.log(1.0 - 2.0 ** (-5.0 - jnp.arange(H, dtype=jnp.float32)))
    j = jnp.arange(C, dtype=jnp.float32)
    diff = j[:, None] - j[None, :]
    D = jnp.where(diff[None] >= 0, jnp.exp(jnp.maximum(diff, 0.0)[None] * log_g[:, None, None]), 0.0).astype(dt)
    zeta = jnp.exp((C - 1 - j)[None, :] * log_g[:, None]).astype(dt)
    xi = jnp.exp((j + 1)[None, :] * log_g[:, None]).astype(dt)
    g_chunk = jnp.exp(C * log_g).astype(dt)

    qc = q.reshape(B, N, C, H, d)
    kc = k.reshape(B, N, C, H, d)
    vc = v.reshape(B, N, C, H, d)
    scores = jnp.einsum('bnchd,bnmhd->bnhcm', qc, kc) * D[None, None]
    inner = jnp.einsum('bnhcm,bnmhe->bnche', scores, vc)
    U = jnp.einsum('bnmhd,bnmhe,hm->nbhde', kc, vc, zeta)

    def step(R, u):
        return g_chunk[None, :, None, None] * R + u, R

    _, R_prev = lax.scan(step, jnp.zeros_like(U[0]), U)
    cross = jnp.einsum('bnchd,nbhde->bnche', qc, R_prev) * xi.T[None, None, :, :, None]
    return (inner + cross).reshape(B, S, H, d)

def mla_causal(q, k, v):
    B, S, H, dqk = q.shape
    dv = v.shape[-1]
    NB = S // Q_BLOCK
    scale = 1.0 / math.sqrt(dqk)
    kt = k.transpose(0, 2, 1, 3)
    vt = v.transpose(0, 2, 1, 3)
    qb = q.reshape(B, NB, Q_BLOCK, H, dqk).transpose(1, 0, 3, 2, 4)
    kpos = jnp.arange(S)

    def block(args):
        qi, bi = args
        s = jnp.einsum('bhqd,bhkd->bhqk', qi, kt).astype(jnp.float32) * scale
        qpos = bi * Q_BLOCK + jnp.arange(Q_BLOCK)
        mask = kpos[None, :] <= qpos[:, None]
        s = jnp.where(mask[None, None], s, -1e30)
        pr = jax.nn.softmax(s, axis=-1).astype(vt.dtype)
        return jnp.einsum('bhqk,bhkd->bhqd', pr, vt)

    out = lax.map(block, (qb, jnp.arange(NB)))
    return out.transpose(1, 0, 3, 2, 4).reshape(B, S, H * dv)

def token_mixer(xn, positions, w_in, ret_gn_w, mla_q_norm, w_uq, mla_kv_norm, w_ukv, w_o):
    B, S, _ = xn.shape
    proj = xn @ w_in
    o = 0
    rq = proj[..., o:o + RET_WIDTH]; o += RET_WIDTH
    rk = proj[..., o:o + RET_WIDTH]; o += RET_WIDTH
    rv = proj[..., o:o + RET_WIDTH]; o += RET_WIDTH
    rg = proj[..., o:o + RET_WIDTH]; o += RET_WIDTH
    cq = proj[..., o:o + MLA_Q_LORA]; o += MLA_Q_LORA
    ckv = proj[..., o:o + MLA_KV_LORA]; o += MLA_KV_LORA
    kr = proj[..., o:o + MLA_ROPE_DIM]

    shp = (B, S, RET_HEADS, RET_HEAD_DIM)
    rq = rope(rq.reshape(shp), positions)
    rk = rope(rk.reshape(shp), positions) * (RET_HEAD_DIM ** -0.5)
    ry = retention_chunkwise(rq, rk, rv.reshape(shp))
    ret_out = jax.nn.silu(rg) * head_groupnorm(ry, ret_gn_w)

    qh = (rmsnorm(cq, mla_q_norm) @ w_uq).reshape(B, S, MLA_HEADS, MLA_QK_DIM)
    q = jnp.concatenate([qh[..., :MLA_NOPE_DIM], rope(qh[..., MLA_NOPE_DIM:], positions)], axis=-1)
    kvh = (rmsnorm(ckv, mla_kv_norm) @ w_ukv).reshape(B, S, MLA_HEADS, MLA_NOPE_DIM + MLA_V_DIM)
    k_rope = rope(kr[:, :, None, :], positions)
    k = jnp.concatenate([kvh[..., :MLA_NOPE_DIM],
                         jnp.broadcast_to(k_rope, (B, S, MLA_HEADS, MLA_ROPE_DIM))], axis=-1)
    v = kvh[..., MLA_NOPE_DIM:]
    mla_out = mla_causal(q, k, v)

    return jnp.concatenate([ret_out, mla_out], axis=-1) @ w_o

def second_inputs(seed: int = 0) -> dict:
    key = jax.random.key(seed)
    ks = jax.random.split(key, 24)
    L = DEPTH

    def nrm(k, shape, fan_in):
        return jax.random.normal(k, shape, jnp.float32) * (fan_in ** -0.5)

    def gain(k, shape):
        return 1.0 + 0.05 * jax.random.normal(k, shape, jnp.float32)

    return {
        "x": jax.random.normal(ks[0], (BATCH, SEQ, D_MODEL), jnp.float32),
        "p": jax.random.normal(ks[1], (DEPTH, BATCH, SEQ, PLE_DIM), jnp.float32),
        "positions": jnp.broadcast_to(jnp.arange(SEQ, dtype=jnp.int32)[None], (BATCH, SEQ)),
        "pre_mix_norm": gain(ks[2], (L, D_MODEL)),
        "w_in": nrm(ks[3], (L, D_MODEL, IN_COLS), D_MODEL),
        "ret_gn_w": gain(ks[4], (L, RET_WIDTH)),
        "mla_q_norm": gain(ks[5], (L, MLA_Q_LORA)),
        "w_uq": nrm(ks[6], (L, MLA_Q_LORA, MLA_HEADS * MLA_QK_DIM), MLA_Q_LORA),
        "mla_kv_norm": gain(ks[7], (L, MLA_KV_LORA)),
        "w_ukv": nrm(ks[8], (L, MLA_KV_LORA, MLA_HEADS * (MLA_NOPE_DIM + MLA_V_DIM)), MLA_KV_LORA),
        "w_o": nrm(ks[9], (L, D_MIX, D_MODEL), D_MIX),
        "post_mix_norm": gain(ks[10], (L, D_MODEL)),
        "pre_ffn_norm": gain(ks[11], (L, D_MODEL)),
        "w_gate": nrm(ks[12], (L, D_MODEL, D_FF_2), D_MODEL),
        "w_up": nrm(ks[13], (L, D_MODEL, D_FF_2), D_MODEL),
        "w_down": nrm(ks[14], (L, D_FF_2, D_MODEL), D_FF_2),
        "post_ffn_norm": gain(ks[15], (L, D_MODEL)),
        "w_ple_proj": nrm(ks[16], (L, PLE_DIM, D_MODEL), PLE_DIM),
        "ple_norm": gain(ks[17], (L, D_MODEL)),
        "w_ple_gate": nrm(ks[18], (L, D_MODEL, D_MODEL), D_MODEL),
        "b_ple_gate": 0.02 * jax.random.normal(ks[19], (L, D_MODEL), jnp.float32),
    }

def second_block(x, p, positions, pre_mix_norm, w_in, ret_gn_w, mla_q_norm, w_uq, mla_kv_norm,
              w_ukv, w_o, post_mix_norm, pre_ffn_norm, w_gate, w_up, w_down, post_ffn_norm,
              w_ple_proj, ple_norm, w_ple_gate, b_ple_gate):
    h = x
    for i in range(DEPTH):
        xn = rmsnorm(h, pre_mix_norm[i])
        mix = token_mixer(xn, positions, w_in[i], ret_gn_w[i], mla_q_norm[i], w_uq[i],
                          mla_kv_norm[i], w_ukv[i], w_o[i])
        h = h + rmsnorm(mix, post_mix_norm[i])
        hn = rmsnorm(h, pre_ffn_norm[i])
        ff = (jax.nn.silu(hn @ w_gate[i]) * (hn @ w_up[i])) @ w_down[i]
        h = h + rmsnorm(ff, post_ffn_norm[i])
        e = rmsnorm(p[i] @ w_ple_proj[i], ple_norm[i])
        gate = jax.nn.sigmoid(h @ w_ple_gate[i] + b_ple_gate[i])
        h = h + e * gate
    return h


def setup_inputs(seed=0):
    out = dict(first_inputs(seed))
    for name, value in second_inputs(seed + 1).items():
        if name != "x":
            out[name + "_2"] = value
    return out


def reference(
    x, c, w_ada, b_ada, norm_mix_g, w_in, b_in, conv_dw_w, conv_dw_b, conv_ln_g, conv_ln_b,
    w_conv_pw, b_conv_pw, qk_conv_w, qk_conv_b, mlstm_norm_g, w_out, norm_ffn_g, w_ffn_up,
    w_ffn_down, final_norm_g, p_2, positions_2, pre_mix_norm_2, w_in_2, ret_gn_w_2,
    mla_q_norm_2, w_uq_2, mla_kv_norm_2, w_ukv_2, w_o_2, post_mix_norm_2, pre_ffn_norm_2,
    w_gate_2, w_up_2, w_down_2, post_ffn_norm_2, w_ple_proj_2, ple_norm_2, w_ple_gate_2,
    b_ple_gate_2,
):
    x = first_block(
        x, c, w_ada, b_ada, norm_mix_g, w_in, b_in, conv_dw_w, conv_dw_b, conv_ln_g, conv_ln_b,
        w_conv_pw, b_conv_pw, qk_conv_w, qk_conv_b, mlstm_norm_g, w_out, norm_ffn_g, w_ffn_up,
        w_ffn_down, final_norm_g,
    )
    return second_block(
        x, p_2, positions_2, pre_mix_norm_2, w_in_2, ret_gn_w_2, mla_q_norm_2, w_uq_2,
        mla_kv_norm_2, w_ukv_2, w_o_2, post_mix_norm_2, pre_ffn_norm_2, w_gate_2, w_up_2,
        w_down_2, post_ffn_norm_2, w_ple_proj_2, ple_norm_2, w_ple_gate_2, b_ple_gate_2,
    )


_drawn_inputs = setup_inputs


def setup_inputs(seed=0):
    import zlib

    import numpy as np

    out = dict(_drawn_inputs(seed))
    spreads = {}
    factors = {'conv_dw_b': 7.233,
     'conv_ln_b': 8.0,
     'b_conv_pw': 8.0,
     'qk_conv_b': 8.0,
     'mlstm_norm_g': 3.301,
     'mla_q_norm_2': 6.58,
     'mla_kv_norm_2': 4.16,
     'ple_norm_2': 3.585,
     'b_ple_gate_2': 8.0,
     'ret_gn_w_2': 8.0}
    for name, (base, spread) in spreads.items():
        noise = np.random.default_rng([zlib.crc32(name.encode()), seed]).standard_normal(out[name].shape)
        drawn = base * np.exp(spread * noise) if base else spread * noise
        out[name] = __import__('jax').numpy.asarray(drawn.astype(out[name].dtype))
    for name, factor in factors.items():
        out[name] = (out[name] * factor).astype(out[name].dtype)
    return out
```

```python
from contextlib import ExitStack

import numpy as np

import concourse.bass as bass
from concourse import mybir

ALU = mybir.AluOpType
ACT = mybir.ActivationFunctionType
AX = mybir.AxisListType
F32 = mybir.dt.float32
F32R = mybir.dt.float32r
I32 = mybir.dt.int32

D, S, T = 1024, 512, 4
NF = 2816
NFT = NF // 128
EPS = 1e-6
BIG = 1e30
CHUNK = 8

VEC = {}
_at = 0
for _name, _n in [("c", 8), ("b_ada", 48), ("g_mix", 8), ("b_glu", 16), ("b_qk", 16), ("b_o", 8), ("b_mg", 16),
                  ("b_if", 1), ("dw_b", 8), ("ln_g", 8), ("ln_b", 8), ("b_pw", 8), ("qk_b", 16), ("ml_g", 8),
                  ("g_ffn", 8), ("g_fin", 8), ("g_pre", 8), ("ret_g", 4), ("g_q", 3), ("g_kv", 2), ("g_post", 8),
                  ("g_pf", 8), ("g_pof", 8), ("g_ple", 8), ("b_pg", 8), ("dw_w", 248), ("qk_w", 64)]:
    VEC[_name] = _at
    _at += _n
NVEC = _at
CONST = {"ident": 0, "mbig": 128, "mneg": 256, "invr": 384, "invm": 385, "sgr": 386, "sgm": 387}
NCONST = 388

TWO_PI_1 = 6.28125
TWO_PI_2 = float(np.float32(int((2 * np.pi - TWO_PI_1) * 2 ** 21) / 2 ** 21))
TWO_PI_3 = float(np.float32(2 * np.pi - TWO_PI_1 - TWO_PI_2))
MAGIC = 12582912.0


class Engine:

    def __init__(self, sem):
        self.sem, self.n, self.items, self.waited = sem, 0, [], {}

    def wait(self, after):
        if after is None:
            return
        if isinstance(after, list):
            for a in after:
                self.wait(a)
            return
        sem, value = after
        if self.waited.get(sem, 0) < value:
            self.waited[sem] = value
            self.items.append(lambda e: e.wait_ge(sem, value))

    def do(self, issue, after=None, mark=True):
        self.wait(after)
        if not mark:
            self.items.append(issue)
            return None
        self.n += 1
        sem = self.sem
        self.items.append(lambda e: issue(e).then_inc(sem, 1))
        return (sem, self.n)

    def last(self):
        return (self.sem, self.n)


class Queue:

    def __init__(self, engine):
        self.engine, self.total = engine, {}

    def load(self, sem, out, in_, after=None):
        self.engine.wait(after)
        self.total[sem] = self.total.get(sem, 0) + 16
        self.engine.items.append(lambda e: e.dma_start(out, in_).then_inc(sem, 16))
        return (sem, self.total[sem])


class Slots:

    def __init__(self, n):
        self.free = [(i, []) for i in range(n)]

    def take(self):
        return self.free.pop(0)

    def give(self, i, after):
        self.free.append((i, after))


def program(nc, A, out):
    ctx = ExitStack()
    with ctx:
        def sem(name):
            return ctx.enter_context(nc.semaphore(name))

        base = 16512

        def at(name, off, shape, dt=F32):
            return nc.alloc_sbuf_tensor_at(name, shape, dt, offset=base + off)

        P_ = [ctx.enter_context(nc.psum_tensor(f"bank{i}", [128, 512], F32)) for i in range(8)]
        o = 0
        XT = at("XT", o, [128, 8, S]); o += 16384
        HH = at("HH", o, [128, 8, S], F32R)
        FFO = at("FFO", o, [128, 8, S]); o += 16384
        HL = at("HL", o, [128, 8, S], F32R); o += 16384
        NRAW, NSPL = 4, 3
        RAW = [at(f"raw{i}", o + 4096 * i, [128, 1024]) for i in range(NRAW)]; o += 4096 * NRAW
        SPH = [at(f"sph{i}", o + 4096 * i, [128, 1024], F32R) for i in range(NSPL)]; o += 4096 * NSPL
        SPL = [at(f"spl{i}", o + 4096 * i, [128, 1024], F32R) for i in range(NSPL)]; o += 4096 * NSPL
        V_ = at("vecs", o, [128, NVEC]); o += (NVEC * 4 + 31) // 32 * 32
        C_ = at("consts", o, [128, NCONST]); o += (NCONST * 4 + 31) // 32 * 32
        ONES = at("ones", o, [128, 128]); o += 512
        SM = at("small", o, [128, 256]); o += 1024
        KEEP = at("kept", o, [128, 160]); o += 640
        MOD = at("mod", o, [128, 48]); o += 192
        XP = at("xpad", o, [128, 2, 516])
        KVL = at("kvl", o, [128, 2, S], F32R); o += 4128
        HT = at("htok", o, [128, 4, 258])
        KVH = at("kvh", o, [128, 2, S], F32R); o += 4128
        MROW = at("mrow", o, [4, S]); o += 2048
        NT = 6
        TMP = [at(f"tmp{i}", o + 2048 * i, [128, S]) for i in range(NT)]; o += 2048 * NT
        B = o
        MH = at("midh", B, [128, NFT, S], F32R)
        ML = at("midl", B + NFT * 2048, [128, NFT, S], F32R)
        CP = at("convin", B, [128, 8, 542])
        GC = at("gconv", B, [128, 8, S])
        CO = at("convout", B + 17344, [128, 8, S])
        VT = at("vtok", B + 33728, [128, T, 4, 257])
        QK = at("qk", B + 50176, [128, 2, 4, S])
        HM = at("hm", B + 66560, [128, 8, S])
        SC = at("sc", B + 82944, [128, 1280])
        VB = at("vbias", B + 82944, [128, 1024])
        SEL = at("sel", B + 88064, [4, 4, 128])
        ADA = [at(f"ada{i}", B + 33728 + 8192 * i, [128, 8, 256]) for i in range(6)]
        ROWS = [at(f"row{i}", B + 50176 + 2048 * i, [4, S]) for i in range(4)]
        ROWC = at("rowc", B + 50176 + 8192, [4, 10, 128])
        AH = at("ah", B + 33728, [128, 8, S], F32R)
        AL = at("al", B + 33728 + 16384, [128, 8, S], F32R)
        RQ = at("rq", B, [128, 4, S])
        RK = at("rk", B + 8192, [128, 4, S])
        RV = at("rv", B + 16384, [128, T, S])
        SRG = at("srg", B + 24576, [128, 4, S])
        RD = at("rd", B + 32768, [128, 4, S])
        RY = at("ry", B + 40960, [128, T, S])
        SC2 = at("sc2", B + 49152, [128, 1280])
        CQ = at("cq", B + 54272, [128, 3, S])
        CKV = at("ckv", B + 60416, [128, 2, S])
        TRIG = at("trig", B + 64512, [128, 4, S])
        KR = at("kr", B + 72704, [128, S])
        CQH = at("cqh", B + 74752, [128, 3, S], F32R)
        CQL = at("cql", B + 74752 + 6144, [128, 3, S], F32R)
        QH = at("qh", B, [96, 8, S])
        KH = at("kh", B + 16384, [96, 8, S])
        VM = at("vm", B + 32768, [128, T, S])
        MO = at("mo", B + 40960, [128, T, S])
        MIXO = at("mixo", B + 54272, [128, 8, S])
        PTS = at("pts", B, [128, 2, S])
        PTH = at("pth", B + 4096, [128, 2, S], F32R)
        PTL = at("ptl", B + 8192, [128, 2, S], F32R)
        EE = at("ee", B + 16384, [128, 8, S])
        assert base + B + 90112 <= 229368, base + B + 90112

        pe, act, dve, pool, sp = (Engine(sem(n)) for n in ("s_pe", "s_act", "s_dve", "s_pool", "s_sp"))
        loads = Queue(sp)
        s_raw = [sem(f"s_raw{i}") for i in range(NRAW)]
        s_ada = [sem(f"s_ada{i}") for i in range(6)]
        s_out = sem("s_out")

        def once(name, out_, in_, after=None):
            return loads.load(sem(name), out_, in_, after)

        def mm(out_, l, r, start, stop, after=None, mark=False):
            return pe.do(lambda e: e.matmul(out_, l, r, start=start, stop=stop), after, mark)

        def tr(out_, in_, ident, after=None, mark=False):
            return pe.do(lambda e: e.transpose(out_, in_, ident), after, mark)

        def ac(out_, in_, f, after=None, bias=0.0, scale=1.0, accum=None):
            if accum is not None:
                return act.do(lambda e: e.activation(out_, in_, f, bias=bias, scale=scale, accum_out=accum), after)
            return act.do(lambda e: e.activation(out_, in_, f, bias=bias, scale=scale), after)

        def tt(out_, a, b, op, after=None, eng=None):
            return (eng or dve).do(lambda e: e.tensor_tensor(out_, a, b, op), after)

        def ts(out_, a, s1, s2, op0, op1=None, after=None, eng=None):
            if op1 is None:
                return (eng or dve).do(lambda e: e.tensor_scalar(out_, a, s1, None, op0), after)
            return (eng or dve).do(lambda e: e.tensor_scalar(out_, a, s1, s2, op0, op1), after)

        def stt(out_, a, s1, b, op0, op1, after=None):
            return dve.do(lambda e: e.scalar_tensor_tensor(out_, a, s1, b, op0, op1), after)

        def cp(out_, a, after=None, eng=None):
            return (eng or dve).do(lambda e: e.tensor_copy(out_, a), after)

        def setv(out_, v, after=None, eng=None):
            return (eng or pool).do(lambda e: e.memset(out_, v), after)

        def recip(out_, a, after=None):
            return dve.do(lambda e: e.reciprocal(out_, a), after)

        def vec(name, i, p=slice(0, 128)):
            return V_[p, VEC[name] + i:VEC[name] + i + 1]

        def const(name, p=slice(0, 128)):
            return C_[p, CONST[name]:CONST[name] + 1]

        IDENT = C_[:, 0:128]
        MBIG = C_[:, 128:256]
        MNEG = C_[:, 256:384]

        main, misc, tmp = Slots(4), Slots(4), Slots(NT)

        def mbank():
            i, t = misc.take()
            return 4 + i, P_[4 + i], t

        def mgive(i, t):
            misc.give(i - 4, t)

        def fence():
            return [pe.last(), act.last(), dve.last(), pool.last()]

        class Weights:
            def __init__(self, plan):
                self.plan, self.seen = plan, []
                self.raw_after = [None] * NRAW
                self.spl_after = [None] * NSPL
                self.loaded = self.cut = self.used = 0
                self.raw_tok, self.spl_tok = {}, {}

            def load(self):
                n = self.loaded
                if n >= len(self.plan):
                    return
                name, tile, first, size = self.plan[n]
                src = A[name][tile, :, first:first + size]
                self.raw_tok[n] = loads.load(s_raw[n % NRAW], RAW[n % NRAW][:, 0:size], src, self.raw_after[n % NRAW])
                self.loaded += 1

            def start(self):
                for _ in range(NRAW):
                    self.load()

            def split(self):
                n = self.cut
                size = self.plan[n][3]
                raw, hi, lo = RAW[n % NRAW][:, 0:size], SPH[n % NSPL][:, 0:size], SPL[n % NSPL][:, 0:size]
                a = ac(hi, raw, ACT.Copy, [self.raw_tok[n], self.spl_after[n % NSPL]])
                b = tt(lo, raw, hi.bitcast(F32), ALU.subtract, [a, self.raw_tok[n], self.spl_after[n % NSPL]],
                       eng=lo_engine[0])
                self.raw_after[n % NRAW] = [a, b]
                self.spl_tok[n] = [a, b]
                self.cut += 1
                self.load()

            def take(self, name, tile, first, size):
                self.seen.append((name, tile, first, size))
                n = self.used
                self.used += 1
                if not self.plan:
                    return n, SPH[n % NSPL][:, 0:size], SPL[n % NSPL][:, 0:size], None
                while self.cut < min(n + NSPL, len(self.plan)):
                    self.split()
                return n, SPH[n % NSPL][:, 0:size], SPL[n % NSPL][:, 0:size], self.spl_tok[n]

            def done(self, n, tok):
                self.spl_after[n % NSPL] = tok

        lo_engine = [pool]
        held = {}
        W = Weights(A["plan"])

        def gemm(src, tile_no, kt, hi, lo, after, evac):
            b, free = main.take()
            k0 = 0
            while k0 < kt:
                kn = min(CHUNK, kt - k0)
                n, wh, wl, wt = W.take(src, tile_no, k0 * 128, kn * 128)
                for k in range(kn):
                    h, l = wh[:, k * 128:(k + 1) * 128], wl[:, k * 128:(k + 1) * 128]
                    kk = k0 + k
                    mm(P_[b][:], h, hi(kk), kk == 0, False, [wt, after, free])
                    mm(P_[b][:], h, lo(kk), False, False)
                    t = mm(P_[b][:], l, hi(kk), False, kk == kt - 1, mark=(k == kn - 1))
                W.done(n, t)
                k0 += kn
            held["bank"] = b
            freed = evac(P_[b], t)
            if freed is not None:
                main.give(b, freed)

        def gemm_tok(src, block, kt, hi, lo, after, evac):
            banks = [main.take() for _ in range(T)]
            for k0 in range(0, kt, 2):
                n, wh, wl, wt = W.take(src, block, k0 * 512, 1024)
                for k in range(2):
                    kk = k0 + k
                    h, l = wh[:, k * 512:(k + 1) * 512], wl[:, k * 512:(k + 1) * 512]
                    for t in range(T):
                        b, free = banks[t]
                        q = slice(t * 128, (t + 1) * 128)
                        mm(P_[b][:], hi(kk)[:, q], h, kk == 0, False, [wt, after, free])
                        mm(P_[b][:], hi(kk)[:, q], l, False, False)
                        tok = mm(P_[b][:], lo(kk)[:, q], h, False, kk == kt - 1, mark=True)
                W.done(n, tok)
            for t in range(T):
                main.give(banks[t][0], evac(t, P_[banks[t][0]], tok))

        small = [0]

        def scratch(n):
            if small[0] + n > 256:
                small[0] = 0
            a = small[0]
            small[0] += n
            return SM[:, a:a + n]

        kept = [0]

        def keepc(n):
            kept[0] += n
            assert kept[0] <= 160
            return KEEP[:, kept[0] - n:kept[0]]

        def rsqrt_cols(src, n, scale, after):
            v, q, r = scratch(n), scratch(n), scratch(n)
            t = ts(v, src, scale, EPS, ALU.mult, ALU.add, after)
            t = ac(q, v, ACT.Sqrt, t)
            return r, recip(r, q, t)

        class SumSq:

            def __init__(self):
                (self.a, self.free), self.t = tmp.take(), None

            def add(self, x, after):
                if self.t is None:
                    self.t = ac(TMP[self.a][:], x, ACT.Square, [after, self.free])
                else:
                    i, free = tmp.take()
                    s = ac(TMP[i][:], x, ACT.Square, [after, free])
                    self.t = tt(TMP[self.a][:], TMP[self.a][:], TMP[i][:], ALU.add, [s, self.t])
                    tmp.give(i, [self.t])
                return self.t

            def rows(self, width):
                b, bank, free = mbank()
                for t in range(T):
                    tok = mm(bank[:, t:t + 1], TMP[self.a][:, t * 128:(t + 1) * 128], ONES[:, 0:1], True, True,
                             [self.t, free, ones], mark=(t == T - 1))
                r, rt = rsqrt_cols(bank[:, 0:T], T, 1.0 / width, tok)
                for t in range(T):
                    dt_ = ts(TMP[self.a][:, t * 128:(t + 1) * 128], IDENT, r[:, t:t + 1], None, ALU.mult,
                             after=[rt, tok])
                for t in range(T):
                    q = slice(t * 128, (t + 1) * 128)
                    tok = mm(bank[:, q], ONES[:], TMP[self.a][:, q], True, True, [dt_, rt], mark=(t == T - 1))
                tmp.give(self.a, [tok])
                return b, bank, tok

        def cut(x, hi, lo, after, after_lo=None, shift=None):
            if shift is None:
                a = ac(hi, x, ACT.Copy, after)
                return [a, tt(lo, x, hi.bitcast(F32), ALU.subtract, [a, after])]
            a = ac(hi, x, ACT.Identity, after, bias=shift)
            return [a, stt(lo, x, shift, hi.bitcast(F32), ALU.add, ALU.subtract, [a, after])]

        def normed(x, n, scale, rows, after, hi, lo, shift=None):
            b, bank, rt = rows
            out_ = []
            for i in range(n):
                j, free = tmp.take()
                t = stt(TMP[j][:], x(i), scale(i), bank[:], ALU.mult, ALU.mult, [rt, after, free])
                c = cut(TMP[j][:], hi(i), lo(i), [t, after], shift=None if shift is None else shift(i))
                tmp.give(j, c)
                out_.append(c)
            mgive(b, [t])
            return out_

        cst = once("l_c", C_[:], A["consts"])
        vecs = once("l_v", V_[:], A["vecs"])
        xt = once("l_x", XT[:], A["xT"])
        ada_src = A["w_ada"]
        ada_tok = [loads.load(s_ada[i], ADA[i][:], ada_src[i]) for i in range(6)]
        ones = setv(ONES[:], 1.0)
        zpad = [setv(CP[:, :, 0:30], 0.0), setv(XP[:, :, 0:3], 0.0)]

        csil = keepc(8)
        cs = ac(csil, V_[:, VEC["c"]:VEC["c"] + 8], ACT.Silu, vecs)
        mod_a, mod_b = mbank(), mbank()
        mod_done = [0]

        def ada(ch):
            i, free = tmp.take()
            acc = TMP[i][:, 0:256]
            wt = ADA[ch % 6]
            t = ts(acc, wt[:, 0, :], csil[:, 0:1], None, ALU.mult, after=[cs, ada_tok[ch], free])
            for k in range(1, 8):
                t = stt(acc, wt[:, k, :], csil[:, k:k + 1], acc, ALU.mult, ALU.add, t)
            if ch + 6 < 24:
                ada_tok.append(loads.load(s_ada[ch % 6], ADA[ch % 6][:], ada_src[ch + 6], t))
            _, bank, bfree = mod_a if ch < 8 else mod_b
            for j in range(2):
                c = 2 * ch + j - (0 if ch < 8 else 16)
                m = mm(bank[:, c:c + 1], acc[:, j * 128:(j + 1) * 128], ONES[:, 0:1], True, True,
                       [t, ones, bfree], mark=(j == 1))
            tmp.give(i, [m])
            return m

        for ch in range(8):
            m = ada(ch)
        if A["plan"]:
            W.start()
        moda = tt(MOD[:, 0:16], mod_a[1][:, 0:16], V_[:, VEC["b_ada"]:VEC["b_ada"] + 16], ALU.add, [m, vecs])
        mgive(mod_a[0], [moda])
        gmix = keepc(8)
        gm = stt(gmix, MOD[:, 8:16], 1.0, V_[:, VEC["g_mix"]:VEC["g_mix"] + 8], ALU.add, ALU.mult, [moda])

        ss = SumSq()
        for i in range(8):
            ss.add(XT[:, i, :], xt)
        rows = ss.rows(D)
        h_tok = normed(lambda i: XT[:, i, :], 8, lambda i: gmix[:, i:i + 1], rows, [gm, moda],
                       lambda i: HH[:, i, :], lambda i: HL[:, i, :], lambda i: MOD[:, i:i + 1])
        hi, lo = (lambda k: HH[:, k, :]), (lambda k: HL[:, k, :])

        conv_ready = {}
        conv_ops = []
        conv_tok = [None] * 8

        def tap(i, j):
            src = CP[:, i, j:j + 512]
            w = V_[:, VEC["dw_w"] + i * 31 + j:VEC["dw_w"] + i * 31 + j + 1]
            if j == 0:
                conv_tok[i] = ts(CO[:, i, :], src, w, vec("dw_b", i), ALU.mult, ALU.add, [conv_ready[i], zpad[0]])
            else:
                conv_tok[i] = stt(CO[:, i, :], src, w, CO[:, i, :], ALU.mult, ALU.add, conv_tok[i])

        def background(n):
            for _ in range(min(n, len(conv_ops))):
                tap(*conv_ops.pop(0))

        W_IN = "w_in"
        for i in range(8):
            pending = {}

            def keep(bank, t):
                pending["v"] = (held["bank"], t)
                return None

            def evac(bank, t):
                j, free = tmp.take()
                a = ac(TMP[j][:], bank[:], ACT.Sigmoid, [t, free, vecs], bias=vec("b_glu", 8 + i))
                v, vt = pending["v"]
                c = stt(CP[:, i, 30:542], P_[v][:], vec("b_glu", i), TMP[j][:], ALU.add, ALU.mult, [a, vt])
                tmp.give(j, [c])
                main.give(v, [c])
                conv_ready[i] = c
                return [a]

            gemm(W_IN, i, 8, hi, lo, h_tok, keep)
            gemm(W_IN, 8 + i, 8, hi, lo, h_tok, evac)
            if i % 2:
                conv_ops += [(i - 1 + z, j) for j in range(31) for z in range(2)]
            for ch in (8 + 2 * i, 9 + 2 * i):
                m = ada(ch)
            background(2)
        modb = tt(MOD[:, 16:48], mod_b[1][:, 0:32], V_[:, VEC["b_ada"] + 16:VEC["b_ada"] + 48], ALU.add, [m, vecs])
        mgive(mod_b[0], [modb])

        f = fence()
        vb_tok = once("l_vb", VB[:], A["b_v"].broadcast_to([128, 1024]), f)
        sel_tok = once("l_sel", SEL[:], A["sel"], f)
        von = setv(VT[:, :, :, 256:257], 1.0, f)
        v_tok = []
        for blk in range(2):
            def evac(t, bank, tok):
                dst = VT[:, t, 2 * blk:2 * blk + 2, 0:256]
                c = tt(dst, bank[:].rearrange("p (a b) -> p a b", a=2),
                       VB[:, blk * 512:(blk + 1) * 512].rearrange("p (a b) -> p a b", a=2), ALU.add,
                       [tok, vb_tok, f])
                v_tok.append(c)
                return [c]
            gemm_tok("w_v", blk, 8, hi, lo, None, evac)
            background(24)
        IR, LF, BR, CR = ROWS

        def gates(bank, t):
            p = slice(32, 36)
            j, free = tmp.take()
            z = TMP[j]
            a0 = ac(IR[:], bank[0:4, :], ACT.Identity, [t, f], bias=vec("b_if", 0, slice(0, 4)))
            a1 = ac(z[p, :], bank[p, :], ACT.Identity, [free], bias=vec("b_if", 0, p))
            k, free2 = tmp.take()
            y = TMP[k]
            a2 = ac(y[p, :], z[p, :], ACT.Abs, [a1, free2])
            a3 = ac(y[p, :], y[p, :], ACT.Exp, a2, scale=-1.0)
            a4 = ac(y[p, :], y[p, :], ACT.Ln, a3, bias=1.0)
            c = stt(LF[:], z[p, :], 0.0, y[p, :], ALU.min, ALU.subtract, [a4, a1, f])
            tmp.give(j, [c])
            tmp.give(k, [c])
            held["g"] = [a0, c]
            return [a0, a1]

        gemm("w_if", 0, 8, hi, lo, None, gates)
        g = held["g"]
        k1, freek = tmp.take()
        onerow = TMP[k1][0:4, 0:128]
        t1 = setv(onerow, 1.0, freek)
        mus = keepc(8)
        mu0 = setv(mus[0:4, 0:1], 0.0, fence())
        ct = [g, t1, mu0]
        for t in range(T):
            q = slice(t * 128, (t + 1) * 128)
            e = slice((t + 1) * 128 - 1, (t + 1) * 128)
            b_ = dve.do(lambda eng, q=q: eng.tensor_tensor_scan(BR[:, q], onerow, LF[:, q], 0.0, ALU.mult, ALU.add), ct)
            c_ = tt(CR[:, q], IR[:, q], BR[:, q], ALU.subtract, [b_, g])
            m_ = dve.do(lambda eng, q=q, t=t: eng.tensor_tensor_scan(
                MROW[:, q], CR[:, q], CR[:, q], mus[0:4, t:t + 1], ALU.max, ALU.max), [c_, mu0])
            ct = [tt(mus[0:4, t + 1:t + 2], MROW[:, e], BR[:, e], ALU.add, [m_, b_])]
        tmp.give(k1, [ct[0]])
        pair = {}
        n = 0
        for k in range(T):
            kq = slice(k * 128, (k + 1) * 128)
            for t in range(k, T):
                pair[(k, t)] = n
                if t == k:
                    z = cp(ROWC[:, n, :], CR[:, kq], ct)
                else:
                    z = ts(ROWC[:, n, :], ROWC[:, n - 1, :], BR[:, t * 128 - 1:t * 128], None, ALU.add, after=z)
                n += 1
        mr = tt(IR[:], MROW[:], BR[:], ALU.add, [z])
        b, bank, free = mbank()
        for i in range(10):
            tk = tr(bank[:, 4 * i:4 * i + 4], ROWC[:, i, :], IDENT[0:4, 0:4], [z, free, cst])
        for t in range(T):
            tk = tr(bank[:, 40 + 4 * t:44 + 4 * t], IR[:, t * 128:(t + 1) * 128], IDENT[0:4, 0:4], [mr], mark=(t == 3))
        CB = keepc(40)
        cb = cp(CB, bank[:, 0:40], tk)
        GD = keepc(16)
        gd = ac(GD, bank[:, 40:56], ACT.Exp, [tk, cb], scale=-1.0)
        mgive(b, [cb, gd])

        f = fence()
        hm_tok = [None] * 8
        xp_free = [zpad[1], zpad[1]]
        qk_w = 0

        def qk_tile(tile_no, dst, w_at, b_at, after):
            def evac(bank, t):
                s = (tile_no) % 2
                a = ac(XP[:, s, 3:515], bank[:], ACT.Identity, [t, xp_free[s]], bias=vec("b_qk", b_at))
                j, free = tmp.take()
                w = lambda tap_: V_[:, VEC["qk_w"] + 4 * b_at + tap_:VEC["qk_w"] + 4 * b_at + tap_ + 1]
                c = ts(TMP[j][:], XP[:, s, 0:512], w(0), vec("qk_b", b_at), ALU.mult, ALU.add, [a, free])
                for z_ in range(1, 4):
                    c = stt(TMP[j][:], XP[:, s, z_:z_ + 512], w(z_), TMP[j][:], ALU.mult, ALU.add, c)
                xp_free[s] = c
                r = ac(dst, TMP[j][:], ACT.Silu, [c, after])
                tmp.give(j, [r])
                held["qk"].append(r)
                return [a]
            return evac

        qk_used = [f, f]
        sc_used = [f]

        def attend(h, qk_done):
            s = h % 2
            mb, mbk, free = mbank()
            mt = mm(mbk[:], SEL[:, h, :], MROW[:], True, True, [ct, sel_tok, free], mark=True)
            jm, freem = tmp.take()
            mrows = TMP[jm]
            mt = ac(mrows[:], mbk[:], ACT.Copy, [mt, freem])
            mgive(mb, [mt])
            off = 0
            sct = []
            offs = {}
            for k in range(T):
                wdt = (T - k) * 128
                b_, bk, free = mbank()
                for d_ in range(2):
                    st = mm(bk[:, 0:wdt], QK[:, s, 2 + d_, k * 128:(k + 1) * 128], QK[:, s, d_, k * 128:512],
                            d_ == 0, d_ == 1, [qk_done, free], mark=(d_ == 1))
                j, freej = tmp.take()
                dm = TMP[j]
                a0 = tt(dm[:, 0:128], mrows[:, k * 128:(k + 1) * 128], MBIG, ALU.add, [mt, freej, cst])
                last = []
                for t in range(k, T):
                    col = CB[:, 4 * pair[(k, t)] + h:4 * pair[(k, t)] + h + 1]
                    src = dm[:, 0:128] if t == k else mrows[:, t * 128:(t + 1) * 128]
                    e_ = ac(dm[:, (t - k) * 128:(t - k + 1) * 128], src, ACT.Exp, [a0, mt, cb, freej], bias=col, scale=-1.0)
                x_ = stt(SC[:, off:off + wdt], bk[:, 0:wdt], 0.0625, dm[:, 0:wdt], ALU.mult, ALU.mult,
                         [st, e_, sc_used[0]])
                tmp.give(j, [x_])
                mgive(b_, [x_])
                offs[k] = off
                off += wdt
                sct.append(x_)
            tmp.give(jm, [e_, a0])
            qk_used[s] = [st]
            ht = []
            stats = []
            for t in range(T):
                b_, bk, free = mbank()
                for k in range(t + 1):
                    c0 = offs[k] + (t - k) * 128
                    pt = mm(bk[:, 0:257], SC[:, c0:c0 + 128], VT[:, k, h, :], k == 0, k == t,
                            [sct, v_tok, von, free], mark=(k == t))
                a_ = ac(HT[:, t, 0:257], bk[:, 0:257], ACT.Copy, [pt, held.get("ht")])
                mgive(b_, [a_])
                ht.append(a_)
            sc_used[0] = pt
            held["ht"] = None
            st6, ag = scratch(24), scratch(8)
            for t in range(T):
                z_ = dve.do(lambda e, t=t, st6=st6: e.bn_stats(st6[:, 6 * t:6 * t + 6], HT[:, t, 0:256]), ht[t])
            for t in range(T):
                z_ = dve.do(lambda e, t=t, st6=st6, ag=ag: e.bn_aggr(ag[:, 2 * t:2 * t + 2], st6[:, 6 * t:6 * t + 6]), z_)
            agv = ag.rearrange("p (t two) -> p t two", two=2)
            den, r_, v_, w_, u_ = scratch(4), scratch(4), scratch(4), scratch(4), scratch(4)
            gcol = GD.rearrange("p (t h) -> p t h", h=4)[:, :, h]
            d1 = stt(den, HT[:, :, 256], -1.0, HT[:, :, 256], ALU.mult, ALU.max, [ht])
            d1 = tt(den, den, gcol, ALU.max, [d1, gd])
            d2 = recip(r_, den, d1)
            d3 = tt(v_, r_, r_, ALU.mult, d2)
            d4 = tt(w_, v_, agv[:, :, 1], ALU.mult, [d3, z_])
            rr, d5 = rsqrt_cols(w_, 4, 1.0, d4)
            d6 = tt(u_, r_, rr, ALU.mult, [d5, d2])
            for t in range(T):
                d7 = ts(HT[:, t, 0:256], HT[:, t, 0:256], agv[:, t, 0:1], u_[:, t:t + 1], ALU.subtract, ALU.mult,
                        after=[d6, z_])
            for d_ in range(2):
                b_, bk, free = mbank()
                for t in range(T):
                    tk_ = tr(bk[:, t * 128:(t + 1) * 128], HT[:, t, d_ * 128:(d_ + 1) * 128], IDENT, [d7, free],
                             mark=(t == 3))
                i_ = 2 * h + d_
                hm_tok[i_] = ac(HM[:, i_, :], bk[:], ACT.Copy, [tk_, f], scale=vec("ml_g", i_))
                mgive(b_, [hm_tok[i_]])
            held["ht"] = tk_

        waiting = None
        for h in range(4):
            held["qk"] = []
            for z_ in range(4):
                i = 2 * h + z_ % 2 + (8 if z_ >= 2 else 0)
                gemm(W_IN, 16 + i, 8, hi, lo, None, qk_tile(z_, QK[:, h % 2, z_, :], 0, i, qk_used[h % 2]))
                background(4)
            done = held["qk"]
            if waiting is not None:
                attend(*waiting)
            waiting = (h, list(done))

        z_tok = [None] * 8

        def gate_mul(bname, boff):
            def make(i):
                def evac(bank, t):
                    j, free = tmp.take()
                    a = ac(TMP[j][:], bank[:], ACT.Sigmoid, [t, free], bias=vec(bname, boff + i))
                    c = tt(HM[:, i, :], HM[:, i, :], TMP[j][:], ALU.mult, [a, hm_tok[i]])
                    hm_tok[i] = c
                    tmp.give(j, [c])
                    return [a]
                return evac
            return make

        mk = gate_mul("b_o", 0)
        gemm(W_IN, 32, 8, hi, lo, None, mk(0))
        background(6)
        gemm(W_IN, 33, 8, hi, lo, None, mk(1))
        attend(*waiting)
        for i in range(2, 8):
            gemm(W_IN, 32 + i, 8, hi, lo, None, mk(i))
            background(8)
        mk = gate_mul("b_mg", 8)
        for i in range(8):
            gemm(W_IN, 48 + i, 8, hi, lo, None, mk(i))
            background(8)
        background(1000)
        f = fence()
        gc_tok = [None] * 8

        j0, free = tmp.take()
        t = tt(TMP[j0][:], CO[:, 0, :], CO[:, 1, :], ALU.add, [conv_tok[0], conv_tok[1], free])
        for i in range(2, 8):
            t = tt(TMP[j0][:], TMP[j0][:], CO[:, i, :], ALU.add, [t, conv_tok[i]])
        for i in range(4):
            def evac(bank, t_, i=i):
                gc_tok[i] = ac(GC[:, i, :], bank[:], ACT.Sigmoid, [t_, f], bias=vec("b_mg", i))
                return [gc_tok[i]]
            gemm(W_IN, 40 + i, 8, hi, lo, None, evac)
            if i == 0:
                b, bank, free = mbank()
                mt = mm(bank[:], ONES[:], TMP[j0][:], True, True, [t, free], mark=True)
                i1, free1 = tmp.take()
                mean = ac(TMP[i1][:], bank[:], ACT.Copy, [mt, free1], scale=1.0 / D)
                mgive(b, [mean])
                tmp.give(j0, [mt])
                ss = SumSq()
                for z in range(8):
                    c = tt(CO[:, z, :], CO[:, z, :], TMP[i1][:], ALU.subtract, [mean])
                    conv_tok[z] = c
                    ss.add(CO[:, z, :], c)
                tmp.give(i1, [c])
        rows = None
        for i in range(4, 8):
            def evac(bank, t_, i=i):
                gc_tok[i] = ac(GC[:, i, :], bank[:], ACT.Sigmoid, [t_, f], bias=vec("b_mg", i))
                return [gc_tok[i]]
            gemm(W_IN, 40 + i, 8, hi, lo, None, evac)
            if i == 5:
                rows = ss.rows(D)
                b, bank, rt = rows
                a_tok = []
                for z in range(8):
                    c = tt(CO[:, z, :], CO[:, z, :], bank[:], ALU.mult, [rt, conv_tok[z]])
                    s_ = ac(CO[:, z, :], CO[:, z, :], ACT.Silu, c, bias=vec("ln_b", z), scale=vec("ln_g", z))
                    a_tok.append(cut(CO[:, z, :], AH[:, z, :], AL[:, z, :], [s_, f]))
                mgive(b, [c])
        f = fence()
        z_tok = []
        for i in range(8):
            def evac(bank, t_, i=i):
                j, free = tmp.take()
                a = stt(TMP[j][:], bank[:], vec("b_pw", i), GC[:, i, :], ALU.add, ALU.mult, [t_, gc_tok[i], free])
                c = tt(TMP[j][:], TMP[j][:], HM[:, i, :], ALU.add, [a, hm_tok[i]])
                z_ = cut(TMP[j][:], HH[:, i, :], HL[:, i, :], [c, f])
                tmp.give(j, z_)
                z_tok.append(z_)
                return [a]
            gemm("w_pw", i, 8, lambda k: AH[:, k, :], lambda k: AL[:, k, :], a_tok, evac)

        ss_ref = [None]
        x_tok = [xt] * 8

        def residual(col):
            def make(i):
                def evac(bank, t_):
                    x_tok[i] = stt(XT[:, i, :], bank[:], MOD[:, col + i:col + i + 1], XT[:, i, :], ALU.mult, ALU.add,
                                   [t_, x_tok[i], modb])
                    ss_ref[0].add(XT[:, i, :], x_tok[i])
                    return [x_tok[i]]
                return evac
            return make

        ss_ref[0] = SumSq()
        mk = residual(16)
        for i in range(8):
            gemm("w_out", i, 8, hi, lo, z_tok, mk(i))

        gffn = keepc(8)
        gf = stt(gffn, MOD[:, 32:40], 1.0, V_[:, VEC["g_ffn"]:VEC["g_ffn"] + 8], ALU.add, ALU.mult, [modb])

        def ffn_up(tiles, h_tok):
            f = fence()
            mid = []
            for i in range(NFT):
                pend = {}

                def keep(bank, t):
                    j, free = tmp.take()
                    pend["a"] = ac(TMP[j][:], bank[:], ACT.Silu, [t, free])
                    pend["j"] = j
                    return [pend["a"]]

                def evac(bank, t):
                    j = pend["j"]
                    c = tt(TMP[j][:], TMP[j][:], bank[:], ALU.mult, [t, pend["a"]])
                    z_ = cut(TMP[j][:], MH[:, i, :], ML[:, i, :], [c, f])
                    tmp.give(j, z_)
                    mid.append(z_)
                    return [c]

                gemm(*tiles(i, 0), 8, hi, lo, h_tok, keep)
                gemm(*tiles(i, 1), 8, hi, lo, h_tok, evac)
            return mid

        lo_engine[0] = dve
        rows = ss_ref[0].rows(D)
        f = fence()
        h_tok = normed(lambda i: XT[:, i, :], 8, lambda i: gffn[:, i:i + 1], rows, [x_tok, gf, f],
                       hi, lo, lambda i: MOD[:, 24 + i:25 + i])
        mid = ffn_up(lambda i, z: ("w_up1", i + z * NFT), h_tok)
        ss_ref[0] = SumSq()
        mk = residual(40)
        for i in range(8):
            gemm("w_down1", i, NFT, lambda k: MH[:, k, :], lambda k: ML[:, k, :], mid, mk(i))
        b, bank, rt = ss_ref[0].rows(D)
        ss = SumSq()
        for i in range(8):
            x_tok[i] = stt(XT[:, i, :], XT[:, i, :], vec("g_fin", i), bank[:], ALU.mult, ALU.mult, [x_tok[i], rt])
            ss.add(XT[:, i, :], x_tok[i])
        mgive(b, [x_tok[7]])

        f = fence()
        posi = at_pos = None
        rd_tok = once("l_rd", RD[:], A["ret_decay"], f)
        j, free = tmp.take()
        POSI = TMP[j][:].bitcast(I32)
        pt = once("l_pos", POSI, A["pos"].broadcast_to([128, S]), free)
        k, free2 = tmp.take()
        pf = cp(TMP[k][:], POSI, [pt, free2])
        trig = []
        i_, free3 = tmp.take()
        for z, (inv, sg) in enumerate((("invr", "sgr"), ("invm", "sgm"))):
            ang, kk = TRIG[:, 2 * z, :], TMP[i_][:]
            t = ts(ang, TMP[k][:], const(inv), None, ALU.mult, after=[pf, f, cst])
            u = free3
            for m in (2048.0, 1.0):
                u = ts(kk, ang, 1.0 / (m * 2 * np.pi), MAGIC, ALU.mult, ALU.add, [t, u])
                u = ts(kk, kk, MAGIC, None, ALU.subtract, after=u)
                for cc in (TWO_PI_1, TWO_PI_2, TWO_PI_3):
                    t = stt(ang, kk, -cc * m, ang, ALU.mult, ALU.add, [u, t])
                u = t
            sn = TRIG[:, 2 * z + 1, :]
            t = ts(ang, ang, float(np.float32(3.14159)), float(np.float32(-3.14159)), ALU.min, ALU.max, t)
            s_ = ac(sn, ang, ACT.Sin, [t, f])
            s_ = ac(sn, sn, ACT.Copy, s_, scale=const(sg))
            u = ts(ang, ang, float(np.pi / 2), None, ALU.add, after=[t, s_])
            t = ts(kk, ang, float(np.pi), -2 * float(np.pi), ALU.is_gt, ALU.mult, u)
            t = tt(ang, ang, kk, ALU.add, t)
            free3 = t
            t = ts(ang, ang, float(np.float32(3.14159)), float(np.float32(-3.14159)), ALU.min, ALU.max, t)
            trig += [s_, ac(ang, ang, ACT.Sin, t)]
        tmp.give(j, [pf])
        tmp.give(k, [free3])
        tmp.give(i_, [free3])
        COSR, SINR, COSM, SINM = (TRIG[:, z, :] for z in range(4))

        rows = ss.rows(D)
        h_tok = normed(lambda i: XT[:, i, :], 8, lambda i: vec("g_pre", i), rows, [x_tok], hi, lo)

        W2 = "w_in2"
        rv_tok, srg_tok, cq_tok, ckv_tok, rq_tok, rk_tok = [], [], [], [], [], []

        def evac_rv(t, bank, tok):
            rv_tok.append(ac(RV[:, t, :], bank[:], ACT.Copy, [tok, f]))
            return [rv_tok[-1]]
        gemm_tok("w_rv", 0, 8, hi, lo, h_tok, evac_rv)
        ssq, sskv = SumSq(), SumSq()
        for i in range(3):
            def evac(bank, t, i=i):
                a = cp(CQ[:, i, :], bank[:], [t, f])
                cq_tok.append(a)
                ssq.add(CQ[:, i, :], a)
                return [a]
            gemm(W2, 12 + i, 8, hi, lo, h_tok, evac)
        for i in range(2):
            def evac(bank, t, i=i):
                a = cp(CKV[:, i, :], bank[:], [t, f])
                ckv_tok.append(a)
                sskv.add(CKV[:, i, :], a)
                return [a]
            gemm(W2, 15 + i, 8, hi, lo, h_tok, evac)
        for i in range(4):
            def evac(bank, t, i=i):
                srg_tok.append(ac(SRG[:, i, :], bank[:], ACT.Silu, [t, f]))
                return [srg_tok[-1]]
            gemm(W2, 8 + i, 8, hi, lo, h_tok, evac)

        def rope_rows(dst, bank, after):
            j, free = tmp.take()
            k, free2 = tmp.take()
            a = tt(TMP[j][64:96, :], bank[64:96, :], COSM[64:96, :], ALU.mult, [after, trig, free])
            b = tt(TMP[k][64:96, :], bank[96:128, :], SINM[96:128, :], ALU.mult, [after, trig, free2])
            c = tt(dst, TMP[j][64:96, :], TMP[k][64:96, :], ALU.add, [a, b])
            tmp.give(j, [c])
            tmp.give(k, [c])
            return [a, b], c

        def evac_kr(bank, t):
            ab, held["kr"] = rope_rows(KR[64:96, :], bank, [t, f])
            return ab
        gemm("w_kr", 0, 8, hi, lo, h_tok, evac_kr)

        def rope_full(dst, toks):
            def evac(bank, t):
                j, free = tmp.take()
                k, free2 = tmp.take()
                a = tt(TMP[j][:], bank[:], COSR, ALU.mult, [t, trig, free])
                b0 = tt(TMP[k][0:64, :], bank[64:128, :], SINR[64:128, :], ALU.mult, [t, free2])
                b1 = tt(TMP[k][64:128, :], bank[0:64, :], SINR[0:64, :], ALU.mult, [t, free2])
                c = tt(dst, TMP[j][:], TMP[k][:], ALU.add, [a, b0, b1, f])
                tmp.give(j, [c])
                tmp.give(k, [c])
                toks.append(c)
                return [a, b0, b1]
            return evac
        for i in range(4):
            gemm(W2, i, 8, hi, lo, h_tok, rope_full(RQ[:, i, :], rq_tok))
            gemm(W2, 4 + i, 8, hi, lo, h_tok, rope_full(RK[:, i, :], rk_tok))
        cqs = normed(lambda i: CQ[:, i, :], 3, lambda i: vec("g_q", i), ssq.rows(384), [cq_tok, f],
                     lambda i: CQH[:, i, :], lambda i: CQL[:, i, :])
        ckvs = normed(lambda i: CKV[:, i, :], 2, lambda i: vec("g_kv", i), sskv.rows(256), [ckv_tok, f],
                      lambda i: KVH[:, i, :], lambda i: KVL[:, i, :])

        fm = fence()
        used = None
        ybanks = []
        ry_tok = []
        yb = [main.take() for _ in range(T)]
        stats, aggs = scratch(96), scratch(32)
        ytok = [None] * T
        for h in range(4):
            off, offs, sct = 0, {}, []
            for k in range(T):
                wdt = (T - k) * 128
                b_, bk, free = mbank()
                st = mm(bk[:, 0:wdt], RK[:, h, k * 128:(k + 1) * 128], RQ[:, h, k * 128:512], True, True,
                        [rq_tok, rk_tok, free], mark=True)
                x_ = tt(SC2[:, off:off + wdt], bk[:, 0:wdt], RD[:, h, 0:wdt], ALU.mult, [st, rd_tok, used, f])
                mgive(b_, [x_])
                offs[k] = off
                off += wdt
                sct.append(x_)
            for t in range(T):
                for k in range(t + 1):
                    c0 = offs[k] + (t - k) * 128
                    pt = mm(P_[yb[t][0]][:, h * 128:(h + 1) * 128], SC2[:, c0:c0 + 128],
                            RV[:, k, h * 128:(h + 1) * 128], k == 0, k == t, [sct, rv_tok, yb[t][1]], mark=(k == t))
                ytok[t] = pt
            used = pt
        for t in range(T):
            bk = P_[yb[t][0]]
            for h in range(4):
                n = 4 * t + h
                z_ = dve.do(lambda e, n=n, h=h, bk=bk: e.bn_stats(stats[:, 6 * n:6 * n + 6], bk[:, h * 128:(h + 1) * 128]),
                            ytok[t])
        for n in range(16):
            z_ = dve.do(lambda e, n=n: e.bn_aggr(aggs[:, 2 * n:2 * n + 2], stats[:, 6 * n:6 * n + 6]), z_)
        av = aggs.rearrange("p (n two) -> p n two", two=2)
        rr, d5 = rsqrt_cols(av[:, :, 1], 16, 1.0, z_)
        for t in range(T):
            for h in range(4):
                n = 4 * t + h
                d7 = ts(RY[:, t, h * 128:(h + 1) * 128], P_[yb[t][0]][:, h * 128:(h + 1) * 128], av[:, n, 0:1],
                        rr[:, n:n + 1], ALU.subtract, ALU.mult, after=[d5, f])
            main.give(yb[t][0], [d7])
        mix_tok = []
        for h in range(4):
            b_, bk, free = mbank()
            for t in range(T):
                tk_ = tr(bk[:, t * 128:(t + 1) * 128], RY[:, t, h * 128:(h + 1) * 128], IDENT, [d7, free], mark=(t == 3))
            j, freej = tmp.take()
            c = stt(TMP[j][:], bk[:], vec("ret_g", h), SRG[:, h, :], ALU.mult, ALU.mult, [tk_, srg_tok, freej])
            mgive(b_, [c])
            z_ = cut(TMP[j][:], HH[:, h, :], HL[:, h, :], [c, fm])
            tmp.give(j, z_)
            mix_tok.append(z_)

        f = fence()
        qh_tok, kh_tok, vm_tok = [], [], []
        cqh, cql = (lambda k: CQH[:, k, :]), (lambda k: CQL[:, k, :])
        kvh, kvl = (lambda k: KVH[:, k, :]), (lambda k: KVL[:, k, :])
        for i in range(4):
            def evac(bank, t, i=i):
                a = ac(KH[0:64, 2 * i, :], bank[0:64, :], ACT.Copy, [t, f])
                b = cp(KH[0:64, 2 * i + 1, :], bank[64:128, :], [t, f, a])
                kh_tok.extend([a, b])
                return [a, b]
            gemm("w_uk", i, 2, kvh, kvl, ckvs, evac)
        for h in range(8):
            kh_tok.append(ac(KH[64:96, h, :], KR[64:96, :], ACT.Copy, [held["kr"], f]))

        n, wh, wl, wt = W.take("w_uv", 0, 0, 1024)
        for t in range(T):
            b, free = main.take()
            q = slice(t * 128, (t + 1) * 128)
            for k in range(2):
                h_, l_ = wh[:, k * 512:(k + 1) * 512], wl[:, k * 512:(k + 1) * 512]
                mm(P_[b][:], kvh(k)[:, q], h_, k == 0, False, [wt, ckvs, free])
                mm(P_[b][:], kvh(k)[:, q], l_, False, False)
                tok = mm(P_[b][:], kvl(k)[:, q], h_, False, k == 1, mark=(k == 1))
            a = ac(VM[:, t, :], P_[b][:], ACT.Copy, [tok, f])
            vm_tok.append(a)
            main.give(b, [a])
        W.done(n, tok)
        for i in range(8):
            def evac(bank, t, i=i):
                a = ac(QH[0:64, i, :], bank[0:64, :], ACT.Copy, [t, f])
                ab, c = rope_rows(QH[64:96, i, :], bank, [t, f, a])
                qh_tok.append([a, c])
                return [a] + ab
            gemm("w_uq", i, 3, cqh, cql, cqs, evac)

        f2 = fence()
        ob = [main.take() for _ in range(T)]
        RSUM = keepc(32)
        scale = 1.0 / float(np.sqrt(96.0))
        used = [f2]
        otok = [None] * T
        for h in range(8):
            ptt = {}
            for t in range(T):
                wdt = (t + 1) * 128
                b_, bk, free = mbank()
                q = slice(t * 128, (t + 1) * 128)
                st = mm(bk[:, 0:wdt], QH[:, h, q], KH[:, h, 0:wdt], True, True, [qh_tok[h], kh_tok, free], mark=True)
                m0 = tt(bk[:, q], bk[:, q], MNEG, ALU.add, st)
                mx, nmx = scratch(1), scratch(1)
                m1 = dve.do(lambda e, mx=mx, bk=bk, wdt=wdt: e.tensor_reduce(mx, bk[:, 0:wdt], AX.X, ALU.max), m0)
                m2 = ts(nmx, mx, -scale, None, ALU.mult, after=m1)
                j, freej = tmp.take()
                e_ = ac(TMP[j][:, 0:wdt], bk[:, 0:wdt], ACT.Exp, [m2, freej], bias=nmx, scale=scale,
                        accum=RSUM[:, 8 * t + h:8 * t + h + 1])
                mgive(b_, [e_])
                b2, bk2, free = mbank()
                for k in range(t + 1):
                    tk_ = tr(bk2[:, k * 128:(k + 1) * 128], TMP[j][:, k * 128:(k + 1) * 128], IDENT, [e_, free],
                             mark=(k == t))
                tmp.give(j, [tk_])
                off = 64 * t * (t + 1)
                c = cp(SC2[:, off:off + wdt], bk2[:, 0:wdt], [tk_, used])
                mgive(b2, [c])
                for k in range(t + 1):
                    pt = mm(P_[ob[t][0]][:, h * 64:(h + 1) * 64], SC2[:, off + k * 128:off + (k + 1) * 128],
                            VM[:, k, h * 64:(h + 1) * 64], k == 0, k == t, [c, vm_tok, ob[t][1]], mark=(k == t))
                otok[t] = pt
            used = [pt]
        RI = keepc(32)
        rt = recip(RI, RSUM, [e_, act.last()])
        for t in range(T):
            rb = RI[:, 8 * t:8 * t + 8].unsqueeze(2).broadcast_to([128, 8, 64])
            c = tt(MO[:, t, :].rearrange("p (h d) -> p h d", h=8), P_[ob[t][0]][:].rearrange("p (h d) -> p h d", h=8),
                   rb, ALU.mult, [rt, otok[t], f])
            main.give(ob[t][0], [c])
        for i in range(4):
            b_, bk, free = mbank()
            for t in range(T):
                tk_ = tr(bk[:, t * 128:(t + 1) * 128], MO[:, t, i * 128:(i + 1) * 128], IDENT, [c, free], mark=(t == 3))
            j, freej = tmp.take()
            c2 = cp(TMP[j][:], bk[:], [tk_, freej])
            mgive(b_, [c2])
            z_ = cut(TMP[j][:], HH[:, 4 + i, :], HL[:, 4 + i, :], [c2, fm])
            tmp.give(j, z_)
            mix_tok.append(z_)

        def branch(dst, f):
            toks = []

            def make(i):
                def evac(bank, t):
                    a = cp(dst[:, i, :], bank[:], [t, f])
                    toks.append(a)
                    ss_ref[0].add(dst[:, i, :], a)
                    return [a]
                return evac
            return toks, make

        def join(src, toks, gname, ss_next):
            b, bank, rt = ss_ref[0].rows(D)
            for i in range(8):
                j, free = tmp.take()
                t = stt(TMP[j][:], src[:, i, :], vec(gname, i), bank[:], ALU.mult, ALU.mult, [rt, toks, free])
                x_tok[i] = tt(XT[:, i, :], XT[:, i, :], TMP[j][:], ALU.add, [t, x_tok[i]])
                tmp.give(j, [x_tok[i]])
                if ss_next is not None:
                    ss_next.add(XT[:, i, :], x_tok[i])
            mgive(b, [t])

        f = fence()
        ss_ref[0] = SumSq()
        toks, mk = branch(MIXO, f)
        for i in range(8):
            gemm("w_o", i, 8, hi, lo, mix_tok, mk(i))
        ss = SumSq()
        join(MIXO, toks, "g_post", ss)

        rows = ss.rows(D)
        f = fence()
        h_tok = normed(lambda i: XT[:, i, :], 8, lambda i: vec("g_pf", i), rows, [x_tok, f], hi, lo)
        mid = ffn_up(lambda i, z: (("w_gate", "w_up")[z], i), h_tok)
        f = fence()
        ss_ref[0] = SumSq()
        toks, mk = branch(FFO, f)
        for i in range(8):
            gemm("w_down", i, NFT, lambda k: MH[:, k, :], lambda k: ML[:, k, :], mid, mk(i))

        f = fence()
        pt = once("l_pt", PTS[:], A["pT"], f)
        ptok = []
        for i in range(2):
            ptok.append(cut(PTS[:, i, :], PTH[:, i, :], PTL[:, i, :], [pt, f]))
        sse = SumSq()
        e_tok = []
        for i in range(8):
            def evac(bank, t, i=i):
                a = cp(EE[:, i, :], bank[:], [t, f])
                e_tok.append(a)
                sse.add(EE[:, i, :], a)
                return [a]
            gemm("w_pp", i, 2, lambda k: PTH[:, k, :], lambda k: PTL[:, k, :], ptok, evac)
        join(FFO, toks, "g_pof", None)
        f = fence()
        x2 = []
        for i in range(8):
            x2.append(cut(XT[:, i, :], HH[:, i, :], HL[:, i, :], [x_tok[i], f]))
        b, bank, rt = sse.rows(D)
        for i in range(8):
            e_tok[i] = stt(EE[:, i, :], EE[:, i, :], vec("g_ple", i), bank[:], ALU.mult, ALU.mult, [rt, e_tok[i]])
        mgive(b, [e_tok[7]])
        for i in range(8):
            def evac(bank, t, i=i):
                j, free = tmp.take()
                a = ac(TMP[j][:], bank[:], ACT.Sigmoid, [t, free], bias=vec("b_pg", i))
                c = tt(TMP[j][:], TMP[j][:], EE[:, i, :], ALU.mult, [a, e_tok[i]])
                c = tt(XT[:, i, :], XT[:, i, :], TMP[j][:], ALU.add, [c, x_tok[i]])
                tmp.give(j, [c])
                loads.load(s_out, out[:, i, :], XT[:, i, :], c)
                return [a]
            gemm("w_pg", i, 8, hi, lo, x2, evac)
        sp.wait((s_out, loads.total[s_out]))

        seen = W.seen
        if not A["plan"]:
            return seen

        block = ctx.enter_context(nc.Block())

        @block.sync
        def _(e):
            for item in sp.items:
                item(e)

        @block.gpsimd
        def _(e):
            for item in pool.items:
                item(e)

        @block.scalar
        def _(e):
            for item in act.items:
                item(e)

        @block.vector
        def _(e):
            for item in dve.items:
                item(e)

        @block.tensor
        def _(e):
            for item in pe.items:
                item(e)
        return seen


def _tiles(w):
    k, n = w.shape
    return np.ascontiguousarray(w.reshape(k // 128, 128, n // 128, 128).transpose(2, 1, 0, 3)).reshape(
        n // 128, 128, k)


def _blocks(w, c):
    k, n = w.shape
    return np.ascontiguousarray(w.reshape(k // 128, 128, n // c, c).transpose(2, 1, 0, 3)).reshape(
        n // c, 128, k // 128 * c)


def _fold(v):
    return np.ascontiguousarray(np.asarray(v).reshape(-1, 128).T)


def layout(x):
    f = np.float32
    win, bin_ = x["w_in"][0], x["b_in"][0]
    o = {}
    o["xT"] = np.ascontiguousarray(x["x"][0].T.reshape(8, 128, S).transpose(1, 0, 2))
    o["pT"] = np.ascontiguousarray(x["p_2"][0, 0].T.reshape(2, 128, S).transpose(1, 0, 2))
    o["pos"] = np.ascontiguousarray(x["positions_2"].reshape(1, S))
    o["w_ada"] = _blocks(x["w_ada"][0], 256).reshape(24, 128, 8, 256)
    o["w_in"] = _tiles(np.concatenate([win[:, 0:4096], win[:, 5120:6144], win[:, 6152:8200]], axis=1))
    o["w_v"] = _blocks(win[:, 4096:5120], 512)
    pad = np.zeros((D, 28), f)
    o["w_if"] = _tiles(np.concatenate([win[:, 6144:6148], pad, win[:, 6148:6152], pad, pad, pad, np.zeros((D, 8), f)],
                                      axis=1))
    o["b_v"] = np.ascontiguousarray(bin_[4096:5120].reshape(1, 1024))
    o["w_pw"] = _tiles(x["w_conv_pw"][0])
    o["w_out"] = _tiles(x["w_out"][0])
    o["w_up1"] = _tiles(x["w_ffn_up"][0])
    o["w_down1"] = _tiles(x["w_ffn_down"][0])
    w2 = x["w_in_2"][0]
    o["w_in2"] = _tiles(np.concatenate([w2[:, 0:1024], w2[:, 1536:2688]], axis=1))
    o["w_rv"] = _blocks(w2[:, 1024:1536], 512)
    kr = w2[:, 2688:2720]
    o["w_kr"] = _tiles(np.concatenate([np.zeros((D, 64), f), kr, kr[:, 16:32], kr[:, 0:16]], axis=1))
    uq = x["w_uq_2"][0].reshape(384, 8, 96)
    o["w_uq"] = _tiles(np.concatenate([uq, uq[:, :, 80:96], uq[:, :, 64:80]], axis=2).reshape(384, 1024))
    ukv = x["w_ukv_2"][0].reshape(256, 8, 128)
    o["w_uk"] = _tiles(np.ascontiguousarray(ukv[:, :, 0:64]).reshape(256, 512))
    o["w_uv"] = _blocks(np.ascontiguousarray(ukv[:, :, 64:128]).reshape(256, 512), 512)
    o["w_o"] = _tiles(x["w_o_2"][0])
    o["w_gate"] = _tiles(x["w_gate_2"][0])
    o["w_up"] = _tiles(x["w_up_2"][0])
    o["w_down"] = _tiles(x["w_down_2"][0])
    o["w_pp"] = _tiles(x["w_ple_proj_2"][0])
    o["w_pg"] = _tiles(x["w_ple_gate_2"][0])

    bif = np.concatenate([bin_[6144:6148], np.zeros(28, f), bin_[6148:6152], np.zeros(92, f)])
    parts = {
        "c": x["c"][0], "b_ada": x["b_ada"][0], "g_mix": x["norm_mix_g"][0], "b_glu": bin_[0:2048],
        "b_qk": bin_[2048:4096], "b_o": bin_[5120:6144], "b_mg": bin_[6152:8200], "b_if": bif,
        "dw_b": x["conv_dw_b"][0], "ln_g": x["conv_ln_g"][0], "ln_b": x["conv_ln_b"][0], "b_pw": x["b_conv_pw"][0],
        "qk_b": x["qk_conv_b"][0], "ml_g": x["mlstm_norm_g"][0], "g_ffn": x["norm_ffn_g"][0],
        "g_fin": x["final_norm_g"], "g_pre": x["pre_mix_norm_2"][0], "ret_g": x["ret_gn_w_2"][0],
        "g_q": x["mla_q_norm_2"][0], "g_kv": x["mla_kv_norm_2"][0], "g_post": x["post_mix_norm_2"][0],
        "g_pf": x["pre_ffn_norm_2"][0], "g_pof": x["post_ffn_norm_2"][0], "g_ple": x["ple_norm_2"][0],
        "b_pg": x["b_ple_gate_2"][0],
    }
    cols = [_fold(parts[n]) for n in VEC if n in parts]
    cols.append(x["conv_dw_w"][0].reshape(31, 8, 128).transpose(2, 1, 0).reshape(128, 248))
    cols.append(x["qk_conv_w"][0].reshape(4, 16, 128).transpose(2, 1, 0).reshape(128, 64))
    o["vecs"] = np.ascontiguousarray(np.concatenate(cols, axis=1))

    p = np.arange(128)
    cst = np.zeros((128, NCONST), f)
    cst[:, 0:128] = np.eye(128, dtype=f)
    cst[:, 128:256] = np.where(p[:, None] > p[None, :], f(BIG), f(0))
    cst[:, 256:384] = np.where(p[None, :] > p[:, None], f(-BIG), f(0))

    def inv(half):
        return (f(1.0) / (f(10000.0) ** (np.arange(half, dtype=f) / f(half)))).astype(f)
    cst[:, 384] = inv(64)[p % 64]
    cst[:, 385] = inv(16)[p % 16]
    cst[:, 386] = np.where(p < 64, 1.0, -1.0)
    cst[:, 387] = np.where(p % 32 < 16, -1.0, 1.0)
    o["consts"] = cst
    sel = np.zeros((4, 4, 128), f)
    for h in range(4):
        sel[h, h, :] = 1.0
    o["sel"] = sel
    t = np.arange(S)
    diff = t[None, :] - p[:, None]
    lg = np.log(1.0 - 2.0 ** (-5.0 - np.arange(4)))
    rd = [np.where(diff >= 0, np.exp(np.maximum(diff, 0) * lg[h]), 0.0) * 128.0 ** -0.5 for h in range(4)]
    o["ret_decay"] = np.ascontiguousarray(np.stack(rd, axis=1).astype(f))
    return o


def declare(nc, arrays, plan):
    A = {n: nc.dram_tensor(f"in_{n}", a.shape, mybir.dt.from_np(a.dtype), kind="ExternalInput").ap()
         for n, a in arrays.items()}
    A["plan"] = plan
    out = nc.dram_tensor("out_0", (128, 8, S), F32, kind="ExternalOutput").ap()
    return program(nc, A, out)


def kernel(**inputs):
    import concourse.bacc as bacc
    from concourse.bass_utils import run_bass_kernel_spmd

    arrays = layout({n: np.asarray(a) for n, a in inputs.items()})
    plan = declare(bacc.Bacc("TRN2", target_bir_lowering=False, num_devices=1), arrays, [])
    nc = bacc.Bacc("TRN2", target_bir_lowering=False, num_devices=1)
    declare(nc, arrays, plan)
    r = run_bass_kernel_spmd(nc, [{f"in_{n}": a for n, a in arrays.items()}], core_ids=[0])
    got = r.results[0]["out_0"]
    return np.ascontiguousarray(got.transpose(1, 0, 2).reshape(D, S).T).reshape(1, S, D)
```

```python
from contextlib import ExitStack

import numpy as np

import concourse.bass as bass
from concourse import mybir

ALU = mybir.AluOpType
ACT = mybir.ActivationFunctionType
AX = mybir.AxisListType
F32 = mybir.dt.float32
F32R = mybir.dt.float32r
I32 = mybir.dt.int32

D, S, T = 1024, 512, 4
NF = 2816
NFT = NF // 128
EPS = 1e-6
BIG = 1e30
CHUNK = 8

VEC = {}
_at = 0
for _name, _n in [("c", 8), ("b_ada", 48), ("g_mix", 8), ("b_glu", 16), ("b_qk", 16), ("b_o", 8), ("b_mg", 16),
                  ("b_if", 1), ("dw_b", 8), ("ln_g", 8), ("ln_b", 8), ("b_pw", 8), ("qk_b", 16), ("ml_g", 8),
                  ("g_ffn", 8), ("g_fin", 8), ("g_pre", 8), ("ret_g", 4), ("g_q", 3), ("g_kv", 2), ("g_post", 8),
                  ("g_pf", 8), ("g_pof", 8), ("g_ple", 8), ("b_pg", 8), ("dw_w", 248), ("qk_w", 64)]:
    VEC[_name] = _at
    _at += _n
NVEC = _at
CONST = {"ident": 0, "mbig": 128, "mneg": 256, "invr": 384, "invm": 385, "sgr": 386, "sgm": 387}
NCONST = 388

TWO_PI_1 = 6.28125
TWO_PI_2 = float(np.float32(int((2 * np.pi - TWO_PI_1) * 2 ** 21) / 2 ** 21))
TWO_PI_3 = float(np.float32(2 * np.pi - TWO_PI_1 - TWO_PI_2))
MAGIC = 12582912.0
PI_IN = 3.14159250259


class Engine:

    def __init__(self, sem):
        self.sem, self.n, self.items, self.waited = sem, 0, [], {}

    def wait(self, after):
        if after is None:
            return
        if isinstance(after, list):
            for a in after:
                self.wait(a)
            return
        sem, value = after
        if self.waited.get(sem, 0) < value:
            self.waited[sem] = value
            self.items.append(lambda e: e.wait_ge(sem, value))

    def do(self, issue, after=None, mark=True):
        self.wait(after)
        if not mark:
            self.items.append(issue)
            return None
        self.n += 1
        sem = self.sem
        self.items.append(lambda e: issue(e).then_inc(sem, 1))
        return (sem, self.n)

    def last(self):
        return (self.sem, self.n)


class Queue:

    def __init__(self, engine):
        self.engine, self.total = engine, {}

    def load(self, sem, out, in_, after=None):
        self.engine.wait(after)
        self.total[sem] = self.total.get(sem, 0) + 16
        self.engine.items.append(lambda e: e.dma_start(out, in_).then_inc(sem, 16))
        return (sem, self.total[sem])


class Slots:

    def __init__(self, n):
        self.free = [(i, []) for i in range(n)]

    def take(self):
        return self.free.pop(0)

    def give(self, i, after):
        self.free.append((i, after))


def program(nc, A, out):
    ctx = ExitStack()
    with ctx:
        def sem(name):
            return ctx.enter_context(nc.semaphore(name))

        base = 16512

        def at(name, off, shape, dt=F32):
            return nc.alloc_sbuf_tensor_at(name, shape, dt, offset=base + off)

        P_ = [ctx.enter_context(nc.psum_tensor(f"bank{i}", [128, 512], F32)) for i in range(8)]
        o = 0
        XT = at("XT", o, [128, 8, S]); o += 16384
        HH = at("HH", o, [128, 8, S], F32R)
        FFO = at("FFO", o, [128, 8, S]); o += 16384
        HL = at("HL", o, [128, 8, S], F32R); o += 16384
        NRAW, NSPL = 4, 3
        RAW = [at(f"raw{i}", o + 4096 * i, [128, 1024]) for i in range(NRAW)]; o += 4096 * NRAW
        SPH = [at(f"sph{i}", o + 4096 * i, [128, 1024], F32R) for i in range(NSPL)]; o += 4096 * NSPL
        SPL = [at(f"spl{i}", o + 4096 * i, [128, 1024], F32R) for i in range(NSPL)]; o += 4096 * NSPL
        V_ = at("vecs", o, [128, NVEC]); o += (NVEC * 4 + 31) // 32 * 32
        C_ = at("consts", o, [128, NCONST]); o += (NCONST * 4 + 31) // 32 * 32
        ONES = at("ones", o, [128, 128]); o += 512
        SM = at("small", o, [128, 256]); o += 1024
        KEEP = at("kept", o, [128, 176]); o += 704
        MOD = at("mod", o, [128, 48]); o += 192
        XP = at("xpad", o, [128, 2, 516])
        TRIG = at("trig", o, [128, 4, S]); o += 4128
        HT = at("htok", o, [128, 4, 258]); o += 4128
        MROW = at("mrow", o, [4, S]); o += 2048
        NT = 6
        RROW = at("rrow", o, [128, S]); o += 2048
        TMP = [at(f"tmp{i}", o + 2048 * i, [128, S]) for i in range(NT)]; o += 2048 * NT
        B = o
        MH = at("midh", B, [128, NFT, S], F32R)
        ML = at("midl", B + NFT * 2048, [128, NFT, S], F32R)
        CP = at("convin", B, [128, 8, 542])
        GC = at("gconv", B, [128, 8, S])
        CO = at("convout", B + 17344, [128, 8, S])
        VT = at("vtok", B + 33728, [128, T, 4, 257])
        QK = at("qk", B + 50176, [128, 2, 4, S])
        HM = at("hm", B + 66560, [128, 8, S])
        SC = at("sc", B + 82944, [128, 1280])
        VB = at("vbias", B + 82944, [128, 1024])
        SEL = at("sel", B + 88064, [4, 4, 128])
        ADA = [at(f"ada{i}", B + 33728 + 8192 * i, [128, 8, 256]) for i in range(6)]
        ROWS = [at(f"row{i}", B + 50176 + 2048 * i, [4, S]) for i in range(4)]
        ROWC = at("rowc", B + 66560, [4, 10, 128])
        AH = at("ah", B + 33728, [128, 8, S], F32R)
        AL = at("al", B + 33728 + 16384, [128, 8, S], F32R)
        RQ = at("rq", B, [128, 4, S])
        RK = at("rk", B + 8192, [128, 4, S])
        RV = at("rv", B + 16384, [128, T, S])
        SRG = at("srg", B + 24576, [128, 4, S])
        RD = at("rd", B + 32768, [128, 4, S])
        RY = at("ry", B + 40960, [128, T, S])
        SC2 = [at("sc2", B + 49152, [128, 1280]), at("sc3", B + 54272, [128, 1280])]
        CQ = at("cq", B + 54272, [128, 3, S])
        CKV = at("ckv", B + 60416, [128, 2, S])
        KVH = at("kvh", B + 64512, [128, 2, S], F32R)
        KVL = at("kvl", B + 68608, [128, 2, S], F32R)
        KR = at("kr", B + 72704, [128, S])
        CQH = at("cqh", B + 74752, [128, 3, S], F32R)
        CQL = at("cql", B + 74752 + 6144, [128, 3, S], F32R)
        QH = at("qh", B, [96, 8, S])
        KH = at("kh", B + 16384, [96, 8, S])
        VM = at("vm", B + 32768, [128, T, S])
        MO = at("mo", B + 40960, [128, T, S])
        MIXO = at("mixo", B + 54272, [128, 8, S])
        PTS = at("pts", B, [128, 2, S])
        PTH = at("pth", B + 4096, [128, 2, S], F32R)
        PTL = at("ptl", B + 8192, [128, 2, S], F32R)
        EE = at("ee", B + 16384, [128, 8, S])
        assert base + B + 90112 <= 229368, base + B + 90112

        pe, act, dve, pool, sp = (Engine(sem(n)) for n in ("s_pe", "s_act", "s_dve", "s_pool", "s_sp"))
        loads = Queue(sp)
        s_raw = [sem(f"s_raw{i}") for i in range(NRAW)]
        s_ada = [sem(f"s_ada{i}") for i in range(6)]
        s_out = sem("s_out")

        def once(name, out_, in_, after=None):
            return loads.load(sem(name), out_, in_, after)

        def mm(out_, l, r, start, stop, after=None, mark=False):
            return pe.do(lambda e: e.matmul(out_, l, r, start=start, stop=stop), after, mark)

        def tr(out_, in_, ident, after=None, mark=False):
            return pe.do(lambda e: e.transpose(out_, in_, ident), after, mark)

        def ac(out_, in_, f, after=None, bias=0.0, scale=1.0, accum=None):
            if accum is not None:
                return act.do(lambda e: e.activation(out_, in_, f, bias=bias, scale=scale, accum_out=accum), after)
            return act.do(lambda e: e.activation(out_, in_, f, bias=bias, scale=scale), after)

        def tt(out_, a, b, op, after=None, eng=None):
            return (eng or dve).do(lambda e: e.tensor_tensor(out_, a, b, op), after)

        def ts(out_, a, s1, s2, op0, op1=None, after=None, eng=None):
            if op1 is None:
                return (eng or dve).do(lambda e: e.tensor_scalar(out_, a, s1, None, op0), after)
            return (eng or dve).do(lambda e: e.tensor_scalar(out_, a, s1, s2, op0, op1), after)

        def stt(out_, a, s1, b, op0, op1, after=None):
            return dve.do(lambda e: e.scalar_tensor_tensor(out_, a, s1, b, op0, op1), after)

        def cp(out_, a, after=None, eng=None):
            return (eng or dve).do(lambda e: e.tensor_copy(out_, a), after)

        def setv(out_, v, after=None, eng=None):
            return (eng or pool).do(lambda e: e.memset(out_, v), after)

        def recip(out_, a, after=None):
            return dve.do(lambda e: e.reciprocal(out_, a), after)

        def always(tok):
            return lambda k: tok

        def by_tile(toks):
            return lambda k: toks[k]

        done_already = always([None, None])

        def bstat(out_, a, after=None):
            return dve.do(lambda e: e.bn_stats(out_, a), after)

        def baggr(out_, a, after=None):
            return dve.do(lambda e: e.bn_aggr(out_, a), after)

        def rmax(out_, a, after=None):
            return dve.do(lambda e: e.tensor_reduce(out_, a, AX.X, ALU.max), after)

        def scan(out_, a, b, first, op0, op1, after=None):
            return dve.do(lambda e: e.tensor_tensor_scan(out_, a, b, first, op0, op1), after)

        def vec(name, i, p=slice(0, 128)):
            return V_[p, VEC[name] + i:VEC[name] + i + 1]

        def const(name, p=slice(0, 128)):
            return C_[p, CONST[name]:CONST[name] + 1]

        IDENT = C_[:, 0:128]
        MBIG = C_[:, 128:256]
        MNEG = C_[:, 256:384]

        main, misc, tmp = Slots(4), Slots(4), Slots(NT)

        def mbank():
            i, t = misc.take()
            return 4 + i, P_[4 + i], t

        def mgive(i, t):
            misc.give(i - 4, t)

        def fence():
            return [pe.last(), act.last(), dve.last(), pool.last()]

        class Weights:
            def __init__(self, plan):
                self.plan, self.seen = plan, []
                self.raw_after = [None] * NRAW
                self.spl_after = [None] * NSPL
                self.loaded = self.cut = self.used = 0
                self.raw_tok, self.spl_tok = {}, {}

            def load(self):
                n = self.loaded
                if n >= len(self.plan):
                    return
                name, tile, first, size = self.plan[n]
                src = A[name][tile, :, first:first + size]
                self.raw_tok[n] = loads.load(s_raw[n % NRAW], RAW[n % NRAW][:, 0:size], src, self.raw_after[n % NRAW])
                self.loaded += 1

            def start(self):
                for _ in range(NRAW):
                    self.load()

            def split(self):
                n = self.cut
                size = self.plan[n][3]
                raw, hi, lo = RAW[n % NRAW][:, 0:size], SPH[n % NSPL][:, 0:size], SPL[n % NSPL][:, 0:size]
                a = ac(hi, raw, ACT.Copy, [self.raw_tok[n], self.spl_after[n % NSPL]])
                b = tt(lo, raw, hi.bitcast(F32), ALU.subtract, [a, self.raw_tok[n], self.spl_after[n % NSPL]],
                       eng=lo_engine[0])
                self.raw_after[n % NRAW] = [a, b]
                self.spl_tok[n] = [a, b]
                self.cut += 1
                self.load()

            def take(self, name, tile, first, size):
                self.seen.append((name, tile, first, size))
                n = self.used
                self.used += 1
                if not self.plan:
                    return n, SPH[n % NSPL][:, 0:size], SPL[n % NSPL][:, 0:size], None
                while self.cut < min(n + NSPL, len(self.plan)):
                    self.split()
                return n, SPH[n % NSPL][:, 0:size], SPL[n % NSPL][:, 0:size], self.spl_tok[n]

            def done(self, n, tok):
                self.spl_after[n % NSPL] = tok

        lo_engine = [pool]
        held = {}
        W = Weights(A["plan"])

        side, conv_ops, rate = [], [], [0, 0]

        def step(n=1):
            for _ in range(n):
                while side:
                    if next(side[0], True):
                        side.pop(0)
                        continue
                    break

        def flush():
            while side:
                step()

        def between():
            step(rate[0])
            background(rate[1])

        def gemm(src, tile_no, kt, hi, lo, after, evac):
            b, free = main.take()
            k0 = 0
            while k0 < kt:
                kn = min(CHUNK, kt - k0)
                n, wh, wl, wt = W.take(src, tile_no, k0 * 128, kn * 128)
                for k in range(kn):
                    q, kk = slice(k * 128, (k + 1) * 128), k0 + k
                    mm(P_[b][:], wh[:, q], hi(kk), kk == 0, False, [wt, free, after(kk)[0]])
                    mm(P_[b][:], wl[:, q], hi(kk), False, False)
                for k in range(kn):
                    q, kk = slice(k * 128, (k + 1) * 128), k0 + k
                    t = mm(P_[b][:], wh[:, q], lo(kk), False, kk == kt - 1, [after(kk)[1]], mark=(k == kn - 1))
                W.done(n, t)
                k0 += kn
                if k0 < kt:
                    between()
            held["bank"] = b
            freed = evac(P_[b], t)
            if freed is not None:
                main.give(b, freed)
            between()

        def gemm_tok(src, block, kt, hi, lo, after, evac):
            banks = [main.take() for _ in range(T)]
            for k0 in range(0, kt, 2):
                n, wh, wl, wt = W.take(src, block, k0 * 512, 1024)
                for k in range(2):
                    kk = k0 + k
                    h, l = wh[:, k * 512:(k + 1) * 512], wl[:, k * 512:(k + 1) * 512]
                    for t in range(T):
                        b, free = banks[t]
                        q = slice(t * 128, (t + 1) * 128)
                        mm(P_[b][:], hi(kk)[:, q], h, kk == 0, False, [wt, after(kk), free])
                        mm(P_[b][:], hi(kk)[:, q], l, False, False)
                        tok = mm(P_[b][:], lo(kk)[:, q], h, False, kk == kt - 1, mark=True)
                W.done(n, tok)
                if k0 + 2 < kt:
                    between()
            for t in range(T):
                main.give(banks[t][0], evac(t, P_[banks[t][0]], tok))
            between()

        small = [0]

        def scratch(n):
            if small[0] + n > 256:
                small[0] = 0
            a = small[0]
            small[0] += n
            return SM[:, a:a + n]

        kept = [0]

        def keepc(n):
            kept[0] += n
            assert kept[0] <= 176
            return KEEP[:, kept[0] - n:kept[0]]

        def rsqrt_cols(src, n, scale, after):
            v, q, r = scratch(n), scratch(n), scratch(n)
            t = ts(v, src, scale, EPS, ALU.mult, ALU.add, after)
            t = ac(q, v, ACT.Sqrt, t)
            return r, recip(r, q, t)

        class SumSq:

            def __init__(self):
                (self.a, self.free), self.t = tmp.take(), None

            def add(self, x, after, scale=1.0, eng=None):
                if self.t is None:
                    self.t = r = ac(TMP[self.a][:], x, ACT.Square, [after, self.free], scale=scale)
                else:
                    i, free = tmp.take()
                    r = ac(TMP[i][:], x, ACT.Square, [after, free], scale=scale)
                    self.t = tt(TMP[self.a][:], TMP[self.a][:], TMP[i][:], ALU.add, [r, self.t], eng=eng)
                    tmp.give(i, [self.t])
                return r

            def columns(self):
                b, bank, free = mbank()
                for t in range(T):
                    tok = mm(bank[:, t:t + 1], TMP[self.a][:, t * 128:(t + 1) * 128], ONES[:, 0:1], True, True,
                             [self.t, free, ones], mark=(t == T - 1))
                tmp.give(self.a, [tok])
                return bank[:, 0:T], tok, b

        def spread(r, after):
            i, free = tmp.take()
            b, bank, bfree = mbank()
            for t in range(T):
                q = slice(t * 128, (t + 1) * 128)
                d = ts(TMP[i][:, q], IDENT, r[:, t:t + 1], None, ALU.mult, after=[after, free, cst])
                tok = mm(bank[:, q], ONES[:], TMP[i][:, q], True, True, [d, bfree], mark=(t == T - 1))
            tmp.give(i, [tok])
            return b, bank, tok

        def rows_of(ss, width):
            c, t, b = ss.columns()
            r, t = rsqrt_cols(c, T, 1.0 / width, t)
            mgive(b, [t])
            return spread(r, t)

        def cut(x, hi, lo, after, shift=None, scale=None, eng=None):
            if shift is not None:
                a = ac(hi, x, ACT.Identity, after, bias=shift)
                return [a, stt(lo, x, shift, hi.bitcast(F32), ALU.add, ALU.subtract, [a, after])]
            if scale is not None:
                a = ac(hi, x, ACT.Copy, after, scale=scale)
                return [a, stt(lo, x, scale, hi.bitcast(F32), ALU.mult, ALU.subtract, [a, after])]
            a = ac(hi, x, ACT.Copy, after)
            return [a, tt(lo, x, hi.bitcast(F32), ALU.subtract, [a, after], eng=eng)]

        def in_turn(n, first, second):
            for i in range(n + 1):
                if i < n:
                    first(i)
                if i:
                    second(i - 1)

        def normed(x, n, scale, rows, after, hi, lo, shift=None):
            b, bank, rt = rows
            out_ = [[None, None] for _ in range(n)]
            js = [None] * n
            last = [None]

            def first(i):
                js[i], free = tmp.take()
                y = TMP[js[i]][:]
                t = last[0] = stt(y, x(i), scale(i), bank[:], ALU.mult, ALU.mult, [rt, after, free])
                if shift is None:
                    out_[i][0] = ac(hi(i), y, ACT.Copy, [t, after])
                    return
                out_[i][0] = ac(hi(i), y, ACT.Identity, [t, after], bias=shift(i))
                if i % 2:
                    out_[i][1] = ac(y, y, ACT.Identity, [t], bias=shift(i))

            def second(i):
                y, (a, full) = TMP[js[i]][:], out_[i]
                h = hi(i).bitcast(F32)
                if i % 2:
                    out_[i][1] = tt(lo(i), y, h, ALU.subtract, [a, full, last[0], after], eng=pool)
                elif shift is None:
                    out_[i][1] = tt(lo(i), y, h, ALU.subtract, [a, after])
                else:
                    out_[i][1] = stt(lo(i), y, shift(i), h, ALU.add, ALU.subtract, [a, after])
                tmp.give(js[i], out_[i])

            in_turn(n, first, second)
            mgive(b, [last[0]])
            return out_

        cst = once("l_c", C_[:], A["consts"])
        vecs = once("l_v", V_[:], A["vecs"])
        xt = once("l_x", XT[:], A["xT"])
        ada_src = A["w_ada"]
        ada_tok = [loads.load(s_ada[i], ADA[i][:], ada_src[i]) for i in range(6)]
        ones = setv(ONES[:], 1.0)
        zpad = [setv(CP[:, :, 0:30], 0.0), setv(XP[:, :, 0:3], 0.0)]

        csil = keepc(8)
        cs = ac(csil, V_[:, VEC["c"]:VEC["c"] + 8], ACT.Silu, vecs)
        ss = SumSq()
        for i in range(8):
            ss.add(XT[:, i, :], xt)
        rows = rows_of(ss, D)

        mod_a, mod_b = mbank(), mbank()
        ada_held = {}

        def ada(chunks):
            accs, toks_ = [], []
            for ch in chunks:
                i, free = tmp.take()
                accs.append((i, TMP[i][:, 0:256]))
                toks_.append([cs, ada_tok[ch], free])
            for k in range(8):
                for z, ch in enumerate(chunks):
                    acc, wt = accs[z][1], ADA[ch % 6]
                    if k == 0:
                        toks_[z] = ts(acc, wt[:, 0, :], csil[:, 0:1], None, ALU.mult, after=toks_[z])
                    else:
                        toks_[z] = stt(acc, wt[:, k, :], csil[:, k:k + 1], acc, ALU.mult, ALU.add, toks_[z])
            for z, ch in enumerate(chunks):
                if ch + 6 < 24:
                    ada_tok.append(loads.load(s_ada[ch % 6], ADA[ch % 6][:], ada_src[ch + 6], toks_[z]))
                ada_held[ch] = (accs[z][0], accs[z][1], toks_[z])

        def ada_columns(ch):
            i, acc, t = ada_held.pop(ch)
            _, bank, bfree = mod_a if ch < 8 else mod_b
            for j in range(2):
                c = 2 * ch + j - (0 if ch < 8 else 16)
                m = mm(bank[:, c:c + 1], acc[:, j * 128:(j + 1) * 128], ONES[:, 0:1], True, True,
                       [t, ones, bfree], mark=(j == 1))
            tmp.give(i, [m])
            return m

        for ch in range(0, 8, 2):
            ada([ch, ch + 1])
            if ch == 0 and A["plan"]:
                W.start()
            m = [ada_columns(ch), ada_columns(ch + 1)]
        moda = tt(MOD[:, 0:16], mod_a[1][:, 0:16], V_[:, VEC["b_ada"]:VEC["b_ada"] + 16], ALU.add, [m, vecs])
        mgive(mod_a[0], [moda])
        gmix = keepc(8)
        gm = stt(gmix, MOD[:, 8:16], 1.0, V_[:, VEC["g_mix"]:VEC["g_mix"] + 8], ALU.add, ALU.mult, [moda])
        h_tok = normed(lambda i: XT[:, i, :], 8, lambda i: gmix[:, i:i + 1], rows, [gm, moda],
                       lambda i: HH[:, i, :], lambda i: HL[:, i, :], lambda i: MOD[:, i:i + 1])
        hi, lo = (lambda k: HH[:, k, :]), (lambda k: HL[:, k, :])

        conv_ready = {}
        conv_tok = [None] * 8

        def tap(i, j):
            src = CP[:, i, j:j + 512]
            w = V_[:, VEC["dw_w"] + i * 31 + j:VEC["dw_w"] + i * 31 + j + 1]
            if j == 0:
                conv_tok[i] = ts(CO[:, i, :], src, w, vec("dw_b", i), ALU.mult, ALU.add, [conv_ready[i], zpad[0]])
            else:
                conv_tok[i] = stt(CO[:, i, :], src, w, CO[:, i, :], ALU.mult, ALU.add, conv_tok[i])

        def background(n):
            for _ in range(min(n, len(conv_ops))):
                tap(*conv_ops.pop(0))

        W_IN = "w_in"
        for i in range(8):
            pending = {}

            def keep(bank, t):
                pending["v"] = (held["bank"], t)
                return None

            def evac(bank, t):
                j, free = tmp.take()
                a = ac(TMP[j][:], bank[:], ACT.Sigmoid, [t, free, vecs], bias=vec("b_glu", 8 + i))
                v, vt = pending["v"]
                c = stt(CP[:, i, 30:542], P_[v][:], vec("b_glu", i), TMP[j][:], ALU.add, ALU.mult, [a, vt])
                tmp.give(j, [c])
                main.give(v, [c])
                conv_ready[i] = c
                return [a]

            gemm(W_IN, i, 8, hi, lo, by_tile(h_tok), keep)
            gemm(W_IN, 8 + i, 8, hi, lo, by_tile(h_tok), evac)
            if i % 2:
                conv_ops += [(i - 1 + z, j) for j in range(31) for z in range(2)]
            for ch in (6 + 2 * i, 7 + 2 * i):
                if ch >= 8:
                    ada_columns(ch)
            ada([8 + 2 * i, 9 + 2 * i])
            background(4)

        modb = []

        def last_columns():
            yield
            m = [ada_columns(22), ada_columns(23)]
            modb.append(tt(MOD[:, 16:48], mod_b[1][:, 0:32], V_[:, VEC["b_ada"] + 16:VEC["b_ada"] + 48], ALU.add,
                           [m, vecs]))
            mgive(mod_b[0], [modb[0]])

        side.append(last_columns())
        rate[:] = [1, 7]
        f = fence()
        vb_tok = once("l_vb", VB[:], A["b_v"].broadcast_to([128, 1024]), f)
        sel_tok = once("l_sel", SEL[:], A["sel"], f)
        von = setv(VT[:, :, :, 256:257], 1.0, f)
        v_tok = []
        for blk in range(2):
            def evac(t, bank, tok):
                dst = VT[:, t, 2 * blk:2 * blk + 2, 0:256]
                c = tt(dst, bank[:].rearrange("p (a b) -> p a b", a=2),
                       VB[:, blk * 512:(blk + 1) * 512].rearrange("p (a b) -> p a b", a=2), ALU.add,
                       [tok, vb_tok, f])
                v_tok.append(c)
                return [c]
            gemm_tok("w_v", blk, 8, hi, lo, done_already, evac)
        IR, LF, BR, CR = ROWS

        def gates(bank, t):
            p = slice(32, 36)
            j, free = tmp.take()
            z = TMP[j]
            a0 = ac(IR[:], bank[0:4, :], ACT.Identity, [t, f], bias=vec("b_if", 0, slice(0, 4)))
            a1 = ac(z[p, :], bank[p, :], ACT.Identity, [free], bias=vec("b_if", 0, p))
            k, free2 = tmp.take()
            y = TMP[k]
            a2 = ac(y[p, :], z[p, :], ACT.Abs, [a1, free2])
            a3 = ac(y[p, :], y[p, :], ACT.Exp, a2, scale=-1.0)
            a4 = ac(y[p, :], y[p, :], ACT.Ln, a3, bias=1.0)
            c = stt(LF[:], z[p, :], 0.0, y[p, :], ALU.min, ALU.subtract, [a4, a1, f])
            tmp.give(j, [c])
            tmp.give(k, [c])
            held["g"] = [a0, c]
            return [a0, a1]

        gemm("w_if", 0, 8, hi, lo, done_already, gates)
        CB, GD, mus, pair = keepc(40), keepc(16), keepc(8), {}

        def decays():
            g = held["g"]
            k1, freek = tmp.take()
            onerow = TMP[k1][0:4, 0:128]
            t1 = setv(onerow, 1.0, freek)
            mu0 = setv(mus[0:4, 0:1], 0.0, fence())
            ct = [g, t1, mu0]
            for t in range(T):
                q = slice(t * 128, (t + 1) * 128)
                e = slice((t + 1) * 128 - 1, (t + 1) * 128)
                b_ = scan(BR[:, q], onerow, LF[:, q], 0.0, ALU.mult, ALU.add, ct)
                c_ = tt(CR[:, q], IR[:, q], BR[:, q], ALU.subtract, [b_, g])
                m_ = scan(MROW[:, q], CR[:, q], CR[:, q], mus[0:4, t:t + 1], ALU.max, ALU.max, [c_, mu0])
                ct = [tt(mus[0:4, t + 1:t + 2], MROW[:, e], BR[:, e], ALU.add, [m_, b_])]
            tmp.give(k1, [ct[0]])
            n = 0
            for k in range(T):
                kq = slice(k * 128, (k + 1) * 128)
                for t in range(k, T):
                    pair[(k, t)] = n
                    if t == k:
                        z = cp(ROWC[:, n, :], CR[:, kq], ct)
                    else:
                        z = ts(ROWC[:, n, :], ROWC[:, n - 1, :], BR[:, t * 128 - 1:t * 128], None, ALU.add, after=z)
                    n += 1
            mr = tt(IR[:], MROW[:], BR[:], ALU.add, [z])
            yield
            yield
            b, bank, free = mbank()
            for i in range(10):
                tk = tr(bank[:, 4 * i:4 * i + 4], ROWC[:, i, :], IDENT[0:4, 0:4], [z, free, cst])
            for t in range(T):
                tk = tr(bank[:, 40 + 4 * t:44 + 4 * t], IR[:, t * 128:(t + 1) * 128], IDENT[0:4, 0:4], [mr], mark=(t == 3))
            cb = cp(CB, bank[:, 0:40], tk)
            gd = ac(GD, bank[:, 40:56], ACT.Exp, [tk, cb], scale=-1.0)
            mgive(b, [cb, gd])
            held.update(ct=ct, cb=cb, gd=gd, rows=tk)

        side.append(decays())

        f = fence()
        hm_tok = [None] * 8
        xp_free = [zpad[1], zpad[1]]
        qk_w = 0

        def qk_tile(tile_no, dst, w_at, b_at, after):
            def evac(bank, t):
                s = (tile_no) % 2
                a = ac(XP[:, s, 3:515], bank[:], ACT.Identity, [t, xp_free[s]], bias=vec("b_qk", b_at))
                j, free = tmp.take()
                w = lambda tap_: V_[:, VEC["qk_w"] + 4 * b_at + tap_:VEC["qk_w"] + 4 * b_at + tap_ + 1]
                c = ts(TMP[j][:], XP[:, s, 0:512], w(0), vec("qk_b", b_at), ALU.mult, ALU.add, [a, free])
                for z_ in range(1, 4):
                    c = stt(TMP[j][:], XP[:, s, z_:z_ + 512], w(z_), TMP[j][:], ALU.mult, ALU.add, c)
                xp_free[s] = c
                r = ac(dst, TMP[j][:], ACT.Silu, [c, after])
                tmp.give(j, [r])
                held["qk"].append(r)
                return [a]
            return evac

        qk_used = [f, f]
        sc_used = [f]

        def attend(h, qk_done):
            s = (h + 1) % 2
            ct, cb, gd = held["ct"], held["cb"], held["gd"]
            ht_used = held.get("ht")
            mb, mbk, free = mbank()
            mt = mm(mbk[:], SEL[:, h, :], MROW[:], True, True, [ct, sel_tok, free], mark=True)
            jm, freem = tmp.take()
            mrows = TMP[jm]
            mt = ac(mrows[:], mbk[:], ACT.Copy, [mt, freem])
            mgive(mb, [mt])
            off = 0
            sct = []
            offs = {}
            for k in range(T):
                wdt = (T - k) * 128
                b_, bk, free = mbank()
                for d_ in range(2):
                    st = mm(bk[:, 0:wdt], QK[:, s, 2 + d_, k * 128:(k + 1) * 128], QK[:, s, d_, k * 128:512],
                            d_ == 0, d_ == 1, [qk_done, free], mark=(d_ == 1))
                j, freej = tmp.take()
                dm = TMP[j]
                a0 = tt(dm[:, 0:128], mrows[:, k * 128:(k + 1) * 128], MBIG, ALU.add, [mt, freej, cst])
                last = []
                for t in range(k, T):
                    col = CB[:, 4 * pair[(k, t)] + h:4 * pair[(k, t)] + h + 1]
                    src = dm[:, 0:128] if t == k else mrows[:, t * 128:(t + 1) * 128]
                    e_ = ac(dm[:, (t - k) * 128:(t - k + 1) * 128], src, ACT.Exp, [a0, mt, cb, freej], bias=col, scale=-1.0)
                x_ = stt(SC[:, off:off + wdt], bk[:, 0:wdt], 0.0625, dm[:, 0:wdt], ALU.mult, ALU.mult,
                         [st, e_, sc_used[0]])
                tmp.give(j, [x_])
                mgive(b_, [x_])
                offs[k] = off
                off += wdt
                sct.append(x_)
                if k in (0, 2):
                    yield
            tmp.give(jm, [e_, a0])
            qk_used[s] = [st]
            ht = []
            stats = []
            for t in range(T):
                b_, bk, free = mbank()
                for k in range(t + 1):
                    c0 = offs[k] + (t - k) * 128
                    pt = mm(bk[:, 0:257], SC[:, c0:c0 + 128], VT[:, k, h, :], k == 0, k == t,
                            [sct[k], v_tok, von, free], mark=(k == t))
                a_ = ac(HT[:, t, 0:257], bk[:, 0:257], ACT.Copy, [pt, ht_used])
                mgive(b_, [a_])
                ht.append(a_)
                if t == 0:
                    yield
            sc_used[0] = pt
            st6, ag = scratch(24), scratch(8)
            for t in range(T):
                z_ = bstat(st6[:, 6 * t:6 * t + 6], HT[:, t, 0:256], ht[t])
            for t in range(T):
                z_ = baggr(ag[:, 2 * t:2 * t + 2], st6[:, 6 * t:6 * t + 6], z_)
            agv = ag.rearrange("p (t two) -> p t two", two=2)
            den, r_, v_, w_, u_ = scratch(4), scratch(4), scratch(4), scratch(4), scratch(4)
            gcol = GD.rearrange("p (t h) -> p t h", h=4)[:, :, h]
            d1 = stt(den, HT[:, :, 256], -1.0, HT[:, :, 256], ALU.mult, ALU.max, [ht])
            d1 = tt(den, den, gcol, ALU.max, [d1, gd])
            d2 = recip(r_, den, d1)
            d3 = tt(v_, r_, r_, ALU.mult, d2)
            d4 = tt(w_, v_, agv[:, :, 1], ALU.mult, [d3, z_])
            rr, d5 = rsqrt_cols(w_, 4, 1.0, d4)
            d6 = tt(u_, r_, rr, ALU.mult, [d5, d2])
            for t in range(T):
                d7 = ts(HT[:, t, 0:256], HT[:, t, 0:256], agv[:, t, 0:1], u_[:, t:t + 1], ALU.subtract, ALU.mult,
                        after=[d6, z_])
            yield
            yield
            yield
            for d_ in range(2):
                b_, bk, free = mbank()
                for t in range(T):
                    tk_ = tr(bk[:, t * 128:(t + 1) * 128], HT[:, t, d_ * 128:(d_ + 1) * 128], IDENT, [d7, free],
                             mark=(t == 3))
                i_ = 2 * h + d_
                hm_tok[i_] = ac(HM[:, i_, :], bk[:], ACT.Copy, [tk_, f], scale=vec("ml_g", i_))
                mgive(b_, [hm_tok[i_]])
                held["ht"] = tk_

        rate[:] = [2, 4]
        for h in range(4):
            held["qk"] = []
            if h >= 2:
                flush()
            for z_ in range(4):
                i = 2 * h + z_ % 2 + (8 if z_ >= 2 else 0)
                used_ = [qk_used[(h + 1) % 2], held.get("rows") if h == 1 else None]
                gemm(W_IN, 16 + i, 8, hi, lo, done_already, qk_tile(z_, QK[:, (h + 1) % 2, z_, :], 0, i, used_))
            side.append(attend(h, list(held["qk"])))

        z_tok = [None] * 8

        def gate_mul(bname, boff):
            def make(i):
                def evac(bank, t):
                    j, free = tmp.take()
                    a = ac(TMP[j][:], bank[:], ACT.Sigmoid, [t, free], bias=vec(bname, boff + i))
                    c = tt(HM[:, i, :], HM[:, i, :], TMP[j][:], ALU.mult, [a, hm_tok[i]])
                    hm_tok[i] = c
                    tmp.give(j, [c])
                    return [a]
                return evac
            return make

        mk = gate_mul("b_o", 0)
        rate[:] = [2, 8]
        for i in range(8):
            if i == 6:
                flush()
            gemm(W_IN, 32 + i, 8, hi, lo, done_already, mk(i))
        rate[1] = 8
        mk = gate_mul("b_mg", 8)
        for i in range(8):
            gemm(W_IN, 48 + i, 8, hi, lo, done_already, mk(i))
        background(1000)
        f = fence()
        gc_tok = [None] * 8

        j0, free = tmp.take()
        t = tt(TMP[j0][:], CO[:, 0, :], CO[:, 1, :], ALU.add, [conv_tok[0], conv_tok[1], free])
        for i in range(2, 8):
            t = tt(TMP[j0][:], TMP[j0][:], CO[:, i, :], ALU.add, [t, conv_tok[i]])
        def gc_evac(i):
            def evac(bank, t_):
                gc_tok[i] = ac(GC[:, i, :], bank[:], ACT.Sigmoid, [t_, f], bias=vec("b_mg", i))
                return [gc_tok[i]]
            return evac

        def layer_norm(t):
            yield
            b, bank, free = mbank()
            mt = mm(bank[:], ONES[:], TMP[j0][:], True, True, [t, free], mark=True)
            i1, free1 = tmp.take()
            mean = ac(TMP[i1][:], bank[:], ACT.Copy, [mt, free1], scale=1.0 / D)
            mgive(b, [mean])
            tmp.give(j0, [mt])
            ss = SumSq()
            for z in range(8):
                c = tt(CO[:, z, :], CO[:, z, :], TMP[i1][:], ALU.subtract, [mean])
                conv_tok[z] = c
                ss.add(CO[:, z, :], c)
            tmp.give(i1, [c])
            yield
            yield
            c, ct_, b = ss.columns()
            r, ct_ = rsqrt_cols(c, T, 1.0 / D, ct_)
            mgive(b, [ct_])
            yield
            b, bank, rt = spread(r, ct_)
            for z in range(8):
                c = tt(CO[:, z, :], CO[:, z, :], bank[:], ALU.mult, [rt, conv_tok[z]])
                s_ = ac(CO[:, z, :], CO[:, z, :], ACT.Silu, c, bias=vec("ln_b", z), scale=vec("ln_g", z))
                a_tok.append(cut(CO[:, z, :], AH[:, z, :], AL[:, z, :], [s_, f], eng=pool))
            mgive(b, [c])

        a_tok = []
        rate[:] = [1, 0]
        side.append(layer_norm(t))
        for i in range(8):
            gemm(W_IN, 40 + i, 8, hi, lo, done_already, gc_evac(i))
        flush()
        f = fence()
        z_tok = []
        for i in range(8):
            def evac(bank, t_, i=i):
                j, free = tmp.take()
                a = stt(TMP[j][:], bank[:], vec("b_pw", i), GC[:, i, :], ALU.add, ALU.mult, [t_, gc_tok[i], free])
                c = tt(TMP[j][:], TMP[j][:], HM[:, i, :], ALU.add, [a, hm_tok[i]])
                z_ = cut(TMP[j][:], HH[:, i, :], HL[:, i, :], [c, f])
                tmp.give(j, z_)
                z_tok.append(z_)
                return [a]
            gemm("w_pw", i, 8, lambda k: AH[:, k, :], lambda k: AL[:, k, :], by_tile(a_tok), evac)

        x_tok = [xt] * 8

        rate[:] = [0, 0]
        lo_engine[0] = dve
        ss = SumSq()

        def out_evac(i):
            def evac(bank, t_):
                x_tok[i] = stt(XT[:, i, :], bank[:], MOD[:, 16 + i:17 + i], XT[:, i, :], ALU.mult, ALU.add,
                               [t_, x_tok[i], modb])
                ss.add(XT[:, i, :], x_tok[i])
                return [x_tok[i]]
            return evac

        for i in range(8):
            gemm("w_out", i, 8, hi, lo, by_tile(z_tok), out_evac(i))

        gffn = keepc(8)
        gf = stt(gffn, MOD[:, 32:40], 1.0, V_[:, VEC["g_ffn"]:VEC["g_ffn"] + 8], ALU.add, ALU.mult, [modb])
        gg = keepc(8)
        ggt = tt(gg, V_[:, VEC["g_fin"]:VEC["g_fin"] + 8], V_[:, VEC["g_pre"]:VEC["g_pre"] + 8], ALU.mult, vecs)

        def ffn_up(tiles, h_tok, f, rows=None):
            mid = []
            for i in range(NFT):
                pend = {}

                def keep(bank, t):
                    j, free = tmp.take()
                    if rows is None:
                        pend["a"] = ac(TMP[j][:], bank[:], ACT.Silu, [t, free])
                        freed = pend["a"]
                    else:
                        freed = tt(TMP[j][:], bank[:], RROW[:], ALU.mult, [t, free, rows[0]])
                        pend["a"] = ac(TMP[j][:], TMP[j][:], ACT.Silu, freed)
                    pend["j"] = j
                    return [freed]

                def evac(bank, t):
                    j = pend["j"]
                    b = c = tt(TMP[j][:], TMP[j][:], bank[:], ALU.mult, [t, pend["a"]])
                    if rows is not None:
                        c = tt(TMP[j][:], TMP[j][:], RROW[:], ALU.mult, c)
                    z_ = cut(TMP[j][:], MH[:, i, :], ML[:, i, :], [c, f], eng=pool if rows is not None else None)
                    tmp.give(j, z_)
                    mid.append(z_)
                    return [b]

                gemm(*tiles(i, 0), 8, hi, lo, by_tile(h_tok), keep)
                gemm(*tiles(i, 1), 8, hi, lo, by_tile(h_tok), evac)
            return mid

        f = fence()
        h_tok = normed(lambda i: XT[:, i, :], 8, lambda i: gffn[:, i:i + 1], rows_of(ss, D), [x_tok, gf],
                       hi, lo, lambda i: MOD[:, 24 + i:25 + i])
        mid = ffn_up(lambda i, z: ("w_up1", i + z * NFT), h_tok, f)

        trig = []

        def rotary():
            j, free = tmp.take()
            posi = TMP[j][:].bitcast(I32)
            pt = once("l_pos", posi, A["pos"].broadcast_to([128, S]), free)
            k, free2 = tmp.take()
            yield
            pf = cp(TMP[k][:], posi, [pt, free2])
            kk = TMP[j][:]
            u = pf
            f = fence()
            for z, (inv, sg) in enumerate((("invr", "sgr"), ("invm", "sgm"))):
                ang = TRIG[:, 2 * z, :]
                t = ts(ang, TMP[k][:], const(inv), None, ALU.mult, after=[pf, f, cst])
                for m in (2048.0, 1.0):
                    u = ts(kk, ang, 1.0 / (m * 2 * np.pi), MAGIC, ALU.mult, ALU.add, [t, u])
                    u = ts(kk, kk, MAGIC, None, ALU.subtract, after=u)
                    for cc in (TWO_PI_1, TWO_PI_2, TWO_PI_3):
                        t = stt(ang, kk, -cc * m, ang, ALU.mult, ALU.add, [u, t])
                    u = t
                    yield
                sn = TRIG[:, 2 * z + 1, :]
                t = ts(ang, ang, PI_IN, -PI_IN, ALU.min, ALU.max, t)
                s_ = ac(sn, ang, ACT.Sin, [t, f])
                s_ = ac(sn, sn, ACT.Copy, s_, scale=const(sg))
                u = ts(ang, ang, float(np.pi / 2), None, ALU.add, after=[t, s_])
                t = ts(kk, ang, float(np.pi), -2 * float(np.pi), ALU.is_gt, ALU.mult, u)
                u = t = tt(ang, ang, kk, ALU.add, t)
                t = ts(ang, ang, PI_IN, -PI_IN, ALU.min, ALU.max, t)
                trig.extend([s_, ac(ang, ang, ACT.Sin, t)])
                yield
            tmp.give(j, [u])
            tmp.give(k, [u])

        COSR, SINR, COSM, SINM = (TRIG[:, z, :] for z in range(4))

        f = fence()
        ss1, ss2 = SumSq(), SumSq()
        h_tok = []

        def down_evac(i):
            def evac(bank, t_):
                x_tok[i] = stt(XT[:, i, :], bank[:], MOD[:, 40 + i:41 + i], XT[:, i, :], ALU.mult, ALU.add,
                               [t_, x_tok[i], modb])
                e = pool if i < 7 else None
                a = ac(HH[:, i, :], XT[:, i, :], ACT.Copy, [x_tok[i], ggt, f], scale=gg[:, i:i + 1])
                ss1.add(XT[:, i, :], x_tok[i], eng=e)
                ss2.add(XT[:, i, :], x_tok[i], scale=vec("g_fin", i), eng=e)
                h_tok.append([a, stt(HL[:, i, :], XT[:, i, :], gg[:, i:i + 1], HH[:, i, :].bitcast(F32), ALU.mult,
                                     ALU.subtract, [a, f])])
                return [x_tok[i]]
            return evac

        side.append(rotary())
        rate[0] = 1
        for i in range(8):
            gemm("w_down1", i, NFT, lambda k: MH[:, k, :], lambda k: ML[:, k, :], by_tile(mid), down_evac(i))
        flush()
        rate[0] = 1
        RCOL = keepc(4)
        rrow = [None]

        def final_rows():
            c1, t1, b1 = ss1.columns()
            c2, t2, b2 = ss2.columns()
            r1, t1 = rsqrt_cols(c1, T, 1.0 / D, t1)
            mgive(b1, [t1])
            v = scratch(4)
            t = tt(v, r1, r1, ALU.mult, t1)
            v2 = scratch(4)
            t = tt(v2, v, c2, ALU.mult, [t, t2])
            mgive(b2, [t])
            r2, t = rsqrt_cols(v2, T, 1.0 / D, t)
            t = tt(RCOL, r1, r2, ALU.mult, t)
            b, bank, rt = spread(RCOL, t)
            rrow[0] = [cp(RROW[:], bank[:], rt), t]
            mgive(b, [rrow[0][0]])
            s_ = tt(SINR, SINR, RROW[:], ALU.mult, [rrow[0], trig])
            trig.extend([s_, tt(COSR, COSR, RROW[:], ALU.mult, [rrow[0], trig])])
            b, bank, rt = spread(r1, t1)
            for i in range(8):
                x_tok[i] = stt(XT[:, i, :], XT[:, i, :], vec("g_fin", i), bank[:], ALU.mult, ALU.mult,
                               [x_tok[i], h_tok, rt])
            mgive(b, [x_tok[7]])

        W2 = "w_in2"
        f = fence()
        rd_tok = once("l_rd", RD[:], A["ret_decay"], f)
        rv_tok, srg_tok, cq_tok, ckv_tok, rq_tok, rk_tok = [], [], [], [], [], []

        def evac_rv(t, bank, tok):
            if t == 0:
                final_rows()
            rv_tok.append(ac(RV[:, t, :], bank[:], ACT.Copy, [tok, f, rrow[0]], scale=RCOL[:, t:t + 1]))
            return [rv_tok[-1]]
        gemm_tok("w_rv", 0, 8, hi, lo, lambda k: h_tok[k], evac_rv)
        ssq, sskv = SumSq(), SumSq()

        def scaled(dst, toks, ss):
            def evac(bank, t):
                a = tt(dst, bank[:], RROW[:], ALU.mult, [t, f, rrow[0]])
                toks.append(a)
                ss.add(dst, a, eng=pool)
                return [a]
            return evac
        for i in range(3):
            gemm(W2, 12 + i, 8, hi, lo, by_tile(h_tok), scaled(CQ[:, i, :], cq_tok, ssq))
        for i in range(2):
            gemm(W2, 15 + i, 8, hi, lo, by_tile(h_tok), scaled(CKV[:, i, :], ckv_tok, sskv))

        def rope_rows(dst, bank, after):
            j, free = tmp.take()
            k, free2 = tmp.take()
            a = tt(TMP[j][64:96, :], bank[64:96, :], COSM[64:96, :], ALU.mult, [after, trig, free])
            b = tt(TMP[k][64:96, :], bank[96:128, :], SINM[96:128, :], ALU.mult, [after, trig, free2])
            c = tt(dst, TMP[j][64:96, :], TMP[k][64:96, :], ALU.add, [a, b])
            tmp.give(j, [c])
            tmp.give(k, [c])
            return [a, b], c

        def evac_kr(bank, t):
            ab, c = rope_rows(KR[64:96, :], bank, [t, f])
            held["kr"] = tt(KR[64:96, :], KR[64:96, :], RROW[64:96, :], ALU.mult, c)
            return ab
        gemm("w_kr", 0, 8, hi, lo, by_tile(h_tok), evac_kr)

        def rope_full(dst, toks):
            def evac(bank, t):
                j, free = tmp.take()
                k, free2 = tmp.take()
                a = tt(TMP[j][:], bank[:], COSR, ALU.mult, [t, trig, free])
                b0 = tt(TMP[k][0:64, :], bank[64:128, :], SINR[64:128, :], ALU.mult, [t, free2])
                b1 = tt(TMP[k][64:128, :], bank[0:64, :], SINR[0:64, :], ALU.mult, [t, free2])
                c = tt(dst, TMP[j][:], TMP[k][:], ALU.add, [a, b0, b1, f], eng=pool)
                tmp.give(j, [c])
                tmp.give(k, [c])
                toks.append(c)
                return [a, b0, b1]
            return evac

        def srg_evac(i):
            def evac(bank, t):
                j, free = tmp.take()
                a = tt(TMP[j][:], bank[:], RROW[:], ALU.mult, [t, free])
                srg_tok.append(ac(SRG[:, i, :], TMP[j][:], ACT.Silu, [a, f]))
                tmp.give(j, [srg_tok[-1]])
                return [a]
            return evac

        cqs, ckvs = [], []

        def latent_norms():
            for ss_, n, name, src, toks, h_, l_, dst in (
                    (ssq, 3, "g_q", CQ, cq_tok, CQH, CQL, cqs), (sskv, 2, "g_kv", CKV, ckv_tok, KVH, KVL, ckvs)):
                c, t, b = ss_.columns()
                r, t = rsqrt_cols(c, T, 1.0 / (128 * n), t)
                mgive(b, [t])
                yield
                dst += normed(lambda i: src[:, i, :], n, lambda i: vec(name, i), spread(r, t), [toks, f],
                              lambda i: h_[:, i, :], lambda i: l_[:, i, :])
                yield

        side.append(latent_norms())
        for i in range(4):
            gemm(W2, i, 8, hi, lo, by_tile(h_tok), rope_full(RQ[:, i, :], rq_tok))
            gemm(W2, 4 + i, 8, hi, lo, by_tile(h_tok), rope_full(RK[:, i, :], rk_tok))
        flush()
        for i in range(4):
            gemm(W2, 8 + i, 8, hi, lo, by_tile(h_tok), srg_evac(i))

        fm = fence()
        yb = [main.take() for _ in range(T)]
        stats, aggs = scratch(96), scratch(32)
        ytok = [None] * T
        rsc = [None] * 4
        rused = [fm, fm]

        def ret_scores(h):
            off, rsc[h] = 0, []
            for k in range(T):
                wdt = (T - k) * 128
                b_, bk, free = mbank()
                st = mm(bk[:, 0:wdt], RK[:, h, k * 128:(k + 1) * 128], RQ[:, h, k * 128:512], True, True,
                        [rq_tok[h], rk_tok[h], free], mark=True)
                x_ = tt(SC2[h % 2][:, off:off + wdt], bk[:, 0:wdt], RD[:, h, 0:wdt], ALU.mult,
                        [st, rd_tok, rused[h % 2]])
                mgive(b_, [x_])
                rsc[h].append((x_, off))
                off += wdt

        def ret_values(h):
            for t in range(T):
                for k in range(t + 1):
                    x_, off = rsc[h][k]
                    c0 = off + (t - k) * 128
                    pt = mm(P_[yb[t][0]][:, h * 128:(h + 1) * 128], SC2[h % 2][:, c0:c0 + 128],
                            RV[:, k, h * 128:(h + 1) * 128], k == 0, k == t, [x_, rv_tok, yb[t][1]], mark=(k == t))
                ytok[t] = pt
            rused[h % 2] = pt

        ret_scores(0)
        for h in range(1, 4):
            ret_scores(h)
            ret_values(h - 1)
        ret_values(3)
        f2 = fence()
        for t in range(T):
            bk = P_[yb[t][0]]
            for h in range(4):
                n = 4 * t + h
                z_ = bstat(stats[:, 6 * n:6 * n + 6], bk[:, h * 128:(h + 1) * 128], ytok[t])
        for n in range(16):
            z_ = baggr(aggs[:, 2 * n:2 * n + 2], stats[:, 6 * n:6 * n + 6], z_)
        av = aggs.rearrange("p (n two) -> p n two", two=2)
        rr, d5 = rsqrt_cols(av[:, :, 1], 16, 1.0, z_)
        for t in range(T):
            for h in range(4):
                n = 4 * t + h
                d7 = ts(RY[:, t, h * 128:(h + 1) * 128], P_[yb[t][0]][:, h * 128:(h + 1) * 128], av[:, n, 0:1],
                        rr[:, n:n + 1], ALU.subtract, ALU.mult, after=[d5, fm])
            main.give(yb[t][0], [d7])
        mix_tok = []

        def ret_out():
            for h in range(4):
                b_, bk, free = mbank()
                for t in range(T):
                    tk_ = tr(bk[:, t * 128:(t + 1) * 128], RY[:, t, h * 128:(h + 1) * 128], IDENT, [d7, free],
                             mark=(t == 3))
                j, freej = tmp.take()
                c = stt(TMP[j][:], bk[:], vec("ret_g", h), SRG[:, h, :], ALU.mult, ALU.mult, [tk_, srg_tok, freej])
                mgive(b_, [c])
                z_ = cut(TMP[j][:], HH[:, h, :], HL[:, h, :], [c, fm], eng=pool)
                tmp.give(j, z_)
                mix_tok.append(z_)

        qh_tok, kh_tok, vm_tok = [], [], []
        cqh, cql = (lambda k: CQH[:, k, :]), (lambda k: CQL[:, k, :])
        kvh, kvl = (lambda k: KVH[:, k, :]), (lambda k: KVL[:, k, :])
        rate[0] = 0
        for i in range(8):
            def evac(bank, t, i=i):
                a = ac(QH[0:64, i, :], bank[0:64, :], ACT.Copy, [t, f2])
                ab, c = rope_rows(QH[64:96, i, :], bank, [t, f2, a])
                qh_tok.append([a, c])
                return [a] + ab
            gemm("w_uq", i, 3, cqh, cql, by_tile(cqs), evac)
        ret_out()
        f = fence()
        for i in range(4):
            def evac(bank, t, i=i):
                a = ac(KH[0:64, 2 * i, :], bank[0:64, :], ACT.Copy, [t, f])
                b = cp(KH[0:64, 2 * i + 1, :], bank[64:128, :], [t, f, a])
                kh_tok.extend([a, b])
                return [a, b]
            gemm("w_uk", i, 2, kvh, kvl, by_tile(ckvs), evac)
        for h in range(8):
            kh_tok.append(cp(KH[64:96, h, :], KR[64:96, :], [held["kr"], f]))

        def evac_vm(t, bank, tok):
            vm_tok.append(ac(VM[:, t, :], bank[:], ACT.Copy, [tok, f]))
            return [vm_tok[-1]]
        gemm_tok("w_uv", 0, 2, kvh, kvl, by_tile(ckvs), evac_vm)

        ob = [main.take() for _ in range(T)]
        RSUM = keepc(32)
        scale = 1.0 / float(np.sqrt(96.0))
        otok = [None] * T
        st_ = [{} for _ in range(32)]
        pt_used = [None] * T
        PTM = SC2[0]
        last_f = fence()

        def mla_scores(n):
            h, t = divmod(n, T)
            wdt = (t + 1) * 128
            q = slice(t * 128, (t + 1) * 128)
            b_, bk, free = mbank()
            m0 = mm(bk[:, 0:wdt], QH[:, h, q], KH[:, h, 0:wdt], True, True, [qh_tok[h], kh_tok, free], mark=True)
            m0 = tt(bk[:, q], bk[:, q], MNEG, ALU.add, m0)
            mx, nmx = scratch(1), scratch(1)
            m1 = rmax(mx, bk[:, 0:wdt], m0)
            m2 = ts(nmx, mx, -scale, None, ALU.mult, after=m1)
            j, freej = tmp.take()
            st_[n]["e"] = ac(TMP[j][:, 0:wdt], bk[:, 0:wdt], ACT.Exp, [m2, freej], bias=nmx, scale=scale,
                             accum=RSUM[:, 8 * t + h:8 * t + h + 1])
            st_[n]["j"] = j
            mgive(b_, [st_[n]["e"]])

        def mla_turn(n):
            h, t = divmod(n, T)
            wdt = (t + 1) * 128
            j = st_[n]["j"]
            b_, bk, free = mbank()
            for k in range(t + 1):
                tk_ = tr(bk[:, k * 128:(k + 1) * 128], TMP[j][:, k * 128:(k + 1) * 128], IDENT,
                         [st_[n]["e"], free], mark=(k == t))
            tmp.give(j, [tk_])
            off = 64 * t * (t + 1)
            st_[n]["c"] = ac(PTM[:, off:off + wdt], bk[:, 0:wdt], ACT.Copy, [tk_, pt_used[t], last_f])
            mgive(b_, [st_[n]["c"]])

        def mla_values(n):
            h, t = divmod(n, T)
            off = 64 * t * (t + 1)
            for k in range(t + 1):
                pt = mm(P_[ob[t][0]][:, h * 64:(h + 1) * 64], PTM[:, off + k * 128:off + (k + 1) * 128],
                        VM[:, k, h * 64:(h + 1) * 64], k == 0, k == t, [st_[n]["c"], vm_tok, ob[t][1]],
                        mark=(k == t))
            otok[t] = pt
            pt_used[t] = pt

        for n in range(32 + 3):
            if n < 32:
                mla_scores(n)
            if 2 <= n < 34:
                mla_turn(n - 2)
            if n >= 3:
                mla_values(n - 3)
        RI = keepc(32)
        rt = recip(RI, RSUM, [st_[31]["e"], act.last()])
        for t in range(T):
            rb = RI[:, 8 * t:8 * t + 8].unsqueeze(2).broadcast_to([128, 8, 64])
            c = tt(MO[:, t, :].rearrange("p (h d) -> p h d", h=8), P_[ob[t][0]][:].rearrange("p (h d) -> p h d", h=8),
                   rb, ALU.mult, [rt, otok[t], f])
            main.give(ob[t][0], [c])
        for i in range(4):
            b_, bk, free = mbank()
            for t in range(T):
                tk_ = tr(bk[:, t * 128:(t + 1) * 128], MO[:, t, i * 128:(i + 1) * 128], IDENT, [c, free], mark=(t == 3))
            a = ac(HH[:, 4 + i, :], bk[:], ACT.Copy, [tk_, fm])
            z_ = tt(HL[:, 4 + i, :], bk[:], HH[:, 4 + i, :].bitcast(F32), ALU.subtract, [a, tk_])
            mgive(b_, [z_])
            mix_tok.append([a, z_])

        f = fence()
        pt = once("l_pt", PTS[:], A["pT"], f)
        ptok = []
        toks = []

        def branch(dst, gname, ss, f):
            def make(i):
                def evac(bank, t):
                    a = ss.add(bank[:], t, eng=pool if i < 7 else None)
                    toks.append(ts(dst[:, i, :], bank[:], vec(gname, i), None, ALU.mult, after=[a, t, f]))
                    return [toks[-1]]
                return evac
            return make

        def join(src, b, bank, rt, then, later):
            last = [None]

            def first(i):
                j, free = tmp.take()
                t = last[0] = tt(TMP[j][:], src[:, i, :], bank[:], ALU.mult, [rt, toks[i], free])
                x_tok[i] = tt(XT[:, i, :], XT[:, i, :], TMP[j][:], ALU.add, [t, x_tok[i]])
                tmp.give(j, [x_tok[i]])
                then(i, t)

            in_turn(8, first, later)
            mgive(b, [last[0]])

        ssm, sse = SumSq(), SumSq()
        mk = branch(MIXO, "g_post", ssm, f)
        for i in range(8):
            gemm("w_o", i, 8, hi, lo, by_tile(mix_tok), mk(i))
            if i == 3:
                for z in range(2):
                    ptok.append(cut(PTS[:, z, :], PTH[:, z, :], PTL[:, z, :], [pt, f]))
        e_tok = []

        def e_gemm(i):
            def evac(bank, t):
                a = ac(EE[:, i, :], bank[:], ACT.Copy, [t, f])
                e_tok.append(a)
                sse.add(EE[:, i, :], a, eng=pool)
                return [a]
            gemm("w_pp", i, 2, lambda k: PTH[:, k, :], lambda k: PTL[:, k, :], by_tile(ptok), evac)

        f3 = fence()
        for i in range(3):
            e_gemm(i)
        c, t, b = ssm.columns()
        r, t = rsqrt_cols(c, T, 1.0 / D, t)
        mgive(b, [t])
        for i in range(3, 6):
            e_gemm(i)
        ss = SumSq()
        h_tok = []

        def then(i, t):
            h_tok.append([ac(hi(i), XT[:, i, :], ACT.Copy, [x_tok[i], f3], scale=vec("g_pf", i)), None])

        def later(i):
            h_tok[i][1] = stt(lo(i), XT[:, i, :], vec("g_pf", i), hi(i).bitcast(F32), ALU.mult, ALU.subtract,
                              [h_tok[i][0], f3])
            ss.add(XT[:, i, :], x_tok[i], eng=pool)

        join(MIXO, *spread(r, t), then, later)
        for i in range(6, 8):
            e_gemm(i)
        c, t, b = sse.columns()
        ECOL, ect = keepc(4), None
        ev, et = rsqrt_cols(c, T, 1.0 / D, t)
        ect = cp(ECOL, ev, et)
        mgive(b, [et])
        espill = loads.load(sem("l_es"), A["e_scratch"], EE[:], e_tok)

        f = [fence(), espill]
        rrow2 = [None]

        def ffn_rows():
            yield
            c, t, b = ss.columns()
            r, t = rsqrt_cols(c, T, 1.0 / D, t)
            mgive(b, [t])
            b, bank, rt = spread(r, t)
            rrow2[0] = cp(RROW[:], bank[:], rt)
            mgive(b, [rrow2[0]])

        g_ = ffn_rows()
        next(g_)
        next(g_, None)
        mid = ffn_up(lambda i, z: (("w_gate", "w_up")[z], i), h_tok, f, rrow2)
        f = fence()
        ssf = SumSq()
        toks = []
        mk = branch(FFO, "g_pof", ssf, f)
        for i in range(8):
            gemm("w_down", i, NFT, lambda k: MH[:, k, :], lambda k: ML[:, k, :], by_tile(mid), mk(i))

        ereload = loads.load(sem("l_er"), EE[:], A["e_scratch"], fence())
        x2 = []

        def last(i, t):
            x2.append([ac(HH[:, i, :], XT[:, i, :], ACT.Copy, [x_tok[i], t]), None])

        def last_lo(i):
            x2[i][1] = tt(HL[:, i, :], XT[:, i, :], HH[:, i, :].bitcast(F32), ALU.subtract, [x2[i][0], x_tok[i]],
                          eng=None if i % 3 == 0 else pool)

        join(FFO, *rows_of(ssf, D), last, last_lo)
        b, bank, rt = spread(ECOL, ect)
        for i in range(8):
            e_tok[i] = stt(EE[:, i, :], EE[:, i, :], vec("g_ple", i), bank[:], ALU.mult, ALU.mult, [rt, ereload])
        mgive(b, [e_tok[7]])
        for i in range(8):
            def evac(bank, t, i=i):
                j, free = tmp.take()
                a = ac(TMP[j][:], bank[:], ACT.Sigmoid, [t, free], bias=vec("b_pg", i))
                c = tt(TMP[j][:], TMP[j][:], EE[:, i, :], ALU.mult, [a, e_tok[i]])
                c = tt(XT[:, i, :], XT[:, i, :], TMP[j][:], ALU.add, [c, x_tok[i]])
                tmp.give(j, [c])
                loads.load(s_out, out[:, i, :], XT[:, i, :], c)
                return [a]
            gemm("w_pg", i, 8, hi, lo, by_tile(x2), evac)
        sp.wait((s_out, loads.total[s_out]))

        seen = W.seen
        if not A["plan"]:
            return seen

        block = ctx.enter_context(nc.Block())

        @block.sync
        def _(e):
            for item in sp.items:
                item(e)

        @block.gpsimd
        def _(e):
            for item in pool.items:
                item(e)

        @block.scalar
        def _(e):
            for item in act.items:
                item(e)

        @block.vector
        def _(e):
            for item in dve.items:
                item(e)

        @block.tensor
        def _(e):
            for item in pe.items:
                item(e)
        return seen


def _tiles(w):
    k, n = w.shape
    return np.ascontiguousarray(w.reshape(k // 128, 128, n // 128, 128).transpose(2, 1, 0, 3)).reshape(
        n // 128, 128, k)


def _blocks(w, c):
    k, n = w.shape
    return np.ascontiguousarray(w.reshape(k // 128, 128, n // c, c).transpose(2, 1, 0, 3)).reshape(
        n // c, 128, k // 128 * c)


def _fold(v):
    return np.ascontiguousarray(np.asarray(v).reshape(-1, 128).T)


def layout(x):
    f = np.float32
    win, bin_ = x["w_in"][0], x["b_in"][0]
    o = {}
    o["xT"] = np.ascontiguousarray(x["x"][0].T.reshape(8, 128, S).transpose(1, 0, 2))
    o["pT"] = np.ascontiguousarray(x["p_2"][0, 0].T.reshape(2, 128, S).transpose(1, 0, 2))
    o["pos"] = np.ascontiguousarray(x["positions_2"].reshape(1, S))
    o["w_ada"] = _blocks(x["w_ada"][0], 256).reshape(24, 128, 8, 256)
    o["w_in"] = _tiles(np.concatenate([win[:, 0:4096], win[:, 5120:6144], win[:, 6152:8200]], axis=1))
    o["w_v"] = _blocks(win[:, 4096:5120], 512)
    pad = np.zeros((D, 28), f)
    o["w_if"] = _tiles(np.concatenate([win[:, 6144:6148], pad, win[:, 6148:6152], pad, pad, pad, np.zeros((D, 8), f)],
                                      axis=1))
    o["b_v"] = np.ascontiguousarray(bin_[4096:5120].reshape(1, 1024))
    o["w_pw"] = _tiles(x["w_conv_pw"][0])
    o["w_out"] = _tiles(x["w_out"][0])
    o["w_up1"] = _tiles(x["w_ffn_up"][0])
    o["w_down1"] = _tiles(x["w_ffn_down"][0])
    w2 = x["w_in_2"][0]
    o["w_in2"] = _tiles(np.concatenate([w2[:, 0:1024], w2[:, 1536:2688]], axis=1))
    o["w_rv"] = _blocks(w2[:, 1024:1536], 512)
    kr = w2[:, 2688:2720]
    o["w_kr"] = _tiles(np.concatenate([np.zeros((D, 64), f), kr, kr[:, 16:32], kr[:, 0:16]], axis=1))
    uq = x["w_uq_2"][0].reshape(384, 8, 96)
    o["w_uq"] = _tiles(np.concatenate([uq, uq[:, :, 80:96], uq[:, :, 64:80]], axis=2).reshape(384, 1024))
    ukv = x["w_ukv_2"][0].reshape(256, 8, 128)
    o["w_uk"] = _tiles(np.ascontiguousarray(ukv[:, :, 0:64]).reshape(256, 512))
    o["w_uv"] = _blocks(np.ascontiguousarray(ukv[:, :, 64:128]).reshape(256, 512), 512)
    o["w_o"] = _tiles(x["w_o_2"][0])
    o["w_gate"] = _tiles(x["w_gate_2"][0])
    o["w_up"] = _tiles(x["w_up_2"][0])
    o["w_down"] = _tiles(x["w_down_2"][0])
    o["w_pp"] = _tiles(x["w_ple_proj_2"][0])
    o["w_pg"] = _tiles(x["w_ple_gate_2"][0])

    bif = np.concatenate([bin_[6144:6148], np.zeros(28, f), bin_[6148:6152], np.zeros(92, f)])
    parts = {
        "c": x["c"][0], "b_ada": x["b_ada"][0], "g_mix": x["norm_mix_g"][0], "b_glu": bin_[0:2048],
        "b_qk": bin_[2048:4096], "b_o": bin_[5120:6144], "b_mg": bin_[6152:8200], "b_if": bif,
        "dw_b": x["conv_dw_b"][0], "ln_g": x["conv_ln_g"][0], "ln_b": x["conv_ln_b"][0], "b_pw": x["b_conv_pw"][0],
        "qk_b": x["qk_conv_b"][0], "ml_g": x["mlstm_norm_g"][0], "g_ffn": x["norm_ffn_g"][0],
        "g_fin": x["final_norm_g"], "g_pre": x["pre_mix_norm_2"][0], "ret_g": x["ret_gn_w_2"][0],
        "g_q": x["mla_q_norm_2"][0], "g_kv": x["mla_kv_norm_2"][0], "g_post": x["post_mix_norm_2"][0],
        "g_pf": x["pre_ffn_norm_2"][0], "g_pof": x["post_ffn_norm_2"][0], "g_ple": x["ple_norm_2"][0],
        "b_pg": x["b_ple_gate_2"][0],
    }
    cols = [_fold(parts[n]) for n in VEC if n in parts]
    cols.append(x["conv_dw_w"][0].reshape(31, 8, 128).transpose(2, 1, 0).reshape(128, 248))
    cols.append(x["qk_conv_w"][0].reshape(4, 16, 128).transpose(2, 1, 0).reshape(128, 64))
    o["vecs"] = np.ascontiguousarray(np.concatenate(cols, axis=1))

    p = np.arange(128)
    cst = np.zeros((128, NCONST), f)
    cst[:, 0:128] = np.eye(128, dtype=f)
    cst[:, 128:256] = np.where(p[:, None] > p[None, :], f(BIG), f(0))
    cst[:, 256:384] = np.where(p[None, :] > p[:, None], f(-BIG), f(0))

    def inv(half):
        return (f(1.0) / (f(10000.0) ** (np.arange(half, dtype=f) / f(half)))).astype(f)
    cst[:, 384] = inv(64)[p % 64]
    cst[:, 385] = inv(16)[p % 16]
    cst[:, 386] = np.where(p < 64, 1.0, -1.0)
    cst[:, 387] = np.where(p % 32 < 16, -1.0, 1.0)
    o["consts"] = cst
    sel = np.zeros((4, 4, 128), f)
    for h in range(4):
        sel[h, h, :] = 1.0
    o["sel"] = sel
    t = np.arange(S)
    diff = t[None, :] - p[:, None]
    lg = np.log(1.0 - 2.0 ** (-5.0 - np.arange(4)))
    rd = [np.where(diff >= 0, np.exp(np.maximum(diff, 0) * lg[h]), 0.0) * 128.0 ** -0.5 for h in range(4)]
    o["ret_decay"] = np.ascontiguousarray(np.stack(rd, axis=1).astype(f))
    return o


def declare(nc, arrays, plan):
    A = {n: nc.dram_tensor(f"in_{n}", a.shape, mybir.dt.from_np(a.dtype), kind="ExternalInput").ap()
         for n, a in arrays.items()}
    A["plan"] = plan
    A["e_scratch"] = nc.dram_tensor("e_scratch", (128, 8, S), F32, kind="Internal").ap()
    out = nc.dram_tensor("out_0", (128, 8, S), F32, kind="ExternalOutput").ap()
    return program(nc, A, out)


def kernel(**inputs):
    import concourse.bacc as bacc
    from concourse.bass_utils import run_bass_kernel_spmd

    arrays = layout({n: np.asarray(a) for n, a in inputs.items()})
    plan = declare(bacc.Bacc("TRN2", target_bir_lowering=False, num_devices=1), arrays, [])
    nc = bacc.Bacc("TRN2", target_bir_lowering=False, num_devices=1)
    declare(nc, arrays, plan)
    r = run_bass_kernel_spmd(nc, [{f"in_{n}": a for n, a in arrays.items()}], core_ids=[0])
    got = r.results[0]["out_0"]
    return np.ascontiguousarray(got.transpose(1, 0, 2).reshape(D, S).T).reshape(1, S, D)
```

```python
from contextlib import ExitStack

import numpy as np

import concourse.bass as bass
from concourse import mybir

ALU = mybir.AluOpType
ACT = mybir.ActivationFunctionType
AX = mybir.AxisListType
F32 = mybir.dt.float32
F32R = mybir.dt.float32r
I32 = mybir.dt.int32

D, S, T = 1024, 512, 4
NF = 2816
NFT = NF // 128
EPS = 1e-6
BIG = 1e30
CHUNK = 8

VEC = {}
_at = 0
for _name, _n in [("c", 8), ("b_ada", 48), ("g_mix", 8), ("b_glu", 16), ("b_qk", 16), ("b_o", 8), ("b_mg", 16),
                  ("b_if", 1), ("dw_b", 8), ("ln_g", 8), ("ln_b", 8), ("b_pw", 8), ("qk_b", 16), ("ml_g", 8),
                  ("g_ffn", 8), ("g_fin", 8), ("g_pre", 8), ("ret_g", 4), ("g_q", 3), ("g_kv", 2), ("g_post", 8),
                  ("g_pf", 8), ("g_pof", 8), ("g_ple", 8), ("b_pg", 8), ("dw_w", 248), ("qk_w", 64)]:
    VEC[_name] = _at
    _at += _n
NVEC = _at
CONST = {"ident": 0, "mbig": 128, "mneg": 256, "invr": 384, "invm": 385, "sgr": 386, "sgm": 387}
NCONST = 388

TWO_PI_1 = 6.28125
TWO_PI_2 = float(np.float32(int((2 * np.pi - TWO_PI_1) * 2 ** 21) / 2 ** 21))
TWO_PI_3 = float(np.float32(2 * np.pi - TWO_PI_1 - TWO_PI_2))
MAGIC = 12582912.0
PI_IN = 3.14159250259


class Engine:

    def __init__(self, sem):
        self.sem, self.n, self.items, self.waited = sem, 0, [], {}

    def wait(self, after):
        if after is None:
            return
        if isinstance(after, list):
            for a in after:
                self.wait(a)
            return
        sem, value = after
        if self.waited.get(sem, 0) < value:
            self.waited[sem] = value
            self.items.append(lambda e: e.wait_ge(sem, value))

    def do(self, issue, after=None, mark=True):
        self.wait(after)
        if not mark:
            self.items.append(issue)
            return None
        self.n += 1
        sem = self.sem
        self.items.append(lambda e: issue(e).then_inc(sem, 1))
        return (sem, self.n)

    def last(self):
        return (self.sem, self.n)


class Queue:

    def __init__(self, engine):
        self.engine, self.total = engine, {}

    def load(self, sem, out, in_, after=None):
        self.engine.wait(after)
        self.total[sem] = self.total.get(sem, 0) + 16
        self.engine.items.append(lambda e: e.dma_start(out, in_).then_inc(sem, 16))
        return (sem, self.total[sem])


class Slots:

    def __init__(self, n):
        self.free = [(i, []) for i in range(n)]

    def take(self):
        return self.free.pop(0)

    def give(self, i, after):
        self.free.append((i, after))


def program(nc, A, out):
    ctx = ExitStack()
    with ctx:
        def sem(name):
            return ctx.enter_context(nc.semaphore(name))

        base = 16512

        def at(name, off, shape, dt=F32):
            return nc.alloc_sbuf_tensor_at(name, shape, dt, offset=base + off)

        P_ = [ctx.enter_context(nc.psum_tensor(f"bank{i}", [128, 512], F32)) for i in range(8)]
        o = 0
        XT = at("XT", o, [128, 8, S]); o += 16384
        HH = at("HH", o, [128, 8, S], F32R)
        FFO = at("FFO", o, [128, 8, S]); o += 16384
        HL = at("HL", o, [128, 8, S], F32R); o += 16384
        NRAW, NSPL = 4, 3
        RAW = [at(f"raw{i}", o + 4096 * i, [128, 1024]) for i in range(NRAW)]; o += 4096 * NRAW
        SPH = [at(f"sph{i}", o + 4096 * i, [128, 1024], F32R) for i in range(NSPL)]; o += 4096 * NSPL
        SPL = [at(f"spl{i}", o + 4096 * i, [128, 1024], F32R) for i in range(NSPL)]; o += 4096 * NSPL
        V_ = at("vecs", o, [128, NVEC]); o += (NVEC * 4 + 31) // 32 * 32
        C_ = at("consts", o, [128, NCONST]); o += (NCONST * 4 + 31) // 32 * 32
        ONES = at("ones", o, [128, 128]); o += 512
        SM = at("small", o, [128, 256]); o += 1024
        KEEP = at("kept", o, [128, 176]); o += 704
        MOD = at("mod", o, [128, 48]); o += 192
        XP = at("xpad", o, [128, 2, 516])
        TRIG = at("trig", o, [128, 4, S]); o += 4128
        HT = at("htok", o, [128, 4, 258]); o += 4128
        MROW = at("mrow", o, [4, S]); o += 2048
        NT = 6
        RROW = at("rrow", o, [128, S]); o += 2048
        TMP = [at(f"tmp{i}", o + 2048 * i, [128, S]) for i in range(NT)]; o += 2048 * NT
        B = o
        MH = at("midh", B, [128, NFT, S], F32R)
        ML = at("midl", B + NFT * 2048, [128, NFT, S], F32R)
        CP = at("convin", B, [128, 8, 542])
        GC = at("gconv", B, [128, 8, S])
        CO = at("convout", B + 17344, [128, 8, S])
        VT = at("vtok", B + 33728, [128, T, 4, 257])
        QK = at("qk", B + 50176, [128, 2, 4, S])
        HM = at("hm", B + 66560, [128, 8, S])
        SC = at("sc", B + 82944, [128, 1280])
        VB = at("vbias", B + 82944, [128, 1024])
        SEL = at("sel", B + 88064, [4, 4, 128])
        ADA = [at(f"ada{i}", B + 33728 + 8192 * i, [128, 8, 256]) for i in range(6)]
        ROWS = [at(f"row{i}", B + 50176 + 2048 * i, [4, S]) for i in range(4)]
        ROWC = at("rowc", B + 66560, [4, 10, 128])
        AH = at("ah", B + 33728, [128, 8, S], F32R)
        AL = at("al", B + 33728 + 16384, [128, 8, S], F32R)
        QH = at("qh", B, [96, 8, S])
        CQ = at("cq", B, [128, 3, S])
        CKV = at("ckv", B + 6144, [128, 2, S])
        KH = at("kh", B + 16384, [96, 8, S])
        VM = at("vm", B + 32768, [128, T, S])
        MO = at("mo", B + 40960, [128, T, S])
        CQH = at("cqh", B + 40960, [128, 3, S], F32R)
        CQL = at("cql", B + 47104, [128, 3, S], F32R)
        PTM = at("ptm", B + 49152, [128, 1280])
        SC2 = at("sc2", B + 54272, [128, 1280])
        KVH = at("kvh", B + 53248, [128, 2, S], F32R)
        KR = at("kr", B + 59392, [128, S])
        RV = at("rv", B + 61440, [128, T, S])
        RQ = at("rq", B + 69632, [128, 2, S])
        RK = at("rk", B + 73728, [128, 2, S])
        RG = at("rg", B + 69632, [128, 4, S])
        KVL = at("kvl", B + 77824, [128, 2, S], F32R)
        RY = at("ry", B + 77824, [128, T, S])
        RD = at("rd", B + 86016, [128, 2, S])
        MIXO = at("mixo", B + 54272, [128, 8, S])
        PTS = at("pts", B, [128, 2, S])
        PTH = at("pth", B + 4096, [128, 2, S], F32R)
        PTL = at("ptl", B + 8192, [128, 2, S], F32R)
        EE = at("ee", B + 16384, [128, 8, S])
        assert base + B + 90112 <= 229368, base + B + 90112

        pe, act, dve, pool, sp = (Engine(sem(n)) for n in ("s_pe", "s_act", "s_dve", "s_pool", "s_sp"))
        loads = Queue(sp)
        s_raw = [sem(f"s_raw{i}") for i in range(NRAW)]
        s_ada = [sem(f"s_ada{i}") for i in range(6)]
        s_out = sem("s_out")

        def once(name, out_, in_, after=None):
            return loads.load(sem(name), out_, in_, after)

        def mm(out_, l, r, start, stop, after=None, mark=False):
            return pe.do(lambda e: e.matmul(out_, l, r, start=start, stop=stop), after, mark)

        def tr(out_, in_, ident, after=None, mark=False):
            return pe.do(lambda e: e.transpose(out_, in_, ident), after, mark)

        def ac(out_, in_, f, after=None, bias=0.0, scale=1.0, accum=None):
            if accum is not None:
                return act.do(lambda e: e.activation(out_, in_, f, bias=bias, scale=scale, accum_out=accum), after)
            return act.do(lambda e: e.activation(out_, in_, f, bias=bias, scale=scale), after)

        def tt(out_, a, b, op, after=None, eng=None):
            return (eng or dve).do(lambda e: e.tensor_tensor(out_, a, b, op), after)

        def ts(out_, a, s1, s2, op0, op1=None, after=None, eng=None):
            if op1 is None:
                return (eng or dve).do(lambda e: e.tensor_scalar(out_, a, s1, None, op0), after)
            return (eng or dve).do(lambda e: e.tensor_scalar(out_, a, s1, s2, op0, op1), after)

        def stt(out_, a, s1, b, op0, op1, after=None):
            return dve.do(lambda e: e.scalar_tensor_tensor(out_, a, s1, b, op0, op1), after)

        def cp(out_, a, after=None, eng=None):
            return (eng or dve).do(lambda e: e.tensor_copy(out_, a), after)

        def setv(out_, v, after=None, eng=None):
            return (eng or pool).do(lambda e: e.memset(out_, v), after)

        def recip(out_, a, after=None):
            return dve.do(lambda e: e.reciprocal(out_, a), after)

        def always(tok):
            return lambda k: tok

        def by_tile(toks):
            return lambda k: toks[k]

        done_already = always([None, None])

        def bstat(out_, a, after=None):
            return dve.do(lambda e: e.bn_stats(out_, a), after)

        def baggr(out_, a, after=None):
            return dve.do(lambda e: e.bn_aggr(out_, a), after)

        def rmax(out_, a, after=None):
            return dve.do(lambda e: e.tensor_reduce(out_, a, AX.X, ALU.max), after)

        def scan(out_, a, b, first, op0, op1, after=None):
            return dve.do(lambda e: e.tensor_tensor_scan(out_, a, b, first, op0, op1), after)

        def vec(name, i, p=slice(0, 128)):
            return V_[p, VEC[name] + i:VEC[name] + i + 1]

        def const(name, p=slice(0, 128)):
            return C_[p, CONST[name]:CONST[name] + 1]

        IDENT = C_[:, 0:128]
        MBIG = C_[:, 128:256]
        MNEG = C_[:, 256:384]

        main, misc, tmp = Slots(4), Slots(4), Slots(NT)

        def mbank():
            i, t = misc.take()
            return 4 + i, P_[4 + i], t

        def mgive(i, t):
            misc.give(i - 4, t)

        def fence():
            return [pe.last(), act.last(), dve.last(), pool.last()]

        class Weights:
            def __init__(self, plan):
                self.plan, self.seen = plan, []
                self.raw_after = [None] * NRAW
                self.spl_after = [None] * NSPL
                self.loaded = self.cut = self.used = self.finished = 0
                self.ahead = 2
                self.raw_tok, self.spl_tok = {}, {}

            def load(self):
                n = self.loaded
                if n >= len(self.plan):
                    return
                name, tile, first, size = self.plan[n]
                src = A[name][tile, :, first:first + size]
                self.raw_tok[n] = loads.load(s_raw[n % NRAW], RAW[n % NRAW][:, 0:size], src, self.raw_after[n % NRAW])
                self.loaded += 1

            def start(self):
                for _ in range(NRAW - 1):
                    self.load()

            def split(self):
                n = self.cut
                size = self.plan[n][3]
                raw, hi, lo = RAW[n % NRAW][:, 0:size], SPH[n % NSPL][:, 0:size], SPL[n % NSPL][:, 0:size]
                a = ac(hi, raw, ACT.Copy, [self.raw_tok[n], self.spl_after[n % NSPL]])
                b = tt(lo, raw, hi.bitcast(F32), ALU.subtract, [a, self.raw_tok[n], self.spl_after[n % NSPL]],
                       eng=lo_engine[0])
                self.raw_after[n % NRAW] = [a, b]
                self.spl_tok[n] = [a, b]
                self.cut += 1
                self.load()

            def ready(self, eng=None):
                was = lo_engine[0]
                lo_engine[0] = eng or was
                while self.cut < min(self.finished + self.ahead, len(self.plan)):
                    self.split()
                lo_engine[0] = was

            def take(self, name, tile, first, size):
                self.seen.append((name, tile, first, size))
                n = self.used
                self.used += 1
                if not self.plan:
                    return n, SPH[n % NSPL][:, 0:size], SPL[n % NSPL][:, 0:size], None
                self.ready()
                return n, SPH[n % NSPL][:, 0:size], SPL[n % NSPL][:, 0:size], self.spl_tok[n]

            def done(self, n, tok):
                self.finished += 1
                self.spl_after[n % NSPL] = tok

        lo_engine = [pool]
        held = {}
        W = Weights(A["plan"])

        far = []
        side, spare, rate, due, later_ops, tick = [], [], [0, 0, 0], [0.0, 0.0], [], [0]

        def step(n=1):
            for _ in range(n):
                while side:
                    if next(side[0], True):
                        side.pop(0)
                        continue
                    break

        def flush():
            while side:
                step()

        def between():
            while later_ops and later_ops[0][0] <= tick[0]:
                later_ops.pop(0)[1]()
            tick[0] += 1
            step(rate[0])
            due[0] += rate[1]
            background(int(due[0]))
            due[0] -= int(due[0])
            due[1] += rate[2]
            while due[1] >= 1:
                due[1] -= 1
                if far:
                    far.pop(0)()

        def gemm(src, tile_no, kt, hi, lo, after, evac):
            b, free = main.take()
            k0 = 0
            while k0 < kt:
                kn = min(CHUNK, kt - k0)
                n, wh, wl, wt = W.take(src, tile_no, k0 * 128, kn * 128)
                for k in range(kn):
                    q, kk = slice(k * 128, (k + 1) * 128), k0 + k
                    mm(P_[b][:], wh[:, q], hi(kk), kk == 0, False, [wt, free, after(kk)[0]])
                    mm(P_[b][:], wl[:, q], hi(kk), False, False)
                    if k in (3, 7):
                        between()
                for k in range(kn):
                    q, kk = slice(k * 128, (k + 1) * 128), k0 + k
                    t = mm(P_[b][:], wh[:, q], lo(kk), False, kk == kt - 1, [after(kk)[1]], mark=(k == kn - 1))
                W.done(n, t)
                k0 += kn
                if k0 < kt:
                    between()
            held["bank"] = b
            freed = evac(P_[b], t)
            if freed is not None:
                main.give(b, freed)
            between()

        def small(src, unit, count, kt, hi, lo, after, evac):
            st = {}

            def tile(c):
                if c == 0:
                    st["unit"] = W.take(src, unit, 0, count * kt * 128)
                n, wh, wl, wt = st["unit"]
                b, free = main.take()
                for k in range(kt):
                    q = slice((c * kt + k) * 128, (c * kt + k + 1) * 128)
                    mm(P_[b][:], wh[:, q], hi(k), k == 0, False, [wt, free, after(k)[0]])
                    mm(P_[b][:], wl[:, q], hi(k), False, False)
                for k in range(kt):
                    q = slice((c * kt + k) * 128, (c * kt + k + 1) * 128)
                    t = mm(P_[b][:], wh[:, q], lo(k), False, k == kt - 1, [after(k)[1]], mark=(k == kt - 1))
                if c == count - 1:
                    W.done(n, t)
                main.give(b, evac(unit * count + c, P_[b], t))
                between()

            return [lambda c=c: tile(c) for c in range(count)]

        def gemms(jobs, hi, lo, after, together=2, hook=None, feed=None):
            group = []
            for src, tile_no, evac, then in jobs[:together]:
                b, free = main.take()
                n, wh, wl, wt = W.take(src, tile_no, 0, 1024)
                group.append((b, free, n, wh, wl, wt, evac, then))
            last = {}
            for k in range(9):
                if feed:
                    feed(k)
                for b, free, n, wh, wl, wt, _, _ in group:
                    if k < 8:
                        q = slice(k * 128, (k + 1) * 128)
                        mm(P_[b][:], wh[:, q], hi(k), k == 0, False, [wt, free, after(k)[0]])
                        mm(P_[b][:], wl[:, q], hi(k), False, False)
                    if k:
                        q = slice((k - 1) * 128, k * 128)
                        last[n] = mm(P_[b][:], wh[:, q], lo(k - 1), False, k == 8, [after(k - 1)[1]], mark=(k == 8))
                    if k == 8:
                        W.done(n, last[n])
            W.ready(dve)
            extra = []
            if hook:
                parts = hook()
                next(parts)
                src, tile_no, evac, then = jobs[together]

                def hold(bank, t):
                    extra.append((held["bank"], t))
                    return None

                gemm(src, tile_no, 8, hi, lo, after, hold)
                next(parts, None)
                group.append((extra[0][0], None, "x", None, None, None, evac, then))
                last["x"] = extra[0][1]
            for b, free, n, wh, wl, wt, evac, then in group:
                held["bank"] = b
                freed = evac(P_[b], last[n])
                if freed is not None:
                    main.give(b, freed)
                between()
                if then:
                    then()
            for src, tile_no, evac, then in jobs[together + len(extra):]:
                gemm(src, tile_no, 8, hi, lo, after, evac)
                if then:
                    then()

        def gemm_tok(src, block, kt, hi, lo, after, evac):
            banks = [main.take() for _ in range(T)]
            for k0 in range(0, kt, 2):
                n, wh, wl, wt = W.take(src, block, k0 * 512, 1024)
                for k in range(2):
                    kk = k0 + k
                    h, l = wh[:, k * 512:(k + 1) * 512], wl[:, k * 512:(k + 1) * 512]
                    for t in range(T):
                        b, free = banks[t]
                        q = slice(t * 128, (t + 1) * 128)
                        mm(P_[b][:], hi(kk)[:, q], h, kk == 0, False, [wt, after(kk), free])
                        mm(P_[b][:], hi(kk)[:, q], l, False, False)
                        tok = mm(P_[b][:], lo(kk)[:, q], h, False, kk == kt - 1, mark=True)
                    if k == 0:
                        between()
                W.done(n, tok)
                if k0 + 2 < kt:
                    between()
            for t in range(T):
                main.give(banks[t][0], evac(t, P_[banks[t][0]], tok))
            between()

        small_at = [0]

        def scratch(n):
            if small_at[0] + n > 256:
                small_at[0] = 0
            a = small_at[0]
            small_at[0] += n
            return SM[:, a:a + n]

        kept = [0]

        def keepc(n):
            kept[0] += n
            assert kept[0] <= 176
            return KEEP[:, kept[0] - n:kept[0]]

        def rsqrt_cols(src, n, scale, after):
            v, q, r = scratch(n), scratch(n), scratch(n)
            t = ts(v, src, scale, EPS, ALU.mult, ALU.add, after)
            t = ac(q, v, ACT.Sqrt, t)
            return r, recip(r, q, t)

        class SumSq:

            def __init__(self):
                (self.a, self.free), self.t = tmp.take(), None

            def add(self, x, after, scale=1.0, eng=None):
                if self.t is None:
                    self.t = r = ac(TMP[self.a][:], x, ACT.Square, [after, self.free], scale=scale)
                else:
                    i, free = tmp.take()
                    r = ac(TMP[i][:], x, ACT.Square, [after, free], scale=scale)
                    self.t = tt(TMP[self.a][:], TMP[self.a][:], TMP[i][:], ALU.add, [r, self.t], eng=eng)
                    tmp.give(i, [self.t])
                return r

            def merge(self, other):
                self.t = tt(TMP[self.a][:], TMP[self.a][:], TMP[other.a][:], ALU.add, [self.t, other.t])
                tmp.give(other.a, [self.t])

            def columns(self):
                b, bank, free = mbank()
                for t in range(T):
                    tok = mm(bank[:, t:t + 1], TMP[self.a][:, t * 128:(t + 1) * 128], ONES[:, 0:1], True, True,
                             [self.t, free, ones], mark=(t == T - 1))
                tmp.give(self.a, [tok])
                return bank[:, 0:T], tok, b

        def spread(r, after):
            i, free = tmp.take()
            b, bank, bfree = mbank()
            for t in range(T):
                q = slice(t * 128, (t + 1) * 128)
                d = ts(TMP[i][:, q], IDENT, r[:, t:t + 1], None, ALU.mult, after=[after, free, cst])
                tok = mm(bank[:, q], ONES[:], TMP[i][:, q], True, True, [d, bfree], mark=(t == T - 1))
            tmp.give(i, [tok])
            return b, bank, tok

        def rows_of(ss, width):
            c, t, b = ss.columns()
            r, t = rsqrt_cols(c, T, 1.0 / width, t)
            mgive(b, [t])
            return spread(r, t)

        def cut(x, hi, lo, after, shift=None, scale=None, eng=None):
            if shift is not None:
                a = ac(hi, x, ACT.Identity, after, bias=shift)
                return [a, stt(lo, x, shift, hi.bitcast(F32), ALU.add, ALU.subtract, [a, after])]
            if scale is not None:
                a = ac(hi, x, ACT.Copy, after, scale=scale)
                return [a, stt(lo, x, scale, hi.bitcast(F32), ALU.mult, ALU.subtract, [a, after])]
            a = ac(hi, x, ACT.Copy, after)
            return [a, tt(lo, x, hi.bitcast(F32), ALU.subtract, [a, after], eng=eng)]

        def in_turn(n, first, second):
            for i in range(n + 1):
                if i < n:
                    first(i)
                if i:
                    second(i - 1)

        def normed(x, n, scale, rows, after, hi, lo, shift=None):
            b, bank, rt = rows
            out_ = [[None, None] for _ in range(n)]
            js = [None] * n
            last = [None]

            def first(i):
                js[i], free = tmp.take()
                y = TMP[js[i]][:]
                t = last[0] = stt(y, x(i), scale(i), bank[:], ALU.mult, ALU.mult, [rt, after, free])
                if shift is None:
                    out_[i][0] = ac(hi(i), y, ACT.Copy, [t, after])
                    return
                out_[i][0] = ac(hi(i), y, ACT.Identity, [t, after], bias=shift(i))
                if i % 2:
                    out_[i][1] = ac(y, y, ACT.Identity, [t], bias=shift(i))

            def second(i):
                y, (a, full) = TMP[js[i]][:], out_[i]
                h = hi(i).bitcast(F32)
                if i % 2:
                    out_[i][1] = tt(lo(i), y, h, ALU.subtract, [a, full, last[0], after], eng=pool)
                elif shift is None:
                    out_[i][1] = tt(lo(i), y, h, ALU.subtract, [a, after])
                else:
                    out_[i][1] = stt(lo(i), y, shift(i), h, ALU.add, ALU.subtract, [a, after])
                tmp.give(js[i], out_[i])

            in_turn(n, first, second)
            mgive(b, [last[0]])
            return out_

        cst = once("l_c", C_[:], A["consts"])
        vecs = once("l_v", V_[:], A["vecs"])
        xts = [once(f"l_x{z}", XT[:, 2 * z:2 * z + 2, :], A["xT"][:, 2 * z:2 * z + 2, :]) for z in range(4)]
        xt = xts
        ada_src = A["w_ada"]
        order = [0, 4, 1, 5, 2, 6, 3, 7] + list(range(8, 24))
        place = {ch: n for n, ch in enumerate(order)}
        ada_tok = {}

        def ada_load(n, after=None):
            ada_tok[order[n]] = loads.load(s_ada[n % 6], ADA[n % 6][:], ada_src[order[n]], after)

        for n in range(6):
            ada_load(n)
        if A["plan"]:
            W.start()
        ones = setv(ONES[:], 1.0)
        zpad = [setv(CP[:, :, 0:30], 0.0), setv(XP[:, :, 0:3], 0.0)]

        csil = keepc(8)
        cs = ac(csil, V_[:, VEC["c"]:VEC["c"] + 8], ACT.Silu, vecs)
        ss, other = SumSq(), SumSq()
        for i in range(8):
            if i % 2:
                other.add(XT[:, i, :], xts[i // 2], eng=pool)
            else:
                ss.add(XT[:, i, :], xts[i // 2])
        ss.merge(other)
        rows = rows_of(ss, D)

        mod_a, mod_b, mod_c = mbank(), mbank(), mbank()
        ada_held = {}

        def ada(chunks):
            accs, toks_ = [], []

            def part(k, z, ch):
                if k == 0:
                    i, free = tmp.take()
                    accs.append((i, TMP[i][:, 0:256]))
                    toks_.append([cs, ada_tok[ch], free])
                acc, wt = accs[z][1], ADA[place[ch] % 6]
                if k == 0:
                    toks_[z] = ts(acc, wt[:, 0, :], csil[:, 0:1], None, ALU.mult, after=toks_[z])
                else:
                    toks_[z] = stt(acc, wt[:, k, :], csil[:, k:k + 1], acc, ALU.mult, ALU.add, toks_[z])
                if k == 7:
                    if place[ch] + 6 < 24:
                        ada_load(place[ch] + 6, toks_[z])
                    ada_held[ch] = (accs[z][0], accs[z][1], toks_[z])

            return [lambda k=k, z=z, ch=ch: part(k, z, ch) for k in range(8) for z, ch in enumerate(chunks)]

        def ada_columns(ch):
            i, acc, t = ada_held.pop(ch)
            _, bank, bfree = mod_b
            for j in range(2):
                c = 2 * ch + j - 16
                m = mm(bank[:, c:c + 1], acc[:, j * 128:(j + 1) * 128], ONES[:, 0:1], True, True,
                       [t, ones, bfree], mark=(j == 1))
            tmp.give(i, [m])
            return m

        XN = CO
        xn = []
        gmix = keepc(8)
        h_tok = []
        turns = [mod_a[1], mod_c[1]]
        turn_free = [mod_a[2], mod_c[2]]
        def mod_sums(p_):
            chs, accs, d = (p_, p_ + 4), [], []
            for ch in chs:
                ai, afree = tmp.take()
                accs.append((ai, TMP[ai][:, 0:256]))
                d.append(afree)
            more = []
            for ch in chs:
                wt = ADA[place[ch] % 6]
                ai, afree = tmp.take()
                x6, x7 = TMP[ai][:, 0:256], TMP[ai][:, 256:512]
                x5 = TMP[accs[len(more)][0]][:, 256:512]
                u = ac(x6, wt[:, 6, :], ACT.Copy, [cs, ada_tok[ch], afree], scale=csil[:, 6:7])
                v = ac(x7, wt[:, 7, :], ACT.Copy, [cs, ada_tok[ch]], scale=csil[:, 7:8])
                w = ac(x5, wt[:, 5, :], ACT.Copy, [d[len(more)]], scale=csil[:, 5:6])
                u = tt(x6, x6, x7, ALU.add, [u, v], eng=pool)
                more.append((ai, tt(x6, x6, x5, ALU.add, [u, w], eng=pool)))
            for k in range(5):
                for z, ch in enumerate(chs):
                    acc, wt = accs[z][1], ADA[place[ch] % 6]
                    if k == 0:
                        d[z] = ts(acc, wt[:, 0, :], csil[:, 0:1], None, ALU.mult, after=[cs, ada_tok[ch], d[z]])
                    else:
                        d[z] = stt(acc, wt[:, k, :], csil[:, k:k + 1], acc, ALU.mult, ALU.add, d[z])
            mbk = turns[p_ % 2]
            for z, ch in enumerate(chs):
                acc = accs[z][1]
                ai, mt = more[z]
                d[z] = tt(acc, acc, TMP[ai][:, 0:256], ALU.add, [d[z], mt])
                tmp.give(ai, [d[z]])
                for j in range(2):
                    c, q = 2 * ch + j, slice(j * 128, (j + 1) * 128)
                    m = mm(mbk[:, c:c + 1], acc[:, q], ONES[:, 0:1], True, True,
                           [d[z], ones, turn_free[p_ % 2]], mark=(j == 1))
                tmp.give(accs[z][0], [m])
                ada_load(place[ch] + 6, [m, d[z]])
            return m

        def mod_tiles(p_, m):
            mbk = turns[p_ % 2]
            p2 = slice(2 * p_, 2 * p_ + 2)
            p8 = slice(8 + 2 * p_, 10 + 2 * p_)

            def two(x, first):
                return x[:, first:first + 16].rearrange("p (a b) -> p a b", a=2)[:, :, p2]

            t0 = tt(two(MOD, 0), two(mbk, 0), two(V_, VEC["b_ada"]), ALU.add, [m, vecs])
            t1 = t0
            turn_free[p_ % 2] = [t0, t1]
            t1 = stt(gmix[:, p2], MOD[:, p8], 1.0, V_[:, VEC["g_mix"] + 2 * p_:VEC["g_mix"] + 2 * p_ + 2],
                     ALU.add, ALU.mult, [t1])
            two_, full = (2 * p_, 2 * p_ + 1), []
            for i in two_:
                full.append(ts(XN[:, i, :], XN[:, i, :], gmix[:, i:i + 1], MOD[:, i:i + 1], ALU.mult, ALU.add,
                               after=[t0, t1, xn[i]]))
            for i in two_:
                c = full[i % 2]
                a = ac(HH[:, i, :], XN[:, i, :], ACT.Copy, [c])
                h_tok.append([a, tt(HL[:, i, :], XN[:, i, :], HH[:, i, :].bitcast(F32), ALU.subtract, [a, c],
                                    eng=pool if i % 2 == 0 else None)])

        sums = {}

        sums[0] = mod_sums(0)
        b, bank, rt = rows
        for i in range(8):
            xn.append(tt(XN[:, i, :], XT[:, i, :], bank[:], ALU.mult, [rt, xt]))
        mgive(b, [xn[7]])
        sums[1] = mod_sums(1)
        if A["plan"]:
            W.load()


        def mod_feed(k):
            if k == 0:
                mod_tiles(0, sums[0])
            if k in (2, 4):
                sums[k // 2 + 1] = mod_sums(k // 2 + 1)
            if k in (2, 4, 6):
                mod_tiles(k // 2, sums[k // 2])
            if k == 6:
                W.ahead = NSPL
                mgive(mod_a[0], turn_free[0])
                mgive(mod_c[0], turn_free[1])

        hi, lo = (lambda k: HH[:, k, :]), (lambda k: HL[:, k, :])

        conv_ready = {}
        conv_tok = [None] * 8

        def tap_far(j, i=7):
            src = CP[:, i, j:j + 512]
            w = V_[:, VEC["dw_w"] + i * 31 + j:VEC["dw_w"] + i * 31 + j + 1]
            if j == 0:
                conv_tok[i] = ts(CO[:, i, :], src, w, vec("dw_b", i), ALU.mult, ALU.add, [conv_ready[i], zpad[0]],
                                 eng=pool)
            else:
                t = ts(RROW[:], src, w, None, ALU.mult, after=conv_tok[i], eng=pool)
                conv_tok[i] = tt(CO[:, i, :], CO[:, i, :], RROW[:], ALU.add, [t, conv_tok[i]], eng=pool)

        conv_total = {}

        def conv_sum(i):
            if i == 1:
                conv_total["j"], free = tmp.take()
                a = TMP[conv_total["j"]][:]
                conv_total["t"] = tt(a, CO[:, 0, :], CO[:, 1, :], ALU.add, [conv_tok[0], conv_tok[1], free])
                return
            a = TMP[conv_total["j"]][:]
            for z in (i - 1, i):
                conv_total["t"] = tt(a, a, CO[:, z, :], ALU.add, [conv_total["t"], conv_tok[z]])

        def tap(i, j):
            src = CP[:, i, j:j + 512]
            w = V_[:, VEC["dw_w"] + i * 31 + j:VEC["dw_w"] + i * 31 + j + 1]
            if j == 0:
                conv_tok[i] = ts(CO[:, i, :], src, w, vec("dw_b", i), ALU.mult, ALU.add, [conv_ready[i], zpad[0]])
            else:
                conv_tok[i] = stt(CO[:, i, :], src, w, CO[:, i, :], ALU.mult, ALU.add, conv_tok[i])

        def background(n):
            for _ in range(min(n, len(spare))):
                spare.pop(0)()

        W_IN = "w_in"
        def glu(i):
            pending = {}

            def keep(bank, t):
                pending["v"] = (held["bank"], t)
                return None

            def evac(bank, t):
                j, free = tmp.take()
                a = ac(TMP[j][:], bank[:], ACT.Sigmoid, [t, free, vecs], bias=vec("b_glu", 8 + i))
                v, vt = pending["v"]
                c = stt(CP[:, i, 30:542], P_[v][:], vec("b_glu", i), TMP[j][:], ALU.add, ALU.mult, [a, vt])
                tmp.give(j, [c])
                main.give(v, [c])
                conv_ready[i] = c
                return [a]

            def then():
                if i % 2:
                    taps.extend(sums_)
                    sums_.clear()
                    if i < 7:
                        sums_.append(lambda: conv_sum(i))
                    taps.extend([lambda z=z, j=j: tap(i - 1 + z, j) for j in range(31) for z in range(2) if i - 1 + z < 7])

            return [(W_IN, i, keep, None), (W_IN, 8 + i, evac, then)]

        taps, sums_ = [], []
        waiting = []
        for ch in range(8, 24, 2):
            parts = ada([ch, ch + 1])
            spare.extend(parts[:6] + waiting + parts[6:])
            waiting = [lambda ch=ch: (ada_columns(ch), ada_columns(ch + 1))]
        rate[:] = [0, 3, 0]
        gemms([job for i in range(8) for job in glu(i)], hi, lo, by_tile(h_tok), feed=mod_feed)
        background(1000)
        spare.extend(taps)
        far.extend([lambda j=j: tap_far(j) for j in range(31)])

        modb = []

        def last_columns():
            yield
            m = [ada_columns(22), ada_columns(23)]
            modb.append(tt(MOD[:, 16:48], mod_b[1][:, 0:32], V_[:, VEC["b_ada"] + 16:VEC["b_ada"] + 48], ALU.add,
                           [m, vecs]))
            mgive(mod_b[0], [modb[0]])

        side.append(last_columns())
        rate[:] = [1, 3.5, 0.3]
        f = fence()
        vb_tok = once("l_vb", VB[:], A["b_v"].broadcast_to([128, 1024]), f)
        sel_tok = once("l_sel", SEL[:], A["sel"], f)
        von = setv(VT[:, :, :, 256:257], 1.0, f)
        v_tok = []
        for blk in range(2):
            def evac(t, bank, tok):
                dst = VT[:, t, 2 * blk:2 * blk + 2, 0:256]
                c = tt(dst, bank[:].rearrange("p (a b) -> p a b", a=2),
                       VB[:, blk * 512:(blk + 1) * 512].rearrange("p (a b) -> p a b", a=2), ALU.add,
                       [tok, vb_tok, f])
                v_tok.append(c)
                return [c]
            gemm_tok("w_v", blk, 8, hi, lo, done_already, evac)
        IR, LF, BR, CR = ROWS

        def gates(bank, t):
            p = slice(32, 36)
            j, free = tmp.take()
            z = TMP[j]
            a0 = ac(IR[:], bank[0:4, :], ACT.Identity, [t, f], bias=vec("b_if", 0, slice(0, 4)))
            a1 = ac(z[p, :], bank[p, :], ACT.Identity, [free], bias=vec("b_if", 0, p))
            k, free2 = tmp.take()
            y = TMP[k]
            a2 = ac(y[p, :], z[p, :], ACT.Abs, [a1, free2])
            a3 = ac(y[p, :], y[p, :], ACT.Exp, a2, scale=-1.0)
            a4 = ac(y[p, :], y[p, :], ACT.Ln, a3, bias=1.0)
            c = stt(LF[:], z[p, :], 0.0, y[p, :], ALU.min, ALU.subtract, [a4, a1, f])
            tmp.give(j, [c])
            tmp.give(k, [c])
            held["g"] = [a0, c]
            return [a0, a1]

        gemm("w_if", 0, 8, hi, lo, done_already, gates)
        CB, GD, mus, pair = keepc(40), keepc(16), keepc(8), {}

        def decays():
            g = held["g"]
            k1, freek = tmp.take()
            onerow = TMP[k1][0:4, 0:128]
            t1 = setv(onerow, 1.0, freek)
            mu0 = setv(mus[0:4, 0:1], 0.0, fence())
            ct = [g, t1, mu0]
            for t in range(T):
                q = slice(t * 128, (t + 1) * 128)
                e = slice((t + 1) * 128 - 1, (t + 1) * 128)
                b_ = scan(BR[:, q], onerow, LF[:, q], 0.0, ALU.mult, ALU.add, ct)
                c_ = tt(CR[:, q], IR[:, q], BR[:, q], ALU.subtract, [b_, g])
                m_ = scan(MROW[:, q], CR[:, q], CR[:, q], mus[0:4, t:t + 1], ALU.max, ALU.max, [c_, mu0])
                ct = [tt(mus[0:4, t + 1:t + 2], MROW[:, e], BR[:, e], ALU.add, [m_, b_])]
                yield
            tmp.give(k1, [ct[0]])
            n = 0
            for k in range(T):
                kq = slice(k * 128, (k + 1) * 128)
                for t in range(k, T):
                    pair[(k, t)] = n
                    if t == k:
                        z = cp(ROWC[:, n, :], CR[:, kq], ct)
                    else:
                        z = ts(ROWC[:, n, :], ROWC[:, n - 1, :], BR[:, t * 128 - 1:t * 128], None, ALU.add, after=z)
                    n += 1
            mr = tt(IR[:], MROW[:], BR[:], ALU.add, [z])
            for _ in range(6):
                yield
            b, bank, free = mbank()
            for i in range(10):
                tk = tr(bank[:, 4 * i:4 * i + 4], ROWC[:, i, :], IDENT[0:4, 0:4], [z, free, cst])
            for t in range(T):
                tk = tr(bank[:, 40 + 4 * t:44 + 4 * t], IR[:, t * 128:(t + 1) * 128], IDENT[0:4, 0:4], [mr], mark=(t == 3))
            cb = cp(CB, bank[:, 0:40], tk)
            gd = ac(GD, bank[:, 40:56], ACT.Exp, [tk, cb], scale=-1.0)
            mgive(b, [cb, gd])
            held.update(ct=ct, cb=cb, gd=gd, rows=tk)

        side.append(decays())

        f = fence()
        hm_tok = [None] * 8
        xp_free = [zpad[1], zpad[1]]

        def qk_tile(tile_no, dst, w_at, b_at, after):
            def evac(bank, t):
                s = (tile_no) % 2
                a = ac(XP[:, s, 3:515], bank[:], ACT.Identity, [t, xp_free[s]], bias=vec("b_qk", b_at))
                j, free = tmp.take()
                w = lambda tap_: V_[:, VEC["qk_w"] + 4 * b_at + tap_:VEC["qk_w"] + 4 * b_at + tap_ + 1]
                c = ac(TMP[j][:], XP[:, s, 0:512], ACT.Identity, [a, free], bias=vec("qk_b", b_at), scale=w(0))
                for z_ in range(1, 4):
                    c = stt(TMP[j][:], XP[:, s, z_:z_ + 512], w(z_), TMP[j][:], ALU.mult, ALU.add, c)
                xp_free[s] = c
                qk_ = held["qk"]

                def silu():
                    r = ac(dst, TMP[j][:], ACT.Silu, [c, after])
                    tmp.give(j, [r])
                    qk_.append(r)
                later_ops.append((tick[0] + 1, silu))
                return [a]
            return evac

        qk_used = [f, f]
        sc_used = [f]

        def attend(h, qk_done):
            while len(qk_done) < 4:
                yield
            yield
            yield
            s = (h + 1) % 2
            ct, cb, gd = held["ct"], held["cb"], held["gd"]
            ht_used = held.get("ht")
            mb, mbk, free = mbank()
            mt = mm(mbk[:], SEL[:, h, :], MROW[:], True, True, [ct, sel_tok, free], mark=True)
            jm, freem = tmp.take()
            mrows = TMP[jm]
            mt = ac(mrows[:], mbk[:], ACT.Copy, [mt, freem])
            mgive(mb, [mt])
            yield
            off = 0
            sct = []
            offs = {}
            for k in range(T):
                wdt = (T - k) * 128
                b_, bk, free = mbank()
                for d_ in range(2):
                    st = mm(bk[:, 0:wdt], QK[:, s, 2 + d_, k * 128:(k + 1) * 128], QK[:, s, d_, k * 128:512],
                            d_ == 0, d_ == 1, [qk_done, free], mark=(d_ == 1))
                j, freej = tmp.take()
                dm = TMP[j]
                a0 = tt(dm[:, 0:128], mrows[:, k * 128:(k + 1) * 128], MBIG, ALU.add, [mt, freej, cst])
                last = []
                for t in range(k, T):
                    col = CB[:, 4 * pair[(k, t)] + h:4 * pair[(k, t)] + h + 1]
                    src = dm[:, 0:128] if t == k else mrows[:, t * 128:(t + 1) * 128]
                    e_ = ac(dm[:, (t - k) * 128:(t - k + 1) * 128], src, ACT.Exp, [a0, mt, cb, freej], bias=col, scale=-1.0)
                x_ = stt(SC[:, off:off + wdt], bk[:, 0:wdt], 0.0625, dm[:, 0:wdt], ALU.mult, ALU.mult,
                         [st, e_, sc_used[0]])
                tmp.give(j, [x_])
                mgive(b_, [x_])
                offs[k] = off
                off += wdt
                sct.append(x_)
                yield
            tmp.give(jm, [e_, a0])
            qk_used[s] = [st]
            held["scored"] = h + 1
            ht = []
            for t in range(T):
                b_, bk, free = mbank()
                for k in range(t + 1):
                    c0 = offs[k] + (t - k) * 128
                    pt = mm(bk[:, 0:257], SC[:, c0:c0 + 128], VT[:, k, h, :], k == 0, k == t,
                            [sct[k], v_tok, von, free], mark=(k == t))
                a_ = ac(HT[:, t, 0:257], bk[:, 0:257], ACT.Copy, [pt, ht_used])
                mgive(b_, [a_])
                ht.append(a_)
                yield
            sc_used[0] = pt
            st6, ag = scratch(24), scratch(8)
            for t in range(T):
                z_ = bstat(st6[:, 6 * t:6 * t + 6], HT[:, t, 0:256], ht[t])
            for t in range(T):
                z_ = baggr(ag[:, 2 * t:2 * t + 2], st6[:, 6 * t:6 * t + 6], z_)
            agv = ag.rearrange("p (t two) -> p t two", two=2)
            den, r_, v_, w_, u_ = scratch(4), scratch(4), scratch(4), scratch(4), scratch(4)
            gcol = GD.rearrange("p (t h) -> p t h", h=4)[:, :, h]
            d1 = stt(den, HT[:, :, 256], -1.0, HT[:, :, 256], ALU.mult, ALU.max, [ht])
            d1 = tt(den, den, gcol, ALU.max, [d1, gd])
            d2 = recip(r_, den, d1)
            d3 = tt(v_, r_, r_, ALU.mult, d2)
            d4 = tt(w_, v_, agv[:, :, 1], ALU.mult, [d3, z_])
            rr, d5 = rsqrt_cols(w_, 4, 1.0, d4)
            d6 = tt(u_, r_, rr, ALU.mult, [d5, d2])
            for t in range(T):
                d7 = ts(HT[:, t, 0:256], HT[:, t, 0:256], agv[:, t, 0:1], u_[:, t:t + 1], ALU.subtract, ALU.mult,
                        after=[d6, z_])
            for _ in range(5):
                yield
            for d_ in range(2):
                b_, bk, free = mbank()
                for t in range(T):
                    tk_ = tr(bk[:, t * 128:(t + 1) * 128], HT[:, t, d_ * 128:(d_ + 1) * 128], IDENT, [d7, free],
                             mark=(t == 3))
                i_ = 2 * h + d_
                hm_tok[i_] = ac(HM[:, i_, :], bk[:], ACT.Copy, [tk_, f], scale=vec("ml_g", i_))
                mgive(b_, [hm_tok[i_]])
                held["ht"] = tk_

        rate[:] = [1, 1.35, 0.3]
        for h in range(4):
            held["qk"] = []
            while h >= 2 and held.get("scored", 0) < h - 1:
                step()
            for z_ in range(4):
                i = 2 * h + z_ % 2 + (8 if z_ >= 2 else 0)
                used_ = [qk_used[(h + 1) % 2], held.get("rows") if h == 1 else None]
                gemm(W_IN, 16 + i, 8, hi, lo, done_already, qk_tile(z_, QK[:, (h + 1) % 2, z_, :], 0, i, used_))
            side.append(attend(h, held["qk"]))

        z_tok = [None] * 8

        def gate_mul(bname, boff):
            def make(i):
                def evac(bank, t):
                    j, free = tmp.take()
                    a = ac(TMP[j][:], bank[:], ACT.Sigmoid, [t, free], bias=vec(bname, boff + i))
                    c = tt(HM[:, i, :], HM[:, i, :], TMP[j][:], ALU.mult, [a, hm_tok[i]])
                    hm_tok[i] = c
                    tmp.give(j, [c])
                    return [a]
                return evac
            return make

        mko, mkm = gate_mul("b_o", 0), gate_mul("b_mg", 8)
        rate[:] = [1, 1.6, 0.3]
        for n, (first, i) in enumerate([(32, i) for i in range(6)] + [(48, i) for i in range(6)] +
                                       [(32, 6), (32, 7), (48, 6), (48, 7)]):
            if n == 8:
                rate[1] = 2.1
            while hm_tok[i] is None:
                step()
            gemm(W_IN, first + i, 8, hi, lo, done_already, (mko if first == 32 else mkm)(i))
        background(1000)
        while far:
            far.pop(0)()
        f = fence()
        gc_tok = [None] * 8

        conv_sum(7)
        j0, t = conv_total["j"], conv_total["t"]

        def gc_evac(i):
            def evac(bank, t_):
                gc_tok[i] = ac(GC[:, i, :], bank[:], ACT.Sigmoid, [t_, f], bias=vec("b_mg", i))
                return [gc_tok[i]]
            return evac

        def layer_norm(t):
            for _ in range(3):
                yield
            b, bank, free = mbank()
            mt = mm(bank[:], ONES[:], TMP[j0][:], True, True, [t, free], mark=True)
            i1, free1 = tmp.take()
            mean = ac(TMP[i1][:], bank[:], ACT.Copy, [mt, free1], scale=1.0 / D)
            mgive(b, [mean])
            tmp.give(j0, [mt])
            ss = SumSq()
            for z in range(8):
                c = tt(CO[:, z, :], CO[:, z, :], TMP[i1][:], ALU.subtract, [mean])
                conv_tok[z] = c
                ss.add(CO[:, z, :], c)
            tmp.give(i1, [c])
            for _ in range(7):
                yield
            c, ct_, b = ss.columns()
            r, ct_ = rsqrt_cols(c, T, 1.0 / D, ct_)
            mgive(b, [ct_])
            yield
            yield
            b, bank, rt = spread(r, ct_)
            for z in range(8):
                c = tt(CO[:, z, :], CO[:, z, :], bank[:], ALU.mult, [rt, conv_tok[z]])
                s_ = ac(CO[:, z, :], CO[:, z, :], ACT.Silu, c, bias=vec("ln_b", z), scale=vec("ln_g", z))
                a_tok.append(cut(CO[:, z, :], AH[:, z, :], AL[:, z, :], [s_, f], eng=pool))
                if z % 3 == 3 - 1:
                    yield
            mgive(b, [c])

        a_tok = []
        rate[:] = [1, 0, 0]
        lo_engine[0] = dve
        side.append(layer_norm(t))
        for i in range(8):
            gemm(W_IN, 40 + i, 8, hi, lo, done_already, gc_evac(i))
        flush()
        f = fence()
        z_tok, jobs = [], []
        for i in range(8):
            def evac(bank, t_, i=i):
                j, free = tmp.take()
                a = stt(TMP[j][:], bank[:], vec("b_pw", i), GC[:, i, :], ALU.add, ALU.mult, [t_, gc_tok[i], free])
                c = tt(TMP[j][:], TMP[j][:], HM[:, i, :], ALU.add, [a, hm_tok[i]])
                z_ = cut(TMP[j][:], HH[:, i, :], HL[:, i, :], [c, f])
                tmp.give(j, z_)
                z_tok.append(z_)
                return [a]
            jobs.append(("w_pw", i, evac, None))
        gemms(jobs, lambda k: AH[:, k, :], lambda k: AL[:, k, :], by_tile(a_tok))

        x_tok = [xt] * 8

        rate[:] = [0, 0, 0]
        lo_engine[0] = dve
        ss = SumSq()

        def out_evac(i):
            def evac(bank, t_):
                x_tok[i] = stt(XT[:, i, :], bank[:], MOD[:, 16 + i:17 + i], XT[:, i, :], ALU.mult, ALU.add,
                               [t_, x_tok[i], modb])
                ss.add(XT[:, i, :], x_tok[i])
                return [x_tok[i]]
            return evac

        gemms([("w_out", i, out_evac(i), None) for i in range(8)], hi, lo, by_tile(z_tok), 0)

        gffn = keepc(8)
        gf = stt(gffn, MOD[:, 32:40], 1.0, V_[:, VEC["g_ffn"]:VEC["g_ffn"] + 8], ALU.add, ALU.mult, [modb])
        gg = keepc(8)
        ggt = tt(gg, V_[:, VEC["g_fin"]:VEC["g_fin"] + 8], V_[:, VEC["g_pre"]:VEC["g_pre"] + 8], ALU.mult, vecs)

        def ffn_up(tiles, h_tok, f, rows=None, hook=None):
            mid, jobs = [], []

            def part(i):
                pend = {}

                def keep(bank, t):
                    j, free = tmp.take()
                    if rows is None:
                        pend["a"] = ac(TMP[j][:], bank[:], ACT.Silu, [t, free])
                        freed = pend["a"]
                    else:
                        freed = tt(TMP[j][:], bank[:], RROW[:], ALU.mult, [t, free, rows[0]])
                        pend["a"] = ac(TMP[j][:], TMP[j][:], ACT.Silu, freed)
                    pend["j"] = j
                    return [freed]

                def evac(bank, t):
                    j = pend["j"]
                    b = c = tt(TMP[j][:], TMP[j][:], bank[:], ALU.mult, [t, pend["a"]])
                    if rows is not None:
                        c = tt(TMP[j][:], TMP[j][:], RROW[:], ALU.mult, c)
                    z_ = cut(TMP[j][:], MH[:, i, :], ML[:, i, :], [c, f], eng=pool if rows is not None else None)
                    tmp.give(j, z_)
                    mid.append(z_)
                    return [b]

                return [(*tiles(i, 0), keep, None), (*tiles(i, 1), evac, None)]

            for i in range(NFT):
                jobs += part(i)
            gemms(jobs, hi, lo, by_tile(h_tok), hook=hook)
            return mid

        f = fence()
        rows = rows_of(ss, D)
        h_tok = normed(lambda i: XT[:, i, :], 8, lambda i: gffn[:, i:i + 1], rows, [x_tok, gf],
                       hi, lo, lambda i: MOD[:, 24 + i:25 + i])
        mid = ffn_up(lambda i, z: ("w_up1", i + z * NFT), h_tok, f)

        trig = []

        def rotary():
            j, free = tmp.take()
            posi = TMP[j][:].bitcast(I32)
            pt = once("l_pos", posi, A["pos"].broadcast_to([128, S]), free)
            k, free2 = tmp.take()
            yield
            pf = cp(TMP[k][:], posi, [pt, free2])
            kk = TMP[j][:]
            u = pf
            f = fence()
            for z, (inv, sg) in enumerate((("invr", "sgr"), ("invm", "sgm"))):
                ang = TRIG[:, 2 * z, :]
                t = ts(ang, TMP[k][:], const(inv), None, ALU.mult, after=[pf, f, cst])
                for m in (2048.0, 1.0):
                    u = ts(kk, ang, 1.0 / (m * 2 * np.pi), MAGIC, ALU.mult, ALU.add, [t, u])
                    u = ts(kk, kk, MAGIC, None, ALU.subtract, after=u)
                    yield
                    for cc in (TWO_PI_1, TWO_PI_2, TWO_PI_3):
                        t = stt(ang, kk, -cc * m, ang, ALU.mult, ALU.add, [u, t])
                    u = t
                    yield
                yield
                sn = TRIG[:, 2 * z + 1, :]
                t = ts(ang, ang, PI_IN, -PI_IN, ALU.min, ALU.max, t)
                s_ = ac(sn, ang, ACT.Sin, [t, f])
                s_ = ac(sn, sn, ACT.Copy, s_, scale=const(sg))
                yield
                u = ts(ang, ang, float(np.pi / 2), None, ALU.add, after=[t, s_])
                t = ts(kk, ang, float(np.pi), -2 * float(np.pi), ALU.is_gt, ALU.mult, u)
                u = t = tt(ang, ang, kk, ALU.add, t)
                yield
                t = ts(ang, ang, PI_IN, -PI_IN, ALU.min, ALU.max, t)
                trig.extend([s_, ac(ang, ang, ACT.Sin, t)])
                yield
            tmp.give(j, [u])
            tmp.give(k, [u])

        COSR, SINR, COSM, SINM = (TRIG[:, z, :] for z in range(4))

        f = fence()
        ss1, ss2 = SumSq(), SumSq()
        h_tok = []

        def down_evac(i):
            def evac(bank, t_):
                x_tok[i] = stt(XT[:, i, :], bank[:], MOD[:, 40 + i:41 + i], XT[:, i, :], ALU.mult, ALU.add,
                               [t_, x_tok[i], modb])
                e = pool if i < 7 else None
                a = ac(HH[:, i, :], XT[:, i, :], ACT.Copy, [x_tok[i], ggt, f], scale=gg[:, i:i + 1])
                ss1.add(XT[:, i, :], x_tok[i], eng=e)
                ss2.add(XT[:, i, :], x_tok[i], scale=vec("g_fin", i), eng=e)
                h_tok.append([a, stt(HL[:, i, :], XT[:, i, :], gg[:, i:i + 1], HH[:, i, :].bitcast(F32), ALU.mult,
                                     ALU.subtract, [a, f])])
                return [x_tok[i]]
            return evac

        side.append(rotary())
        rate[0] = 1
        for i in range(8):
            gemm("w_down1", i, NFT, lambda k: MH[:, k, :], lambda k: ML[:, k, :], by_tile(mid), down_evac(i))
        flush()
        rate[0] = 1
        RCOL = keepc(4)
        rrow = [None]

        def final_rows():
            c1, t1, b1 = ss1.columns()
            c2, t2, b2 = ss2.columns()
            r1, t1 = rsqrt_cols(c1, T, 1.0 / D, t1)
            mgive(b1, [t1])
            v = scratch(4)
            t = tt(v, r1, r1, ALU.mult, t1)
            v2 = scratch(4)
            t = tt(v2, v, c2, ALU.mult, [t, t2])
            mgive(b2, [t])
            r2, t = rsqrt_cols(v2, T, 1.0 / D, t)
            t = tt(RCOL, r1, r2, ALU.mult, t)
            yield
            yield
            b, bank, rt = spread(RCOL, t)
            rrow[0] = [cp(RROW[:], bank[:], rt), t]
            mgive(b, [rrow[0][0]])
            s_ = tt(SINR, SINR, RROW[:], ALU.mult, [rrow[0], trig])
            trig.extend([s_, tt(COSR, COSR, RROW[:], ALU.mult, [rrow[0], trig])])
            yield
            b, bank, rt = spread(r1, t1)
            for i in range(8):
                x_tok[i] = stt(XT[:, i, :], XT[:, i, :], vec("g_fin", i), bank[:], ALU.mult, ALU.mult,
                               [x_tok[i], h_tok, rt])
                if i == 7:
                    mgive(b, [x_tok[7]])
                yield

        W2 = "w_in2"
        f = fence()
        s_rd = [sem("s_rd0"), sem("s_rd1")]
        rd_tok = [loads.load(s_rd[h], RD[:, h, :], A["ret_decay"][:, h, :], f) for h in range(2)]
        rv_tok, cq_tok, ckv_tok, rq_tok, rk_tok = [], [], [], [], []

        def evac_rv(t, bank, tok):
            rv_tok.append(ac(RV[:, t, :], bank[:], ACT.Copy, [tok, f, rrow[0]], scale=RCOL[:, t:t + 1]))
            return [rv_tok[-1]]
        side.append(final_rows())
        rate[:] = [1, 0, 0]
        gemm_tok("w_rv", 0, 8, hi, lo, lambda k: h_tok[k], evac_rv)
        ssq, sskv = SumSq(), SumSq()

        def scaled(dst, toks, ss):
            def evac(bank, t):
                a = tt(dst, bank[:], RROW[:], ALU.mult, [t, f, rrow[0]])
                toks.append(a)
                ss.add(dst, a, eng=pool)
                return [a]
            return evac
        for i in range(3):
            gemm(W2, 12 + i, 8, hi, lo, by_tile(h_tok), scaled(CQ[:, i, :], cq_tok, ssq))
        for i in range(2):
            gemm(W2, 15 + i, 8, hi, lo, by_tile(h_tok), scaled(CKV[:, i, :], ckv_tok, sskv))

        def rope_rows(dst, bank, after):
            j, free = tmp.take()
            k, free2 = tmp.take()
            a = tt(TMP[j][64:96, :], bank[64:96, :], COSM[64:96, :], ALU.mult, [after, trig, free])
            b = tt(TMP[k][64:96, :], bank[96:128, :], SINM[96:128, :], ALU.mult, [after, trig, free2])
            c = tt(dst, TMP[j][64:96, :], TMP[k][64:96, :], ALU.add, [a, b])
            tmp.give(j, [c])
            tmp.give(k, [c])
            return [a, b], c

        def evac_kr(bank, t):
            ab, c = rope_rows(KR[64:96, :], bank, [t, f])
            held["kr"] = tt(KR[64:96, :], KR[64:96, :], RROW[64:96, :], ALU.mult, c)
            return ab
        gemm("w_kr", 0, 8, hi, lo, by_tile(h_tok), evac_kr)

        def rope_full(dst, toks, h):
            def evac(bank, t):
                j, free = tmp.take()
                k, free2 = tmp.take()
                a = tt(TMP[j][:], bank[:], COSR, ALU.mult, [t, trig, free])
                b0 = tt(TMP[k][0:64, :], bank[64:128, :], SINR[64:128, :], ALU.mult, [t, free2])
                b1 = tt(TMP[k][64:128, :], bank[0:64, :], SINR[0:64, :], ALU.mult, [t, free2])
                c = tt(dst, TMP[j][:], TMP[k][:], ALU.add, [a, b0, b1, f, score_tok[h - 2] if h > 1 else None], eng=pool)
                tmp.give(j, [c])
                tmp.give(k, [c])
                toks.append(c)
                return [a, b0, b1]
            return evac

        cqs, ckvs = [], []

        def latent_norm(ss_, n, name, src, toks, h_, l_, dst):
            yield
            c, t, b = ss_.columns()
            r, t = rsqrt_cols(c, T, 1.0 / (128 * n), t)
            mgive(b, [t])
            yield
            yield
            dst += normed(lambda i: src[:, i, :], n, lambda i: vec(name, i), spread(r, t), [toks, f],
                          lambda i: h_[:, i, :], lambda i: l_[:, i, :])

        def rotated(h):
            gemm(W2, h, 8, hi, lo, by_tile(h_tok), rope_full(RQ[:, h % 2, :], rq_tok, h))
            gemm(W2, 4 + h, 8, hi, lo, by_tile(h_tok), rope_full(RK[:, h % 2, :], rk_tok, h))

        side.append(latent_norm(ssq, 3, "g_q", CQ, cq_tok, CQH, CQL, cqs))
        side.append(latent_norm(sskv, 2, "g_kv", CKV, ckv_tok, KVH, KVL, ckvs))
        rotated(0)
        flush()

        qh_tok, kh_tok, vm_tok = [], [], []
        cqh, cql = (lambda k: CQH[:, k, :]), (lambda k: CQL[:, k, :])
        kvh, kvl = (lambda k: KVH[:, k, :]), (lambda k: KVL[:, k, :])
        rate[0] = 0
        f2 = fence()

        def evac_q(i, bank, t):
            a = ac(QH[0:64, i, :], bank[0:64, :], ACT.Copy, [t, f2])
            ab, c = rope_rows(QH[64:96, i, :], bank, [t, f2, a])
            qh_tok.append([a, c])
            return [a] + ab

        def evac_k(i, bank, t):
            a = ac(KH[0:64, 2 * i, :], bank[0:64, :], ACT.Copy, [t, f])
            b = cp(KH[0:64, 2 * i + 1, :], bank[64:128, :], [t, f, a])
            kh_tok.extend([a, b])
            return [a, b]

        for u in range(4):
            for product in small("w_uq", u, 2, 3, cqh, cql, by_tile(cqs), evac_q):
                product()
        for product in small("w_uk", 0, 4, 2, kvh, kvl, by_tile(ckvs), evac_k):
            product()
        for h in range(8):
            if h % 2:
                kh_tok.append(cp(KH[64:96, h, :], KR[64:96, :], [held["kr"], f]))
            else:
                kh_tok.append(ac(KH[64:96, h, :], KR[64:96, :], ACT.Copy, [held["kr"], f]))

        def evac_vm(t, bank, tok):
            vm_tok.append(ac(VM[:, t, :], bank[:], ACT.Copy, [tok, f]))
            return [vm_tok[-1]]
        gemm_tok("w_uv", 0, 2, kvh, kvl, by_tile(ckvs), evac_vm)

        RSUM, RI = keepc(32), keepc(32)
        scale = 1.0 / float(np.sqrt(96.0))
        st_ = [{} for _ in range(32)]
        pt_used = [None] * T
        head = {}
        mo_tok = [None] * 8

        def mla_scores(n):
            h, t = divmod(n, T)
            wdt = (t + 1) * 128
            q = slice(t * 128, (t + 1) * 128)
            b_, bk, free = mbank()
            m0 = mm(bk[:, 0:wdt], QH[:, h, q], KH[:, h, 0:wdt], True, True, [qh_tok[h], kh_tok, free], mark=True)
            m0 = tt(bk[:, q], bk[:, q], MNEG, ALU.add, m0)
            mx, nmx = scratch(1), scratch(1)
            m1 = rmax(mx, bk[:, 0:wdt], m0)
            m2 = ts(nmx, mx, -scale, None, ALU.mult, after=m1)
            j, freej = tmp.take()
            st_[n]["e"] = ac(TMP[j][:, 0:wdt], bk[:, 0:wdt], ACT.Exp, [m2, freej], bias=nmx, scale=scale,
                             accum=RSUM[:, 4 * h + t:4 * h + t + 1])
            st_[n]["j"] = j
            mgive(b_, [st_[n]["e"]])

        def mla_turn(n):
            h, t = divmod(n, T)
            wdt = (t + 1) * 128
            j = st_[n]["j"]
            b_, bk, free = mbank()
            for k in range(t + 1):
                tk_ = tr(bk[:, k * 128:(k + 1) * 128], TMP[j][:, k * 128:(k + 1) * 128], IDENT,
                         [st_[n]["e"], free], mark=(k == t))
            tmp.give(j, [tk_])
            off = 64 * t * (t + 1)
            st_[n]["c"] = ac(PTM[:, off:off + wdt], bk[:, 0:wdt], ACT.Copy, [tk_, pt_used[t]])
            mgive(b_, [st_[n]["c"]])

        def mla_values(n):
            h, t = divmod(n, T)
            off = 64 * t * (t + 1)
            if t == 0:
                head["b"], head["free"] = main.take()
            bk = P_[head["b"]]
            for k in range(t + 1):
                pt = mm(bk[:, t * 64:(t + 1) * 64], PTM[:, off + k * 128:off + (k + 1) * 128],
                        VM[:, k, h * 64:(h + 1) * 64], k == 0, k == t, [st_[n]["c"], vm_tok, head["free"]],
                        mark=(k == t))
            pt_used[t] = pt
            if t == 3:
                rt = recip(RI[:, 4 * h:4 * h + 4], RSUM[:, 4 * h:4 * h + 4], st_[n]["e"])
                rb = RI[:, 4 * h:4 * h + 4].unsqueeze(2).broadcast_to([128, T, 64])
                mo_tok[h] = tt(MO[:, :, h * 64:(h + 1) * 64], bk[:, 0:256].rearrange("p (t d) -> p t d", t=T), rb,
                               ALU.mult, [rt, pt])
                main.give(head["b"], [mo_tok[h]])

        ret = {"scored": 0, "done": 0, "values": None}
        ry_tok, score_tok = [None] * 4, [None] * 4

        def ret_head(h):
            off, xs = 0, []
            for k in range(T):
                wdt = (T - k) * 128
                b_, bk, free = mbank()
                st = mm(bk[:, 0:wdt], RK[:, h % 2, k * 128:(k + 1) * 128], RQ[:, h % 2, k * 128:512], True, True,
                        [rq_tok[h], rk_tok[h], free], mark=True)
                x_ = tt(SC2[:, off:off + wdt], bk[:, 0:wdt], RD[:, h % 2, 0:wdt], ALU.mult,
                        [st, rd_tok[h], ret["values"]])
                mgive(b_, [x_])
                xs.append((x_, off))
                off += wdt
                if k == 3:
                    score_tok[h] = st
                    ret["scored"] = h + 1
                    if h < 2:
                        rd_tok.append(loads.load(s_rd[h], RD[:, h, :], A["ret_decay"][:, h + 2, :], x_))
                yield
            yb, yfree = main.take()
            bk = P_[yb]
            for t in range(T):
                for k in range(t + 1):
                    x_, off = xs[k]
                    c0 = off + (t - k) * 128
                    pt = mm(bk[:, t * 128:(t + 1) * 128], SC2[:, c0:c0 + 128], RV[:, k, h * 128:(h + 1) * 128],
                            k == 0, k == t, [x_, rv_tok, yfree], mark=(k == t))
                if t in (1, 2):
                    yield
            ret["values"] = pt
            stats, aggs = scratch(24), scratch(8)
            for t in range(T):
                z_ = bstat(stats[:, 6 * t:6 * t + 6], bk[:, t * 128:(t + 1) * 128], pt)
            for t in range(T):
                z_ = baggr(aggs[:, 2 * t:2 * t + 2], stats[:, 6 * t:6 * t + 6], z_)
            av = aggs.rearrange("p (n two) -> p n two", two=2)
            rr, d5 = rsqrt_cols(av[:, :, 1], T, 1.0, z_)
            for t in range(T):
                d7 = ts(RY[:, t, h * 128:(h + 1) * 128], bk[:, t * 128:(t + 1) * 128], av[:, t, 0:1],
                        rr[:, t:t + 1], ALU.subtract, ALU.mult, after=[d5])
            main.give(yb, [d7])
            ry_tok[h] = d7
            ret["done"] = h + 1

        def attention():
            current = None
            n = 0
            while n < 37 or ret["done"] < 4:
                if current is None and ret["done"] < 4 and len(rk_tok) > ret["done"]:
                    current = ret_head(ret["done"])
                for _ in range(2 if n % 6 == 5 else 1):
                    if 3 <= n < 35:
                        mla_turn(n - 3)
                    if 5 <= n < 37:
                        mla_values(n - 5)
                    if n < 32:
                        mla_scores(n)
                    n += 1
                if current is not None and next(current, True):
                    current = None
                yield

        side.append(attention())
        rate[0] = 1
        for h in range(1, 4):
            while h > 1 and ret["scored"] < h - 1:
                step()
            rotated(h)
        rg_tok = [None] * 4

        def srg_evac(i):
            def evac(bank, t):
                j, free = tmp.take()
                a = tt(TMP[j][:], bank[:], RROW[:], ALU.mult, [t, free])
                s_ = ac(TMP[j][:], TMP[j][:], ACT.Silu, a)
                b_, bk, free2 = mbank()
                for z in range(T):
                    tk_ = tr(bk[:, z * 128:(z + 1) * 128], RY[:, z, i * 128:(i + 1) * 128], IDENT, [ry_tok[i], free2],
                             mark=(z == 3))
                rg_tok[i] = stt(RG[:, i, :], bk[:], vec("ret_g", i), TMP[j][:], ALU.mult, ALU.mult,
                                [tk_, s_, score_tok])
                mgive(b_, [rg_tok[i]])
                tmp.give(j, [rg_tok[i]])
                return [a]
            return evac

        for i, scored, done in ((0, 3, 1), (2, 3, 3), (1, 4, 2), (3, 4, 4)):
            while ret["scored"] < scored or ret["done"] < done:
                step()
            gemm(W2, 8 + i, 8, hi, lo, by_tile(h_tok), srg_evac(i))
        flush()
        fm = fence()
        mix_tok = [cut(RG[:, h, :], HH[:, h, :], HL[:, h, :], [rg_tok[h], fm], eng=pool if h % 2 else None)
                   for h in range(4)]
        for i in range(4):
            b_, bk, free = mbank()
            for t in range(T):
                tk_ = tr(bk[:, t * 128:(t + 1) * 128], MO[:, t, i * 128:(i + 1) * 128], IDENT,
                         [mo_tok[2 * i], mo_tok[2 * i + 1], free], mark=(t == 3))
            a = ac(HH[:, 4 + i, :], bk[:], ACT.Copy, [tk_, fm])
            z_ = tt(HL[:, 4 + i, :], bk[:], HH[:, 4 + i, :].bitcast(F32), ALU.subtract, [a, tk_])
            mgive(b_, [z_])
            mix_tok.append([a, z_])
        rate[0] = 0

        f = fence()
        pt = once("l_pt", PTS[:], A["pT"], f)
        ptok = []
        toks = []

        def branch(dst, gname, ss, f):
            def make(i):
                def evac(bank, t):
                    a = ss.add(bank[:], t, eng=pool if i < 7 else None)
                    toks.append(ts(dst[:, i, :], bank[:], vec(gname, i), None, ALU.mult, after=[a, t, f]))
                    return [toks[-1]]
                return evac
            return make

        def join(src, b, bank, rt, then, later):
            last = [None]

            def first(i):
                j, free = tmp.take()
                t = last[0] = tt(TMP[j][:], src[:, i, :], bank[:], ALU.mult, [rt, toks[i], free])
                x_tok[i] = tt(XT[:, i, :], XT[:, i, :], TMP[j][:], ALU.add, [t, x_tok[i]],
                              eng=None)
                tmp.give(j, [x_tok[i]])
                then(i, t)

            in_turn(8, first, later)
            mgive(b, [last[0]])

        ssm, sse = SumSq(), SumSq()
        mk = branch(MIXO, "g_post", ssm, f)
        def p_parts():
            for z in range(2):
                ptok.append(cut(PTS[:, z, :], PTH[:, z, :], PTL[:, z, :], [pt, f]))

        gemms([("w_o", i, mk(i), p_parts if i == 3 else None) for i in range(8)], hi, lo, by_tile(mix_tok))
        e_tok = []

        def evac_e(i, bank, t):
            a = ac(EE[:, i, :], bank[:], ACT.Copy, [t, f])
            e_tok.append(a)
            sse.add(EE[:, i, :], a, eng=pool)
            return [a]

        e_products = [product for u in range(2) for product in
                      small("w_pp", u, 4, 2, lambda k: PTH[:, k, :], lambda k: PTL[:, k, :], by_tile(ptok), evac_e)]
        f3 = fence()
        for i in range(3):
            e_products[i]()
        c, t, b = ssm.columns()
        r, t = rsqrt_cols(c, T, 1.0 / D, t)
        mgive(b, [t])
        for i in range(3, 6):
            e_products[i]()
        rows = spread(r, t)
        e_products[6]()
        e_products[7]()
        ss = SumSq()
        h_tok = []

        def then(i, t):
            h_tok.append([ac(hi(i), XT[:, i, :], ACT.Copy, [x_tok[i], f3], scale=vec("g_pf", i)), None])

        def later(i):
            h_tok[i][1] = stt(lo(i), XT[:, i, :], vec("g_pf", i), hi(i).bitcast(F32), ALU.mult, ALU.subtract,
                              [h_tok[i][0], f3])
            ss.add(XT[:, i, :], x_tok[i], eng=pool)

        join(MIXO, *rows, then, later)
        espill = loads.load(sem("l_es"), A["e_scratch"], EE[:], e_tok)
        f = [fence(), espill]
        rrow2 = [None]
        ECOL, ect = keepc(4), [None]

        def ffn_rows():
            c, t, b = ss.columns()
            r, t = rsqrt_cols(c, T, 1.0 / D, t)
            mgive(b, [t])
            yield
            b, bank, rt = spread(r, t)
            rrow2[0] = cp(RROW[:], bank[:], rt)
            mgive(b, [rrow2[0]])
            c, t, b = sse.columns()
            ev, et = rsqrt_cols(c, T, 1.0 / D, t)
            ect[0] = cp(ECOL, ev, et)
            mgive(b, [et])

        mid = ffn_up(lambda i, z: (("w_gate", "w_up")[z], i), h_tok, f, rrow2, ffn_rows)
        f = fence()
        ssf = SumSq()
        toks = []
        mk = branch(FFO, "g_pof", ssf, f)
        for i in range(8):
            gemm("w_down", i, NFT, lambda k: MH[:, k, :], lambda k: ML[:, k, :], by_tile(mid), mk(i))

        ereload = loads.load(sem("l_er"), EE[:], A["e_scratch"], fence())
        x2 = []

        def last(i, t):
            x2.append([ac(HH[:, i, :], XT[:, i, :], ACT.Copy, [x_tok[i], t]), None])

        def last_lo(i):
            x2[i][1] = tt(HL[:, i, :], XT[:, i, :], HH[:, i, :].bitcast(F32), ALU.subtract, [x2[i][0], x_tok[i]],
                          eng=None if i % 3 == 0 else pool)

        rows = rows_of(ssf, D)
        join(FFO, *rows, last, last_lo)

        def e_rows():
            yield
            b, bank, rt = spread(ECOL, ect[0])
            for i in range(8):
                e_tok[i] = stt(EE[:, i, :], EE[:, i, :], vec("g_ple", i), bank[:], ALU.mult, ALU.mult, [rt, ereload])
            mgive(b, [e_tok[7]])

        jobs = []
        for i in range(8):
            def evac(bank, t, i=i):
                j, free = tmp.take()
                a = ac(TMP[j][:], bank[:], ACT.Sigmoid, [t, free], bias=vec("b_pg", i))
                c = tt(TMP[j][:], TMP[j][:], EE[:, i, :], ALU.mult, [a, e_tok[i]])
                c = tt(XT[:, i, :], XT[:, i, :], TMP[j][:], ALU.add, [c, x_tok[i]])
                tmp.give(j, [c])
                loads.load(s_out, out[:, i, :], XT[:, i, :], c)
                return [a]
            jobs.append(("w_pg", i, evac, None))
        gemms(jobs, hi, lo, by_tile(x2), hook=e_rows)
        sp.wait((s_out, loads.total[s_out]))

        seen = W.seen
        if not A["plan"]:
            return seen

        block = ctx.enter_context(nc.Block())

        @block.sync
        def _(e):
            for item in sp.items:
                item(e)

        @block.gpsimd
        def _(e):
            for item in pool.items:
                item(e)

        @block.scalar
        def _(e):
            for item in act.items:
                item(e)

        @block.vector
        def _(e):
            for item in dve.items:
                item(e)

        @block.tensor
        def _(e):
            for item in pe.items:
                item(e)
        return seen


def _tiles(w):
    k, n = w.shape
    return np.ascontiguousarray(w.reshape(k // 128, 128, n // 128, 128).transpose(2, 1, 0, 3)).reshape(
        n // 128, 128, k)


def _several(w, c):
    t = _tiles(w)
    n, _, k = t.shape
    return np.ascontiguousarray(t.reshape(n // c, c, 128, k).transpose(0, 2, 1, 3)).reshape(n // c, 128, c * k)


def _blocks(w, c):
    k, n = w.shape
    return np.ascontiguousarray(w.reshape(k // 128, 128, n // c, c).transpose(2, 1, 0, 3)).reshape(
        n // c, 128, k // 128 * c)


def _fold(v):
    return np.ascontiguousarray(np.asarray(v).reshape(-1, 128).T)


def layout(x):
    f = np.float32
    win, bin_ = x["w_in"][0], x["b_in"][0]
    o = {}
    o["xT"] = np.ascontiguousarray(x["x"][0].T.reshape(8, 128, S).transpose(1, 0, 2))
    o["pT"] = np.ascontiguousarray(x["p_2"][0, 0].T.reshape(2, 128, S).transpose(1, 0, 2))
    o["pos"] = np.ascontiguousarray(x["positions_2"].reshape(1, S))
    o["w_ada"] = _blocks(x["w_ada"][0], 256).reshape(24, 128, 8, 256)
    o["w_in"] = _tiles(np.concatenate([win[:, 0:4096], win[:, 5120:6144], win[:, 6152:8200]], axis=1))
    o["w_v"] = _blocks(win[:, 4096:5120], 512)
    pad = np.zeros((D, 28), f)
    o["w_if"] = _tiles(np.concatenate([win[:, 6144:6148], pad, win[:, 6148:6152], pad, pad, pad, np.zeros((D, 8), f)],
                                      axis=1))
    o["b_v"] = np.ascontiguousarray(bin_[4096:5120].reshape(1, 1024))
    o["w_pw"] = _tiles(x["w_conv_pw"][0])
    o["w_out"] = _tiles(x["w_out"][0])
    o["w_up1"] = _tiles(x["w_ffn_up"][0])
    o["w_down1"] = _tiles(x["w_ffn_down"][0])
    w2 = x["w_in_2"][0]
    o["w_in2"] = _tiles(np.concatenate([w2[:, 0:1024], w2[:, 1536:2688]], axis=1))
    o["w_rv"] = _blocks(w2[:, 1024:1536], 512)
    kr = w2[:, 2688:2720]
    o["w_kr"] = _tiles(np.concatenate([np.zeros((D, 64), f), kr, kr[:, 16:32], kr[:, 0:16]], axis=1))
    uq = x["w_uq_2"][0].reshape(384, 8, 96)
    o["w_uq"] = _several(np.concatenate([uq, uq[:, :, 80:96], uq[:, :, 64:80]], axis=2).reshape(384, 1024), 2)
    ukv = x["w_ukv_2"][0].reshape(256, 8, 128)
    o["w_uk"] = _several(np.ascontiguousarray(ukv[:, :, 0:64]).reshape(256, 512), 4)
    o["w_uv"] = _blocks(np.ascontiguousarray(ukv[:, :, 64:128]).reshape(256, 512), 512)
    o["w_o"] = _tiles(x["w_o_2"][0])
    o["w_gate"] = _tiles(x["w_gate_2"][0])
    o["w_up"] = _tiles(x["w_up_2"][0])
    o["w_down"] = _tiles(x["w_down_2"][0])
    o["w_pp"] = _several(x["w_ple_proj_2"][0], 4)
    o["w_pg"] = _tiles(x["w_ple_gate_2"][0])

    bif = np.concatenate([bin_[6144:6148], np.zeros(28, f), bin_[6148:6152], np.zeros(92, f)])
    parts = {
        "c": x["c"][0], "b_ada": x["b_ada"][0], "g_mix": x["norm_mix_g"][0], "b_glu": bin_[0:2048],
        "b_qk": bin_[2048:4096], "b_o": bin_[5120:6144], "b_mg": bin_[6152:8200], "b_if": bif,
        "dw_b": x["conv_dw_b"][0], "ln_g": x["conv_ln_g"][0], "ln_b": x["conv_ln_b"][0], "b_pw": x["b_conv_pw"][0],
        "qk_b": x["qk_conv_b"][0], "ml_g": x["mlstm_norm_g"][0], "g_ffn": x["norm_ffn_g"][0],
        "g_fin": x["final_norm_g"], "g_pre": x["pre_mix_norm_2"][0], "ret_g": x["ret_gn_w_2"][0],
        "g_q": x["mla_q_norm_2"][0], "g_kv": x["mla_kv_norm_2"][0], "g_post": x["post_mix_norm_2"][0],
        "g_pf": x["pre_ffn_norm_2"][0], "g_pof": x["post_ffn_norm_2"][0], "g_ple": x["ple_norm_2"][0],
        "b_pg": x["b_ple_gate_2"][0],
    }
    cols = [_fold(parts[n]) for n in VEC if n in parts]
    cols.append(x["conv_dw_w"][0].reshape(31, 8, 128).transpose(2, 1, 0).reshape(128, 248))
    cols.append(x["qk_conv_w"][0].reshape(4, 16, 128).transpose(2, 1, 0).reshape(128, 64))
    o["vecs"] = np.ascontiguousarray(np.concatenate(cols, axis=1))

    p = np.arange(128)
    cst = np.zeros((128, NCONST), f)
    cst[:, 0:128] = np.eye(128, dtype=f)
    cst[:, 128:256] = np.where(p[:, None] > p[None, :], f(BIG), f(0))
    cst[:, 256:384] = np.where(p[None, :] > p[:, None], f(-BIG), f(0))

    def inv(half):
        return (f(1.0) / (f(10000.0) ** (np.arange(half, dtype=f) / f(half)))).astype(f)
    cst[:, 384] = inv(64)[p % 64]
    cst[:, 385] = inv(16)[p % 16]
    cst[:, 386] = np.where(p < 64, 1.0, -1.0)
    cst[:, 387] = np.where(p % 32 < 16, -1.0, 1.0)
    o["consts"] = cst
    sel = np.zeros((4, 4, 128), f)
    for h in range(4):
        sel[h, h, :] = 1.0
    o["sel"] = sel
    t = np.arange(S)
    diff = t[None, :] - p[:, None]
    lg = np.log(1.0 - 2.0 ** (-5.0 - np.arange(4)))
    rd = [np.where(diff >= 0, np.exp(np.maximum(diff, 0) * lg[h]), 0.0) * 128.0 ** -0.5 for h in range(4)]
    o["ret_decay"] = np.ascontiguousarray(np.stack(rd, axis=1).astype(f))
    return o


def declare(nc, arrays, plan):
    A = {n: nc.dram_tensor(f"in_{n}", a.shape, mybir.dt.from_np(a.dtype), kind="ExternalInput").ap()
         for n, a in arrays.items()}
    A["plan"] = plan
    A["e_scratch"] = nc.dram_tensor("e_scratch", (128, 8, S), F32, kind="Internal").ap()
    out = nc.dram_tensor("out_0", (128, 8, S), F32, kind="ExternalOutput").ap()
    return program(nc, A, out)


def kernel(**inputs):
    import concourse.bacc as bacc
    from concourse.bass_utils import run_bass_kernel_spmd

    arrays = layout({n: np.asarray(a) for n, a in inputs.items()})
    plan = declare(bacc.Bacc("TRN2", target_bir_lowering=False, num_devices=1), arrays, [])
    nc = bacc.Bacc("TRN2", target_bir_lowering=False, num_devices=1)
    declare(nc, arrays, plan)
    r = run_bass_kernel_spmd(nc, [{f"in_{n}": a for n, a in arrays.items()}], core_ids=[0])
    got = r.results[0]["out_0"]
    return np.ascontiguousarray(got.transpose(1, 0, 2).reshape(D, S).T).reshape(1, S, D)
```
